# Optimizing a Trainium2 kernel written in Bass

```python
import jax, jax.numpy as jnp
from jax import lax
import numpy as np

D_MODEL = 1024
BATCH = 1
SEQ = 512
DEPTH = 1

GRID_W = 64
CTX_LEN = 256
N_HEADS = 16
N_KV_HEADS = 4
GROUP = N_HEADS // N_KV_HEADS
HEAD_DIM = 64
ATTN_WIDTH = N_HEADS * HEAD_DIM
KV_WIDTH = N_KV_HEADS * HEAD_DIM
WINDOW = 128
BLOCK = 128
ROPE_AXIS_DIM = HEAD_DIM // 2
ROPE_BASE = 10000.0
CONV_CH = D_MODEL // 2
CONV_WIDTH = 31
N_BRANCHES = 2
Q_OFF = 0
K_OFF = Q_OFF + ATTN_WIDTH
V_OFF = K_OFF + KV_WIDTH
CONV_OFF = V_OFF + KV_WIDTH
GATE_OFF = CONV_OFF + 2 * CONV_CH
IN_WIDTH = GATE_OFF + N_BRANCHES * D_MODEL
PEER_HEADS = 8
N_KEYS = 128
N_EXPERTS = N_KEYS * N_KEYS
PEER_QDIM = 256
PEER_HALF = PEER_QDIM // 2
PEER_TOPK = 16
PEER_CHUNK = 128
NORM_EPS = 1e-6
NEG_INF = -1e30

kernel_name = "hybrid_dit_wgqa_conformer_peer"

def rmsnorm(x, g):
    xf = x.astype(jnp.float32)
    y = xf * lax.rsqrt(jnp.mean(xf * xf, axis=-1, keepdims=True) + NORM_EPS)
    return (y * g.astype(jnp.float32)).astype(x.dtype)

def layernorm(x, g, b):
    xf = x.astype(jnp.float32)
    mu = jnp.mean(xf, axis=-1, keepdims=True)
    var = jnp.mean(jnp.square(xf - mu), axis=-1, keepdims=True)
    y = (xf - mu) * lax.rsqrt(var + NORM_EPS)
    return (y * g.astype(jnp.float32) + b.astype(jnp.float32)).astype(x.dtype)

def adaln(cond, w_ada, b_ada):
    return jnp.split(jax.nn.silu(cond) @ w_ada + b_ada, 6, axis=-1)

def modulate(h, shift, scale):
    return h * (1.0 + scale) + shift

def axial_rope_tables(rows):
    t = jnp.arange(rows * GRID_W, dtype=jnp.int32)
    row = (t // GRID_W).astype(jnp.float32)
    col = (t % GRID_W).astype(jnp.float32)
    freqs = ROPE_BASE ** (-jnp.arange(0, ROPE_AXIS_DIM, 2, dtype=jnp.float32) / ROPE_AXIS_DIM)
    ang_r = row[:, None] * freqs[None, :]
    ang_c = col[:, None] * freqs[None, :]
    return (jnp.cos(ang_r), jnp.sin(ang_r), jnp.cos(ang_c), jnp.sin(ang_c))

def rope_rotate_half(x, cos, sin):
    x1, x2 = jnp.split(x, 2, axis=-1)
    cos = cos[None, :, None, :]
    sin = sin[None, :, None, :]
    return jnp.concatenate([x1 * cos - x2 * sin, x2 * cos + x1 * sin], axis=-1)

def apply_axial_rope(x, rope):
    cos_r, sin_r, cos_c, sin_c = rope
    xf = x.astype(jnp.float32)
    xr = rope_rotate_half(xf[..., :ROPE_AXIS_DIM], cos_r, sin_r)
    xc = rope_rotate_half(xf[..., ROPE_AXIS_DIM:], cos_c, sin_c)
    return jnp.concatenate([xr, xc], axis=-1).astype(x.dtype)

def window_attention(q, k, v, k_ctx, v_ctx, sink):
    B, S = q.shape[:2]
    nb = S // BLOCK
    qb = q.reshape(B, nb, BLOCK, N_KV_HEADS, GROUP, HEAD_DIM)
    pad = ((0, 0), (WINDOW, WINDOW), (0, 0), (0, 0))
    kb = jnp.pad(k, pad).reshape(B, nb + 2, BLOCK, N_KV_HEADS, HEAD_DIM)
    vb = jnp.pad(v, pad).reshape(B, nb + 2, BLOCK, N_KV_HEADS, HEAD_DIM)
    k_win = jnp.concatenate([kb[:, :-2], kb[:, 1:-1], kb[:, 2:]], axis=2)
    v_win = jnp.concatenate([vb[:, :-2], vb[:, 1:-1], vb[:, 2:]], axis=2)
    qpos = jnp.arange(nb)[:, None, None] * BLOCK + jnp.arange(BLOCK)[None, :, None]
    kpos = (jnp.arange(nb)[:, None, None] - 1) * BLOCK + jnp.arange(3 * BLOCK)[None, None, :]
    valid = (kpos >= 0) & (kpos < S) & (jnp.abs(qpos - kpos) <= WINDOW)
    s_win = jnp.einsum('bnqhgd,bnkhd->bnhgqk', qb, k_win).astype(jnp.float32)
    s_win = jnp.where(valid[None, :, None, None], s_win, NEG_INF)
    s_ctx = jnp.einsum('bnqhgd,bchd->bnhgqc', qb, k_ctx).astype(jnp.float32)
    s_sink = jnp.broadcast_to(
        sink.astype(jnp.float32).reshape(N_KV_HEADS, GROUP)[None, None, :, :, None, None],
        s_win.shape[:-1] + (1,))
    p = jax.nn.softmax(jnp.concatenate([s_win, s_ctx, s_sink], axis=-1), axis=-1)
    n_win = 3 * BLOCK
    n_ctx = k_ctx.shape[1]
    p_win = p[..., :n_win].astype(v.dtype)
    p_ctx = p[..., n_win:n_win + n_ctx].astype(v.dtype)
    o = (jnp.einsum('bnhgqk,bnkhd->bnqhgd', p_win, v_win)
         + jnp.einsum('bnhgqc,bchd->bnqhgd', p_ctx, v_ctx))
    return o.reshape(B, S, ATTN_WIDTH)

def context_attention(q, k, v, sink):
    B, L = q.shape[:2]
    qg = q.reshape(B, L, N_KV_HEADS, GROUP, HEAD_DIM)
    s = jnp.einsum('blhgd,bmhd->bhglm', qg, k).astype(jnp.float32)
    s_sink = jnp.broadcast_to(
        sink.astype(jnp.float32).reshape(N_KV_HEADS, GROUP)[None, :, :, None, None],
        s.shape[:-1] + (1,))
    p = jax.nn.softmax(jnp.concatenate([s, s_sink], axis=-1), axis=-1)[..., :L]
    o = jnp.einsum('bhglm,bmhd->blhgd', p.astype(v.dtype), v)
    return o.reshape(B, L, ATTN_WIDTH)

def conformer_conv(u_glu, conv_dw, conv_dw_b, conv_ln_g, conv_ln_b, w_o_conv):
    a, g = jnp.split(u_glu, 2, axis=-1)
    u = a * jax.nn.sigmoid(g)
    u = lax.conv_general_dilated(
        u, conv_dw[:, None, :].astype(u.dtype), window_strides=(1,),
        padding=[(CONV_WIDTH // 2, CONV_WIDTH // 2)],
        dimension_numbers=('NWC', 'WIO', 'NWC'), feature_group_count=CONV_CH) + conv_dw_b
    u = jax.nn.silu(layernorm(u, conv_ln_g, conv_ln_b))
    return u @ w_o_conv

def merge_branches(y_attn, y_conv, gate_logits, w_out):
    g_attn, g_conv = jnp.split(gate_logits, N_BRANCHES, axis=-1)
    return (jax.nn.sigmoid(g_attn) * y_attn + jax.nn.sigmoid(g_conv) * y_conv) @ w_out

def peer_ffn(h, peer_wq, peer_keys, peer_u, peer_v):
    B, S, D = h.shape
    t = B * S
    hf = h.reshape(t, D)
    q = (hf @ peer_wq).reshape(t, PEER_HEADS, 2, PEER_HALF)
    s = jnp.einsum('thpd,hpkd->thpk', q, peer_keys).astype(jnp.float32)
    s1, i1 = lax.top_k(s[:, :, 0], PEER_TOPK)
    s2, i2 = lax.top_k(s[:, :, 1], PEER_TOPK)
    cand = (s1[..., :, None] + s2[..., None, :]).reshape(t, PEER_HEADS, PEER_TOPK * PEER_TOPK)
    best, pos = lax.top_k(cand, PEER_TOPK)
    idx = (jnp.take_along_axis(i1, pos // PEER_TOPK, axis=-1) * N_KEYS
           + jnp.take_along_axis(i2, pos % PEER_TOPK, axis=-1))
    gates = jax.nn.softmax(best, axis=-1).astype(h.dtype)
    n_chunks = t // PEER_CHUNK

    def expert_block(args):
        xb, ib, gb = args
        act = jax.nn.gelu(jnp.einsum('td,thkd->thk', xb, peer_u[ib]), approximate=False)
        return jnp.einsum('thk,thkd->td', gb * act, peer_v[ib])

    out = lax.map(expert_block, (hf.reshape(n_chunks, PEER_CHUNK, D),
                                 idx.reshape(n_chunks, PEER_CHUNK, PEER_HEADS, PEER_TOPK),
                                 gates.reshape(n_chunks, PEER_CHUNK, PEER_HEADS, PEER_TOPK)))
    return out.reshape(B, S, D)

def trunk_layer(x, h_ctx, c, c_ctx, rope, update_ctx,
                w_ada, b_ada, g_pre_mix, g_post_mix, g_pre_ffn, g_post_ffn,
                w_in, attn_sink, w_o_attn, conv_dw, conv_dw_b, conv_ln_g, conv_ln_b,
                w_o_conv, w_out, peer_wq, peer_keys, peer_u, peer_v):
    B, S, _ = x.shape
    L = h_ctx.shape[1]
    sh1, sc1, gt1, sh2, sc2, gt2 = [m[:, None, :] for m in adaln(c, w_ada, b_ada)]
    csh1, csc1, cgt1, csh2, csc2, cgt2 = adaln(c_ctx, w_ada, b_ada)
    q_scale = HEAD_DIM ** -0.5

    hx = modulate(rmsnorm(x, g_pre_mix), sh1, sc1)
    hc = modulate(rmsnorm(h_ctx, g_pre_mix), csh1, csc1)
    p = hx @ w_in
    q = apply_axial_rope(p[..., Q_OFF:K_OFF].reshape(B, S, N_HEADS, HEAD_DIM), rope) * q_scale
    k = apply_axial_rope(p[..., K_OFF:V_OFF].reshape(B, S, N_KV_HEADS, HEAD_DIM), rope)
    v = p[..., V_OFF:CONV_OFF].reshape(B, S, N_KV_HEADS, HEAD_DIM)
    if update_ctx:
        pc = hc @ w_in
        kvc = pc[..., K_OFF:CONV_OFF]
    else:
        kvc = hc @ w_in[:, K_OFF:CONV_OFF]
    k_c = kvc[..., :KV_WIDTH].reshape(B, L, N_KV_HEADS, HEAD_DIM)
    v_c = kvc[..., KV_WIDTH:].reshape(B, L, N_KV_HEADS, HEAD_DIM)

    y_attn = window_attention(q, k, v, k_c, v_c, attn_sink) @ w_o_attn
    y_conv = conformer_conv(p[..., CONV_OFF:GATE_OFF], conv_dw, conv_dw_b, conv_ln_g, conv_ln_b, w_o_conv)
    mixed = merge_branches(y_attn, y_conv, p[..., GATE_OFF:], w_out)
    x = x + gt1 * rmsnorm(mixed, g_post_mix)

    if update_ctx:
        q_c = pc[..., Q_OFF:K_OFF].reshape(B, L, N_HEADS, HEAD_DIM) * q_scale
        yc_attn = context_attention(q_c, k_c, v_c, attn_sink) @ w_o_attn
        yc_conv = conformer_conv(pc[..., CONV_OFF:GATE_OFF], conv_dw, conv_dw_b, conv_ln_g, conv_ln_b, w_o_conv)
        mixed_c = merge_branches(yc_attn, yc_conv, pc[..., GATE_OFF:], w_out)
        h_ctx = h_ctx + cgt1 * rmsnorm(mixed_c, g_post_mix)

    h2 = modulate(rmsnorm(x, g_pre_ffn), sh2, sc2)
    x = x + gt2 * rmsnorm(peer_ffn(h2, peer_wq, peer_keys, peer_u, peer_v), g_post_ffn)
    if update_ctx:
        hc2 = modulate(rmsnorm(h_ctx, g_pre_ffn), csh2, csc2)
        h_ctx = h_ctx + cgt2 * rmsnorm(peer_ffn(hc2, peer_wq, peer_keys, peer_u, peer_v), g_post_ffn)
    return x, h_ctx

def setup_inputs(seed: int = 0) -> dict:
    key = jax.random.key(seed)
    ks = jax.random.split(key, 24)
    f32 = jnp.float32
    D = D_MODEL

    def nrm(k, shape, scale):
        return jax.random.normal(k, shape, f32) * scale

    def gain(k, shape):
        return 1.0 + 0.05 * jax.random.normal(k, shape, f32)

    return {
        "x": nrm(ks[0], (BATCH, SEQ, D), 1.0),
        "c": nrm(ks[1], (BATCH, D), 1.0),
        "ctx": nrm(ks[2], (BATCH, CTX_LEN, D), 1.0),
        "c_ctx": nrm(ks[3], (D,), 1.0),
        "w_ada": nrm(ks[4], (DEPTH, D, 6 * D), 0.5 * D ** -0.5),
        "b_ada": nrm(ks[5], (DEPTH, 6 * D), 0.01),
        "g_pre_mix": gain(ks[6], (DEPTH, D)),
        "g_post_mix": gain(ks[7], (DEPTH, D)),
        "g_pre_ffn": gain(ks[8], (DEPTH, D)),
        "g_post_ffn": gain(ks[9], (DEPTH, D)),
        "w_in": nrm(ks[10], (DEPTH, D, IN_WIDTH), D ** -0.5),
        "attn_sink": nrm(ks[11], (DEPTH, N_HEADS), 0.5),
        "w_o_attn": nrm(ks[12], (DEPTH, ATTN_WIDTH, D), ATTN_WIDTH ** -0.5),
        "conv_dw": nrm(ks[13], (DEPTH, CONV_WIDTH, CONV_CH), CONV_WIDTH ** -0.5),
        "conv_dw_b": nrm(ks[14], (DEPTH, CONV_CH), 0.01),
        "conv_ln_g": gain(ks[15], (DEPTH, CONV_CH)),
        "conv_ln_b": nrm(ks[16], (DEPTH, CONV_CH), 0.01),
        "w_o_conv": nrm(ks[17], (DEPTH, CONV_CH, D), CONV_CH ** -0.5),
        "w_out": nrm(ks[18], (DEPTH, D, D), D ** -0.5),
        "peer_wq": nrm(ks[19], (DEPTH, D, PEER_HEADS * PEER_QDIM), D ** -0.5),
        "peer_keys": nrm(ks[20], (DEPTH, PEER_HEADS, 2, N_KEYS, PEER_HALF), PEER_HALF ** -0.5),
        "peer_u": nrm(ks[21], (DEPTH, N_EXPERTS, D), D ** -0.5),
        "peer_v": nrm(ks[22], (DEPTH, N_EXPERTS, D), D ** -0.5),
    }

def reference(x, c, ctx, c_ctx, w_ada, b_ada, g_pre_mix, g_post_mix, g_pre_ffn, g_post_ffn,
              w_in, attn_sink, w_o_attn, conv_dw, conv_dw_b, conv_ln_g, conv_ln_b, w_o_conv,
              w_out, peer_wq, peer_keys, peer_u, peer_v):
    rows = x.shape[1] // GRID_W
    rope = axial_rope_tables(rows)
    h_ctx = ctx
    for layer in range(DEPTH):
        x, h_ctx = trunk_layer(
            x, h_ctx, c, c_ctx, rope, layer + 1 < DEPTH,
            w_ada[layer], b_ada[layer], g_pre_mix[layer], g_post_mix[layer],
            g_pre_ffn[layer], g_post_ffn[layer], w_in[layer], attn_sink[layer],
            w_o_attn[layer], conv_dw[layer], conv_dw_b[layer], conv_ln_g[layer],
            conv_ln_b[layer], w_o_conv[layer], w_out[layer], peer_wq[layer],
            peer_keys[layer], peer_u[layer], peer_v[layer])
    return x


_drawn_inputs = setup_inputs


def setup_inputs(seed=0):
    import zlib

    import numpy as np

    out = dict(_drawn_inputs(seed))
    spreads = {}
    factors = {'g_post_ffn': 3.796, 'attn_sink': 8.0, 'conv_ln_b': 3.153}
    for name, (base, spread) in spreads.items():
        noise = np.random.default_rng([zlib.crc32(name.encode()), seed]).standard_normal(out[name].shape)
        drawn = base * np.exp(spread * noise) if base else spread * noise
        out[name] = __import__('jax').numpy.asarray(drawn.astype(out[name].dtype))
    for name, factor in factors.items():
        out[name] = (out[name] * factor).astype(out[name].dtype)
    return out
```

```python
from contextlib import ExitStack

import numpy as np

import concourse.bass as bass
from concourse import mybir

D = 1024
T = 512
C = 256
P = 128
KD = D // P
TT = T // P
GRID_W = 64
HEADS, KV_HEADS, HD = 16, 4, 64
GROUP = HEADS // KV_HEADS
CONV = 512
KC = CONV // P
TAPS = 31
PEER_HEADS, KEYS, TOPK = 8, 128, 16
EPS = 1e-6
NEG = -1e30
FLOOR = -3.0e38

CHUNK = 512
RING = 3
N_ADA = 6 * D // CHUNK
ADA_FIRST = 4
ORDER = [("ada", n) for n in range(ADA_FIRST)]
for _i, _kind in enumerate(["conv_a", "conv_g", "kv", "q0", "q1", "gate0", "gate1", "gate2", "gate3"]):
    ORDER.append((_kind, 0))
    if ADA_FIRST + _i < N_ADA:
        ORDER.append(("ada", ADA_FIRST + _i))
ORDER += [("o_attn", 0), ("o_attn", 1), ("o_conv", 0), ("out", 0), ("out", 1)]
ORDER += [("wq", n) for n in range(4)]

V_BADA, V_PREMIX, V_POSTMIX, V_PREFFN, V_POSTFFN = 0, 48, 56, 64, 72
V_DW, V_DWB, V_LNG, V_LNB, V_SINK, V_N = 80, 204, 208, 212, 216, 232
SH1, SC1, GT1, SH2, SC2, GT2 = (8 * n for n in range(6))
SWAP = [(i + 16) % 32 for i in range(32)]
HEAD_ORDER = [GROUP * (2 * a + s) + j for a in range(2) for j in range(GROUP) for s in range(2)]

NSTEP = 2 * KEYS
ROW = KD * P


def windows(qb):
    return list(range(max(0, qb - 1), min(TT - 1, qb + 1) + 1)) + [TT, TT + 1]


def layer_kernel(nc, xT, ctxT, cc, wchunks, vec, keysT, expert_rows, consts, out):
    fp32 = mybir.dt.float32
    f32r = mybir.dt.float32r
    u32 = mybir.dt.uint32
    ALU = mybir.AluOpType
    ACT = mybir.ActivationFunctionType
    AX = mybir.AxisListType.X

    act_dram = nc.dram_tensor("act_dram", [KEYS, P, T], fp32).ap()
    w_dram = nc.dram_tensor("w_dram", [T // 32, P, KEYS, 32], fp32).ap()

    ctx = ExitStack()
    with ctx:
        BASE = 16512
        ctx.enter_context(nc.sbuf_tensor("slab", [P, (229344 - BASE) // 4], fp32))
        top = [BASE]

        def at(name, shape, offset, dt=fp32):
            return nc.alloc_sbuf_tensor_at(name, [P, *shape], dt, offset=offset)

        def take(n):
            top[0] += n
            return top[0] - n

        KB = 1024
        x1 = at("x1", [KD, T], take(16 * KB))
        vecs = at("vecs", [V_N], take(KB))
        mod = at("mod", [48, 2], take(512))
        ident = at("ident", [P], take(512))
        iota = at("iota", [P], take(512))
        ones = at("ones", [P], take(512))
        cond = at("cond", [KD, 2], take(64))
        coef = at("coef", [6, KD], take(256))
        rstd = at("rstd", [T], take(2 * KB))
        sq = at("sq", [2, T], take(4 * KB))
        small = at("small", [256], take(KB))
        r_ring, r_h, r_ctx, r_q, r_gate = take(RING * 16 * KB), take(16 * KB), take(16 * KB), take(16 * KB), take(32 * KB)
        r_tail = take(46 * KB)
        assert top[0] <= 229368, top[0]
        ring = at("ring", [RING, KD, CHUNK], r_ring)
        hT = at("hT", [KD, T], r_h)
        yT = at("yT", [KD, T], r_h)
        mixed = at("mixed", [KD, T], r_h)
        ctx_sb = at("ctx_sb", [KD, C], r_ctx)
        hcT = at("hcT", [KD, C], r_ctx + 8 * KB)
        probs = at("probs", [2, 640], r_ctx)
        probsT = at("probsT", [2, 640], r_ctx + 5120)
        q_now = at("q_now", [T], r_ctx + 10240)
        sink_now = at("sink_now", [2], r_ctx + 10240 + 2048)
        qT = at("qT", [KD, T], r_q)
        gates = at("gates", [2 * KD, T], r_gate)
        kT = at("kT", [2, T + C], r_tail)
        v_sb = at("v_sb", [6, 256], r_tail + 6144)
        u_w = T + TAPS - 1
        conv_in = at("conv_in", [KC, u_w], r_tail + 12288)
        conv_acc = at("conv_acc", [KC, T], r_tail + 12288 + 4 * KC * u_w)
        o = r_tail + 12288 + 4 * KC * u_w + 8 * KB
        cos_t = at("cos_t", [T], o)
        sin_t = at("sin_t", [T], o + 2048)
        mask = at("mask", [640 + 512], o + 4096)
        glu = at("glu", [KC, T], o + 4096 + 4608)
        assert o + 4096 + 4608 + 8 * KB <= r_tail + 46 * KB
        h2 = at("h2", [KD, T], r_q)
        h2_hi = at("h2_hi", [KD, T], r_gate, f32r)
        h2_lo = at("h2_lo", [KD, T], r_gate + 16 * KB, f32r)
        scores = at("scores", [TT * PEER_HEADS * 2, KEYS], r_h)
        keys = at("keys", [2 * PEER_HEADS, KEYS], r_tail)
        q_peer = at("q_peer", [2, T], r_tail + 8 * KB)
        raw = at("raw", [4, ROW], r_tail + 12 * KB)
        st_hi = at("st_hi", [2, ROW], r_ring, f32r)
        st_lo = at("st_lo", [2, ROW], r_ring + 8 * KB, f32r)
        w_tile = at("w_tile", [2, KEYS, 32], r_ring + 16 * KB)
        o = r_tail + 28 * KB
        best = at("best", [32, TOPK], o)
        i1_all = at("i1_all", [32, TOPK], o + 2 * KB)
        i2_all = at("i2_all", [32, TOPK], o + 4 * KB)
        sc_now = at("sc_now", [4, KEYS], o + 6 * KB)
        cand = at("cand", [2, TOPK * TOPK], o + 8 * KB)
        hit = at("hit", [2, TOPK, TOPK], o + 10 * KB)
        p_lo = at("p_lo", [2, T], o + 12 * KB, f32r)
        tops = at("tops", [4, TOPK], o + 16 * KB)
        top_ix = at("top_ix", [4, TOPK], o + 16 * KB + 256, u32)
        top_ixf = at("top_ixf", [4, TOPK], o + 16 * KB + 512)
        best_now = at("best_now", [2, TOPK], o + 16 * KB + 768)
        pos = at("pos", [2, TOPK], o + 16 * KB + 896, u32)
        pos_ab = at("pos_ab", [2, 2, TOPK], o + 16 * KB + 1024, u32)
        pos_f = at("pos_f", [2, 2, TOPK], o + 16 * KB + 1280)
        e_sum = at("e_sum", [2, 32], o + 16 * KB + 1536)
        act_out = at("act_out", [2, T], r_q)
        i1T = at("i1T", [T], r_q + 4 * KB)
        i2T = at("i2T", [T], r_q + 6 * KB)
        gT = at("gT", [T], r_q + 8 * KB)
        g_hi = at("g_hi", [T], r_q + 10 * KB, f32r)
        g_lo = at("g_lo", [T], r_q + 12 * KB)
        now = at("now", [4, 64], r_q + 14 * KB)
        one_hi = at("one_hi", [2, 4, P], r_h, f32r)
        one_lo = at("one_lo", [2, 4, P], r_h + 4 * KB, f32r)
        one_b = at("one_b", [2, 4, P], r_h + 8 * KB, f32r)
        w_in = at("w_in", [2, 16, 4, 32], r_h + 12 * KB)
        p_full = at("p_full", [2, T], r_h + 28 * KB)
        act_in = at("act_in", [4, T], r_q)
        p_hi = at("p_hi", [2, T], r_q + 8 * KB, f32r)
        zeros = at("zeros", [T], r_q + 12 * KB, mybir.dt.bfloat16)
        ffn = at("ffn", [KD, T], r_ring)
        ps = ctx.enter_context(nc.psum_tensor("ps", [P, 8, 512], fp32))
        BANK_STAT, BANK_ADA = 4, 7

        def sem(name):
            return ctx.enter_context(nc.semaphore(name))

        x_in, ctx_in, cc_in, vec_in, const_in, keys_in = map(sem, ("x_in", "ctx_in", "cc_in", "vec_in", "const_in", "keys_in"))
        chunk_in = [sem(f"chunk_in{i}") for i in range(RING)]
        ada_used = sem("ada_used")
        cond_ready, filled = sem("cond_ready"), sem("filled")
        sq_ready, sq_used, mean_done, var_ready, rstd_ready = map(
            sem, ("sq_ready", "sq_used", "mean_done", "var_ready", "rstd_ready"))
        hx_ready, hc_ready = sem("hx_ready"), sem("hc_ready")
        tile_done, tile_out_act, tile_out_dve = sem("tile_done"), sem("tile_out_act"), sem("tile_out_dve")
        conv_summed, conv_centred, conv_normed, conv_out = map(sem, ("conv_summed", "conv_centred", "conv_normed", "conv_out"))
        rotated = sem("rotated")
        q_ready, s_done, neg_ready, exp_done, inv_ready, p_ready = map(
            sem, ("q_ready", "s_done", "neg_ready", "exp_done", "inv_ready", "p_ready"))
        ta_done, tb_done, ta_out, tb_out, pv_done, y_out = map(sem, ("ta_done", "tb_done", "ta_out", "tb_out", "pv_done", "y_out"))
        z_ready, x1_ready, h2_ready, h2_split, h2_parts = map(sem, ("z_ready", "x1_ready", "h2_ready", "h2_split", "h2_parts"))
        qp_ready, sc_done, sc_out = sem("qp_ready"), sem("sc_done"), sem("sc_out")
        row_in = [sem(f"row_in{i}") for i in range(4)]
        hi_ready, lo_ready, step_done = sem("hi_ready"), sem("lo_ready"), sem("step_done")
        gelu_done, act_stored = sem("gelu_done"), [sem(f"act_stored{i}") for i in range(2)]
        picked, gate_exp, gate_ready, turned, turned_out = map(sem, ("picked", "gate_exp", "gate_ready", "turned", "turned_out"))
        gates_split, now_ready, b_ready, a_ready, w_done, w_out_s = map(
            sem, ("gates_split", "now_ready", "b_ready", "a_ready", "w_done", "w_out_s"))
        w_stored = [sem(f"w_stored{i}") for i in range(2)]
        w_loaded = [sem(f"w_loaded{i}") for i in range(2)]
        act_loaded = [sem(f"act_loaded{i}") for i in range(4)]
        pf_ready, ph_ready, pl_ready, acc_out, final_ready, out_done = map(
            sem, ("pf_ready", "ph_ready", "pl_ready", "acc_out", "final_ready", "out_done"))
        dve_chain, act_chain, zero_ready = sem("dve_chain"), sem("act_chain"), sem("zero_ready")
        settled = sem("settled")

        tiles, chunk_tiles = [], []
        for kind, n in ORDER:
            if kind in ("conv_a", "conv_g"):
                tiles += [(kind, i, "act") for i in range(4)]
            elif kind == "kv":
                tiles += [("k", i, "act") for i in range(2)] + [("kc", i, "act") for i in range(2)]
                tiles += [("v", i, "act") for i in range(4)] + [("vc", i, "act") for i in range(2)]
            elif kind in ("q0", "q1"):
                tiles += [("q", 4 * int(kind[1]) + i, "act") for i in range(4)]
            elif kind.startswith("gate"):
                tiles += [("gate", 4 * int(kind[4]) + i, "act") for i in range(4)]
            elif kind == "o_attn":
                tiles += [("ya", 4 * n + i, "dve") for i in range(4)]
            elif kind == "o_conv":
                tiles += [("yc", i, "dve") for i in range(8)]
            elif kind == "out":
                tiles += [("mix", 4 * n + i, "act") for i in range(4)]
            elif kind == "wq":
                tiles += [("peer", 4 * n + i, "act") for i in range(4)]
            chunk_tiles.append(len(tiles))
        tile_no = {(k, i): n for n, (k, i, _) in enumerate(tiles)}
        tile_count = []
        for n, (_, _, e) in enumerate(tiles):
            tile_count.append(sum(x == e for _, _, x in tiles[: n + 1]))

        def tile_bank(n):
            return n % 4

        def wait_tile_out(eng, n):
            eng.wait_ge(tile_out_act if tiles[n][2] == "act" else tile_out_dve, tile_count[n])

        def settle(eng):
            eng.sem_inc(settled, 1)

        def wait_chunk_used(eng, n):
            if ORDER[n][0] == "ada":
                eng.wait_ge(ada_used, sum(k == "ada" for k, _ in ORDER[: n + 1]))
            else:
                eng.wait_ge(tile_done, chunk_tiles[n])

        def g2(col, k):
            return vecs[:, col + k:col + k + 1]

        block = ctx.enter_context(nc.Block())

        @block.sync
        def _(sp):
            sp.dma_start(cond[:, :, :], cc).then_inc(cc_in, 16)
            sp.dma_start(vecs[:, :], vec).then_inc(vec_in, 16)
            sp.dma_start(ctx_sb[:, :, :], ctxT).then_inc(ctx_in, 16)
            sp.dma_start(x1[:, :, :], xT).then_inc(x_in, 16)
            for dst, a, b in ((ident, 0, 128), (iota, 128, 256), (cos_t, 256, 768), (sin_t, 768, 1280), (mask, 1280, 2432)):
                sp.dma_start(dst[:, :], consts[:, a:b]).then_inc(const_in, 16)
            for n in range(len(ORDER)):
                if n >= RING:
                    wait_chunk_used(sp, n - RING)
                sp.dma_start(ring[:, n % RING, :, :], wchunks[n]).then_inc(chunk_in[n % RING], 16)
                if n == len(ORDER) - 4:
                    wait_tile_out(sp, tile_no["yc", 7])
                    sp.dma_start(keys[:, :, :], keysT).then_inc(keys_in, 16)
                    for s in range(4):
                        sp.dma_start(raw[:, s, :], expert_rows[s]).then_inc(row_in[s], 16)

            def load_row(n, s):
                sp.wait_ge(lo_ready, n + 1)
                sp.dma_start(raw[:, s, :], expert_rows[bass.ds(n + 4, 1)].rearrange("a p n -> (a p) n")).then_inc(row_in[s], 16)

            def store_act(n, s):
                sp.wait_ge(gelu_done, n + 3)
                sp.dma_start(act_dram[bass.ds(n, 1)].rearrange("a p n -> (a p) n"), act_out[:, s, :]).then_inc(act_stored[s], 16)

            with sp.Fori(0, 16) as it:
                for s in range(4):
                    load_row(it * 4 + s, s)
                    store_act(it * 4 + s, s % 2)
            with sp.Fori(0, 8) as it:
                for s in range(8):
                    load_row(it * 8 + (64 + s), s % 4)
                    store_act(it * 8 + (64 + s), s % 2)
                    if s % 4 == 3:
                        h = s // 4
                        sp.wait_ge(w_out_s, it * 16 + (8 * (h + 1) + 2))
                        sp.dma_start(w_dram[bass.ds(it * 2 + h, 1)].rearrange("a p i t -> (a p) (i t)"),
                                     w_tile[:, h, :, :].rearrange("p i t -> p (i t)")).then_inc(w_stored[h], 16)
            for s in range(2):
                sp.wait_ge(act_stored[s], 16 * (KEYS // 2 + 1))
                sp.wait_ge(w_stored[s], 16 * (8 + 1))
            sp.wait_ge(w_done, T // 4 + 2)

            def load_w(g, h):
                sp.dma_start(w_in[:, h, :, :, :].rearrange("p t i s -> p t (i s)"),
                             w_dram[:, :, bass.ds(g * 4, 4), :].rearrange("t p i s -> p t (i s)")).then_inc(w_loaded[h], 16)

            def load_act(i2, s):
                sp.dma_start(act_in[:, s, :], act_dram[bass.ds(i2, 1)].rearrange("a p n -> (a p) n")).then_inc(act_loaded[s], 16)

            for s in range(4):
                load_act(s, s)
            load_w(0, 0)
            load_w(1, 1)

            with sp.Fori(0, 15) as it:
                for s in range(8):
                    i2 = it * 8 + s
                    load_row(i2 + KEYS, s % 4)
                    sp.wait_ge(pf_ready, i2 + 1)
                    load_act(i2 + 4, s % 4)
                    if s % 4 == 3:
                        load_w(it * 2 + (2 + s // 4), s // 4)
            for s in range(4):
                load_row(NSTEP - 8 + s, s)
                sp.wait_ge(pf_ready, KEYS - 8 + s + 1)
                load_act(KEYS - 4 + s, s)
            for k in range(KD):
                sp.wait_ge(final_ready, k + 1)
                sp.dma_start(out[:, k, :], x1[:, k, :]).then_inc(out_done, 16)
            sp.wait_ge(out_done, 16 * KD)

        @block.gpsimd
        def _(pool):
            nc.gpsimd.memset(ones[:, :], 1.0).then_inc(filled, 1)
            nc.gpsimd.memset(conv_in[:, :, 0:TAPS // 2], 0.0).then_inc(filled, 1)
            nc.gpsimd.memset(conv_in[:, :, T + TAPS // 2:u_w], 0.0).then_inc(filled, 1)
            pool.wait_ge(vec_in, 16)
            pool.wait_ge(rotated, 10)
            for a in range(2):
                with pool.Fori(0, 4) as it:
                    r = it + 4 * a
                    pool.wait_ge(s_done, r * 8 + 1)
                    nc.gpsimd.tensor_copy(q_now[:, :], qT[:, bass.ds(r, 1), :].rearrange("p a t -> p (a t)")).then_inc(q_ready, 1)
                    nc.gpsimd.tensor_copy(sink_now[:, :], vecs[:, bass.ds(r * 2 + V_SINK, 2)]).then_inc(q_ready, 1)
                    for u in range(8):
                        n = P * len(windows(u // 2))
                        pool.wait_ge(inv_ready, r * 8 + u + 1)
                        settle(pool)
                        nc.gpsimd.tensor_scalar(probs[:, u % 2, 0:n], probs[:, u % 2, 0:n], small[:, 8 + u % 2:9 + u % 2],
                                                None, ALU.mult).then_inc(p_ready, 1)
            pool.sem_inc(b_ready, 1)
            with pool.Fori(0, 8) as it:
                pool.wait_ge(now_ready, it * 3 + 3)
                for g in range(16):
                    pool.wait_ge(w_done, it * 16 + (g + 1))
                    settle(pool)
                    for j in range(4):
                        ins = nc.gpsimd.tensor_scalar(one_b[:, g % 2, j, :], iota[:, :], now[:, 1, 4 * g + j:4 * g + j + 1],
                                                      None, ALU.is_equal)
                    ins.then_inc(b_ready, 1)

        @block.scalar
        def _(act):
            n_sq = [0]
            n_stat = [0]

            def square(dst_src, width):
                n = n_sq[0]
                if n >= 2:
                    act.wait_ge(sq_used, n - 1)
                nc.scalar.activation(sq[:, n % 2, 0:width], dst_src, ACT.Square).then_inc(sq_ready, 1)
                n_sq[0] += 1

            def root(width):
                n_stat[0] += 1
                act.wait_ge(var_ready, n_stat[0])
                nc.scalar.activation(rstd[:, 0:width], rstd[:, 0:width], ACT.Sqrt).then_inc(rstd_ready, 1)

            act.wait_ge(cc_in, 16)
            nc.scalar.activation(cond[:, :, :], cond[:, :, :], ACT.Silu).then_inc(cond_ready, 1)
            act.wait_ge(ctx_in, 16)
            for k in range(KD):
                square(ctx_sb[:, k, :], C)
            root(C)
            act.wait_ge(x_in, 16)
            for k in range(KD):
                square(x1[:, k, :], T)
            root(T)

            def drain_tiles(kinds):
                for n, (k, i, e) in enumerate(tiles):
                    if k not in kinds:
                        continue
                    act.wait_ge(tile_done, n + 1)
                    src = ps[:, tile_bank(n), :]
                    if k == "conv_a":
                        if i == 0:
                            act.wait_ge(filled, 3)
                        dst, fn, sc = conv_in[:, i, TAPS // 2:TAPS // 2 + T], ACT.Copy, 1.0
                    elif k == "conv_g":
                        dst, fn, sc = glu[:, i, :], ACT.Sigmoid, 1.0
                    elif k == "k":
                        dst, fn, sc = kT[:, i, 0:T], ACT.Copy, 1.0
                    elif k == "kc":
                        dst, src, fn, sc = kT[:, i, T:T + C], src[:, 0:C], ACT.Copy, 1.0
                    elif k == "v":
                        dst, src, fn, sc = v_sb[:, i, :], src[:, 0:256], ACT.Copy, 1.0
                    elif k == "vc":
                        dst, src, fn, sc = v_sb[:, TT + i, :], src[:, 0:256], ACT.Copy, 1.0
                    elif k == "q":
                        dst, fn, sc = qT[:, i, :], ACT.Copy, float(HD) ** -0.5
                    elif k == "gate":
                        dst, fn, sc = gates[:, i, :], ACT.Sigmoid, 1.0
                    nc.scalar.activation(dst, src, fn, scale=sc).then_inc(tile_out_act, 1)

            drain_tiles(("conv_a", "conv_g", "k", "kc", "v", "vc", "q"))
            drain_tiles(("gate",))
            act.wait_ge(conv_centred, KC)
            for c in range(KC):
                square(conv_acc[:, c, :], T)
            root(T)
            act.wait_ge(conv_normed, KC)
            for c in range(KC):
                nc.scalar.activation(conv_acc[:, c, :], conv_acc[:, c, :], ACT.Silu, bias=g2(V_LNB, c),
                                     scale=g2(V_LNG, c)).then_inc(conv_out, 1)
            for a in range(2):
                with act.Fori(0, 4) as it:
                    r = it + 4 * a
                    for u in range(9):
                        if u < 8:
                            n = P * len(windows(u // 2))
                            act.wait_ge(neg_ready, r * 8 + u + 1)
                            nc.scalar.activation(probs[:, u % 2, 0:n], probs[:, u % 2, 0:n], ACT.Exp,
                                                 bias=small[:, 2 + u % 2:3 + u % 2],
                                                 accum_out=small[:, 4 + u % 2:5 + u % 2]).then_inc(act_chain, 1)
                            nc.scalar.activation(small[:, 6 + u % 2:7 + u % 2], sink_now[:, u % 2:u % 2 + 1], ACT.Exp,
                                                 bias=small[:, 2 + u % 2:3 + u % 2]).then_inc(exp_done, 1)
                        if u >= 1:
                            w = u - 1
                            act.wait_ge(ta_done, r * 8 + w + 1)
                            act.wait_ge(pv_done, r * 8 + w + 1)
                            nc.scalar.copy(probsT[:, w % 2, 0:384], ps[:, 4, 0:384]).then_inc(ta_out, 1)
                    act.wait_ge(pv_done, r * 8 + 8 + 2)
                    nc.scalar.copy(yT[:, bass.ds(r, 1), :].rearrange("p a t -> p (a t)"), ps[:, 6, :]).then_inc(y_out, 1)
            for i in range(KD):
                n = tile_no["mix", i]
                act.wait_ge(tile_done, n + 1)
                square(ps[:, tile_bank(n), :], T)
                nc.scalar.copy(mixed[:, i, :], ps[:, tile_bank(n), :]).then_inc(tile_out_act, 1)
            root(T)
            for k in range(KD):
                act.wait_ge(x1_ready, k + 1)
                square(x1[:, k, :], T)
            root(T)
            for k in range(KD):
                act.wait_ge(h2_ready, k + 1)
                nc.scalar.copy(h2_hi[:, k, :], h2[:, k, :]).then_inc(h2_split, 1)
            for i in range(2 * PEER_HEADS):
                n = tile_no["peer", i]
                act.wait_ge(tile_done, n + 1)
                if i >= 2:
                    act.wait_ge(sc_done, i - 1)
                nc.scalar.copy(q_peer[:, i % 2, :], ps[:, tile_bank(n), :]).then_inc(tile_out_act, 1)
                act.wait_ge(sc_done, i + 1)
                nc.scalar.copy(scores[:, i:i + 2 * PEER_HEADS * (TT - 1) + 1:2 * PEER_HEADS, :],
                               ps[:, 4 + i % 2, :].rearrange("p (t k) -> p t k", t=TT)).then_inc(sc_out, 1)

            def high(n, s, rounds):
                act.wait_ge(row_in[s % 4], rounds * 16)
                act.wait_ge(step_done, n + 1)
                nc.scalar.copy(st_hi[:, s % 2, :], raw[:, s % 4, :]).then_inc(hi_ready, 1)

            def gelu(n, s, stored):
                act.wait_ge(step_done, n + 3)
                act.wait_ge(act_stored[s % 2], stored)
                nc.scalar.activation(act_out[:, s % 2, :], ps[:, s % 2, :], ACT.Gelu).then_inc(gelu_done, 1)

            act.wait_ge(step_done, 2)
            high(0, 0, 1)
            act.sem_inc(act_stored[0], 16)
            act.sem_inc(act_stored[1], 16)
            act.sem_inc(w_stored[0], 16)
            act.sem_inc(w_stored[1], 16)
            act.sem_inc(gelu_done, 2)
            act.sem_inc(w_out_s, 2)
            nc.scalar.preload_act_table(ACT.Gelu)
            with act.Fori(0, 16) as it:
                for s in range(4):
                    high(it * 4 + (s + 1), s + 1, it + (1 if s < 3 else 2))
                    gelu(it * 4 + s, s, it * 32 + 16 * (1 + s // 2))
            act.wait_ge(picked, 1)
            nc.scalar.activation(best[:, :, :], best[:, :, :], ACT.Exp).then_inc(gate_exp, 1)
            for j in range(3):
                act.wait_ge(turned, j + 1)
                nc.scalar.copy((i1T, i2T, gT)[j][:, :], ps[:, 4 + j, :]).then_inc(turned_out, 1)
            act.wait_ge(turned_out, 3)
            nc.scalar.copy(g_hi[:, :], gT[:, :]).then_inc(gates_split, 1)
            nc.scalar.preload_act_table(ACT.Gelu)
            with act.Fori(0, 8) as it:
                for s in range(8):
                    n = it * 8 + (64 + s)
                    high(n + 1, s + 1, it * 2 + (16 + (s + 1) // 4 + 1))
                    gelu(n, s, it * 64 + (16 * 32 + 16 * (1 + s // 2)))
                    for g in (2 * s, 2 * s + 1):
                        act.wait_ge(w_done, it * 16 + (g + 3))
                        if g % 8 == 0:
                            act.wait_ge(w_stored[g // 8], it * 16 + 16)
                        nc.scalar.copy(w_tile[:, g // 8, :, 4 * (g % 8):4 * (g % 8) + 4].rearrange("p i t -> p t i"),
                                       ps[:, 2 + g % 2, :].rearrange("p (t i) -> p t i", t=4)).then_inc(w_out_s, 1)

            def split_p(i2, s):
                act.wait_ge(pf_ready, i2 + 1)
                act.wait_ge(step_done, i2 + (KEYS + 1))
                nc.scalar.copy(p_hi[:, s % 2, :], p_full[:, s % 2, :]).then_inc(ph_ready, 1)

            split_p(0, 0)
            with act.Fori(0, 15) as it:
                for s in range(8):
                    i2 = it * 8 + s
                    high(i2 + (KEYS + 1), s + 1, it * 2 + (32 + (s + 1) // 4 + 1))
                    split_p(i2 + 1, s + 1)
            for s in range(7):
                i2 = KEYS - 8 + s
                high(i2 + KEYS + 1, s + 1, 62 + (s + 1) // 4 + 1)
                split_p(i2 + 1, s + 1)
            act.wait_ge(step_done, NSTEP + 2)
            act.wait_ge(lo_ready, NSTEP)
            for k in range(KD):
                nc.scalar.copy(ffn[:, k, :], ps[:, k, :]).then_inc(acc_out, 1)
            for k in range(KD):
                act.wait_ge(acc_out, k + 1)
                square(ffn[:, k, :], T)
            root(T)

        @block.vector
        def _(dve):
            chain = [0]

            def link(ins):
                chain[0] += 1
                ins.then_inc(dve_chain, 1)
                dve.wait_ge(dve_chain, chain[0])

            n_stat = [0]

            def inverse_variance(features, width):
                dve.drain()
                n_stat[0] += 1
                link(nc.vector.tensor_scalar(rstd[:, 0:width], ps[:, BANK_STAT, 0:width], 1.0 / features, EPS, ALU.mult, ALU.add))
                nc.vector.reciprocal(rstd[:, 0:width], rstd[:, 0:width]).then_inc(var_ready, 1)
                dve.wait_ge(rstd_ready, n_stat[0])

            dve.wait_ge(sq_used, 8)
            inverse_variance(D, C)
            for k in range(KD):
                ins = nc.vector.tensor_tensor(hcT[:, k, :], ctx_sb[:, k, :], rstd[:, 0:C], ALU.mult)
            dve.wait_ge(sq_used, 16)
            inverse_variance(D, T)
            for k in range(KD):
                ins = nc.vector.tensor_tensor(hT[:, k, :], x1[:, k, :], rstd[:, :], ALU.mult)
            link(ins)
            dve.wait_ge(vec_in, 16)

            def mod_tiles(a, b):
                bada = vecs[:, V_BADA + a:V_BADA + b].unsqueeze(2).to_broadcast([P, b - a, 2])
                link(nc.vector.tensor_tensor(mod[:, a:b, :], ps[:, BANK_ADA, 2 * a:2 * b].rearrange("p (n c) -> p n c", c=2),
                                             bada, ALU.add))

            wait_chunk_used(dve, ADA_FIRST - 1)
            mod_tiles(0, 16)
            for w in range(2):
                link(nc.vector.scalar_tensor_tensor(coef[:, w, :], mod[:, SC1:SC1 + 8, w], 1.0, vecs[:, V_PREMIX:V_PREMIX + 8],
                                                    ALU.add, ALU.mult))
            for k in range(KD):
                nc.vector.tensor_scalar(hT[:, k, :], hT[:, k, :], coef[:, 0, k:k + 1], mod[:, SH1 + k, 0:1],
                                        ALU.mult, ALU.add).then_inc(hx_ready, 1)
            for k in range(KD):
                nc.vector.tensor_scalar(hcT[:, k, :], hcT[:, k, :], coef[:, 1, k:k + 1], mod[:, SH1 + k, 1:2],
                                        ALU.mult, ALU.add).then_inc(hc_ready, 1)
            for c in range(KC):
                dve.wait_ge(tile_out_act, tile_count[tile_no["conv_g", c]])
                ci = conv_in[:, c, TAPS // 2:TAPS // 2 + T]
                link(nc.vector.tensor_tensor(ci, ci, glu[:, c, :], ALU.mult))
            for c in range(KC):
                link(nc.vector.tensor_scalar(conv_acc[:, c, :], conv_in[:, c, 0:T], g2(V_DW, c * TAPS), g2(V_DWB, c),
                                             ALU.mult, ALU.add))
            for t in range(1, TAPS):
                for c in range(KC):
                    ins = nc.vector.scalar_tensor_tensor(conv_acc[:, c, :], conv_in[:, c, t:t + T], g2(V_DW, c * TAPS + t),
                                                         conv_acc[:, c, :], ALU.mult, ALU.add)
                    if t == TAPS - 1:
                        ins.then_inc(conv_summed, 1)
                    elif c == KC - 1:
                        link(ins)
            dve.wait_ge(const_in, 16 * 5)

            def rotate(x):
                dve.drain()
                link(nc.vector.stream_shuffle(glu[:, 0, :], x, SWAP))
                link(nc.vector.tensor_tensor(glu[:, 0, :], glu[:, 0, :], sin_t[:, :], ALU.mult))
                link(nc.vector.tensor_tensor(x, x, cos_t[:, :], ALU.mult))
                nc.vector.tensor_tensor(x, x, glu[:, 0, :], ALU.add).then_inc(rotated, 1)

            for i in range(2):
                dve.wait_ge(tile_out_act, tile_count[tile_no["k", i]])
                rotate(kT[:, i, 0:T])
            for i in range(KD):
                dve.wait_ge(tile_out_act, tile_count[tile_no["q", i]])
                rotate(qT[:, i, :])
            dve.drain()
            dve.wait_ge(mean_done, 1)
            link(nc.vector.tensor_scalar(rstd[:, :], ps[:, BANK_STAT, :], 1.0 / CONV, None, ALU.mult))
            for c in range(KC):
                nc.vector.tensor_tensor(conv_acc[:, c, :], conv_acc[:, c, :], rstd[:, :], ALU.subtract).then_inc(conv_centred, 1)
            dve.wait_ge(sq_used, 20)
            inverse_variance(CONV, T)
            for c in range(KC):
                ins = nc.vector.tensor_tensor(conv_acc[:, c, :], conv_acc[:, c, :], rstd[:, :], ALU.mult)
                ins.then_inc(conv_normed, 1)
            wait_chunk_used(dve, max(n for n, (k, _) in enumerate(ORDER) if k == "ada"))
            mod_tiles(16, 48)
            link(nc.vector.tensor_tensor(coef[:, 2, :], mod[:, GT1:GT1 + 8, 0], vecs[:, V_POSTMIX:V_POSTMIX + 8], ALU.mult))
            link(nc.vector.scalar_tensor_tensor(coef[:, 3, :], mod[:, SC2:SC2 + 8, 0], 1.0, vecs[:, V_PREFFN:V_PREFFN + 8],
                                                ALU.add, ALU.mult))
            link(nc.vector.tensor_tensor(coef[:, 4, :], mod[:, GT2:GT2 + 8, 0], vecs[:, V_POSTFFN:V_POSTFFN + 8], ALU.mult))
            base = chain[0]
            for a in range(2):
                with dve.Fori(0, 4) as it:
                    r = it + 4 * a
                    dve.wait_ge(q_ready, r * 2 + 2)
                    for u in range(10):
                        if u < 8:
                            w = windows(u // 2)
                            n = P * len(w)
                            col = 128 if len(w) == 5 else 256
                            mk = mask[:, 0:640] if len(w) == 5 else (mask[:, 128:640] if u // 2 == 0 else mask[:, 640:1152])
                            dve.wait_ge(s_done, r * 8 + u + 2)
                            dve.wait_ge(tb_done, r * 8 + u + 1)
                            s_ps = ps[:, 2 * (u % 2):2 * (u % 2) + 2, :].rearrange("p b n -> p (b n)")[:, col:col + n]
                            settle(dve)
                            nc.vector.tensor_tensor_reduce(out=probs[:, u % 2, 0:n], in0=s_ps, in1=mk, scale=1.0,
                                                           scalar=sink_now[:, u % 2:u % 2 + 1], op0=ALU.add, op1=ALU.max,
                                                           accum_out=small[:, u % 2:u % 2 + 1]).then_inc(dve_chain, 1)
                            dve.wait_ge(dve_chain, r * 16 + (base + u + 1 + max(0, u - 1)))
                            nc.vector.tensor_scalar(small[:, 2 + u % 2:3 + u % 2], small[:, u % 2:u % 2 + 1], -1.0, None,
                                                    ALU.mult).then_inc(neg_ready, 1)
                        if 1 <= u <= 8:
                            w = u - 1
                            dve.wait_ge(exp_done, r * 8 + w + 1)
                            dve.wait_ge(act_chain, r * 8 + w + 1)
                            nc.vector.tensor_tensor(small[:, 10 + w % 2:11 + w % 2], small[:, 4 + w % 2:5 + w % 2],
                                                    small[:, 6 + w % 2:7 + w % 2], ALU.add).then_inc(dve_chain, 1)
                            dve.wait_ge(dve_chain, r * 16 + (base + min(u + 1, 8) + w + 1))
                            nc.vector.reciprocal(small[:, 8 + w % 2:9 + w % 2],
                                                 small[:, 10 + w % 2:11 + w % 2]).then_inc(inv_ready, 1)
                        if u >= 2:
                            w = u - 2
                            n = P * len(windows(w // 2))
                            dve.wait_ge(tb_done, r * 8 + w + 3)
                            dve.wait_ge(pv_done, r * 8 + w + 1)
                            nc.vector.tensor_copy(probsT[:, w % 2, 384:n], ps[:, 5, 0:n - 384]).then_inc(tb_out, 1)
            chain[0] = base + 16 * 8
            for i in range(KD):
                n = tile_no["ya", i]
                dve.wait_ge(tile_done, n + 1)
                nc.vector.tensor_tensor(gates[:, i, :], gates[:, i, :], ps[:, tile_bank(n), :], ALU.mult).then_inc(tile_out_dve, 1)
            for i in range(KD):
                n = tile_no["yc", i]
                dve.wait_ge(tile_done, n + 1)
                nc.vector.tensor_tensor(gates[:, KD + i, :], gates[:, KD + i, :], ps[:, tile_bank(n), :],
                                        ALU.mult).then_inc(tile_out_dve, 1)
                dve.wait_ge(tile_out_dve, KD + i + 1)
                nc.vector.tensor_tensor(gates[:, i, :], gates[:, i, :], gates[:, KD + i, :], ALU.add).then_inc(z_ready, 1)
            dve.wait_ge(sq_used, 28)
            inverse_variance(D, T)
            for k in range(KD):
                link(nc.vector.tensor_tensor(mixed[:, k, :], mixed[:, k, :], rstd[:, :], ALU.mult))
            for k in range(KD):
                nc.vector.scalar_tensor_tensor(x1[:, k, :], mixed[:, k, :], coef[:, 2, k:k + 1], x1[:, k, :],
                                               ALU.mult, ALU.add).then_inc(x1_ready, 1)
            dve.wait_ge(sq_used, 36)
            inverse_variance(D, T)
            for k in range(KD):
                link(nc.vector.tensor_tensor(h2[:, k, :], x1[:, k, :], rstd[:, :], ALU.mult))
            for k in range(KD):
                nc.vector.tensor_scalar(h2[:, k, :], h2[:, k, :], coef[:, 3, k:k + 1], mod[:, SH2 + k, 0:1],
                                        ALU.mult, ALU.add).then_inc(h2_ready, 1)
            for k in range(KD):
                dve.wait_ge(h2_split, k + 1)
                nc.vector.tensor_tensor(h2_lo[:, k, :], h2[:, k, :], h2_hi[:, k, :].bitcast(fp32), ALU.subtract).then_inc(h2_parts, 1)

            def low(n, s):
                dve.wait_ge(hi_ready, n + 1)
                nc.vector.tensor_tensor(st_lo[:, s % 2, :], raw[:, s % 4, :], st_hi[:, s % 2, :].bitcast(fp32),
                                        ALU.subtract).then_inc(lo_ready, 1)

            low(0, 0)
            dve.wait_ge(sc_out, 2 * PEER_HEADS)
            with dve.Fori(0, 16) as it:

                def lk(ins):
                    dve.drain()

                def top16(values, ix, x):
                    lk(nc.vector.max(values[:, 0:8], x))
                    nc.vector.max_index(ix[:, 0:8], values[:, 0:8], x)
                    lk(nc.vector.match_replace(x, values[:, 0:8], x, FLOOR))
                    lk(nc.vector.max(values[:, 8:16], x))
                    lk(nc.vector.max_index(ix[:, 8:16], values[:, 8:16], x))

                low(it * 4 + 1, 1)
                lk(nc.vector.tensor_copy(sc_now[:, :, :], scores[:, bass.ds(it * 4, 4), :]))
                for x in range(4):
                    top16(tops[:, x, :], top_ix[:, x, :], sc_now[:, x, :])
                    if x == 1:
                        low(it * 4 + 2, 2)
                    if x == 3:
                        low(it * 4 + 3, 3)
                lk(nc.vector.tensor_copy(top_ixf[:, :, :], top_ix[:, :, :]))
                for x in range(2):
                    lk(nc.vector.tensor_tensor(cand[:, x, :].rearrange("p (a b) -> p a b", a=TOPK),
                                               tops[:, 2 * x, :].unsqueeze(2).to_broadcast([P, TOPK, TOPK]),
                                               tops[:, 2 * x + 1, :].unsqueeze(1).to_broadcast([P, TOPK, TOPK]), ALU.add))
                    top16(best_now[:, x, :], pos[:, x, :], cand[:, x, :])
                lk(nc.vector.tensor_copy(best[:, bass.ds(it * 2, 2), :], best_now[:, :, :]))
                lk(nc.vector.tensor_scalar(pos_ab[:, 0, :, :], pos[:, :, :], 4, None, ALU.logical_shift_right))
                lk(nc.vector.tensor_scalar(pos_ab[:, 1, :, :], pos[:, :, :], 15, None, ALU.bitwise_and))
                lk(nc.vector.tensor_copy(pos_f[:, :, :, :], pos_ab[:, :, :, :]))
                low(it * 4 + 4, 4)
                for half, dst in ((0, i1_all), (1, i2_all)):
                    for x in range(2):
                        lk(nc.vector.tensor_tensor(hit[:, x, :, :], pos_f[:, half, x, :].unsqueeze(2).to_broadcast([P, TOPK, TOPK]),
                                                   iota[:, 0:TOPK].unsqueeze(1).to_broadcast([P, TOPK, TOPK]), ALU.is_equal))
                        lk(nc.vector.tensor_tensor(hit[:, x, :, :], hit[:, x, :, :],
                                                   top_ixf[:, 2 * x + half, :].unsqueeze(1).to_broadcast([P, TOPK, TOPK]), ALU.mult))
                    lk(nc.vector.tensor_reduce(dst[:, bass.ds(it * 2, 2), :], hit[:, :, :, :], AX, ALU.add))
            link(nc.vector.tensor_copy(tops[:, 0:2, :].rearrange("p a b -> p (a b)").unsqueeze(2), best[:, :, 0:1]))
            nc.vector.tensor_tensor(best[:, :, :], best[:, :, :],
                                    tops[:, 0:2, :].rearrange("p a b -> p (a b)").unsqueeze(2).to_broadcast([P, 32, TOPK]),
                                    ALU.subtract).then_inc(picked, 1)
            dve.wait_ge(gate_exp, 1)
            link(nc.vector.tensor_reduce(e_sum[:, 0, :], best[:, :, :], AX, ALU.add))
            link(nc.vector.reciprocal(e_sum[:, 1, :], e_sum[:, 0, :]))
            nc.vector.tensor_tensor(best[:, :, :], best[:, :, :], e_sum[:, 1, :].unsqueeze(2).to_broadcast([P, 32, TOPK]),
                                    ALU.mult).then_inc(gate_ready, 1)
            dve.wait_ge(gates_split, 1)
            link(nc.vector.tensor_tensor(g_lo[:, :], gT[:, :], g_hi[:, :].bitcast(fp32), ALU.subtract))
            with dve.Fori(0, 8) as it:
                dve.drain()
                dve.wait_ge(b_ready, it * 16 + 1)
                for j, src in ((0, i1T), (2, g_hi), (3, g_lo)):
                    s_ = src[:, bass.ds(it * 64, 64)]
                    nc.vector.tensor_copy(now[:, j, :], s_.bitcast(fp32) if src is g_hi else s_)
                nc.vector.tensor_copy(now[:, 1, :], i2T[:, bass.ds(it * 64, 64)]).then_inc(now_ready, 3)
                dve.drain()
                for s in range(8):
                    low(it * 8 + (64 + s + 1), s + 1)
                    for g in (2 * s, 2 * s + 1):
                        dve.wait_ge(w_done, it * 16 + (g + 1))
                        for j in range(4):
                            t = 4 * g + j
                            for dst, row in ((one_hi, 2), (one_lo, 3)):
                                ins = nc.vector.tensor_scalar(dst[:, g % 2, j, :], iota[:, :], now[:, 0, t:t + 1],
                                                              now[:, row, t:t + 1], ALU.is_equal, ALU.mult)
                        ins.then_inc(a_ready, 1)
            dve.wait_ge(w_done, T // 4 + 2)
            nc.vector.memset(zeros[:, :], 0.0).then_inc(zero_ready, 1)

            def product(i2, s, acts, ws):
                dve.wait_ge(act_loaded[s % 4], acts)
                dve.wait_ge(w_loaded[(s // 4) % 2], ws)
                nc.vector.tensor_tensor(p_full[:, s % 2, :].rearrange("p (t s) -> p t s", s=32),
                                        act_in[:, s % 4, :].rearrange("p (t s) -> p t s", s=32),
                                        w_in[:, (s // 4) % 2, :, s % 4, :], ALU.mult).then_inc(pf_ready, 1)

            def low_p(i2, s):
                dve.wait_ge(ph_ready, i2 + 1)
                nc.vector.tensor_tensor(p_lo[:, s % 2, :], p_full[:, s % 2, :], p_hi[:, s % 2, :].bitcast(fp32),
                                        ALU.subtract).then_inc(pl_ready, 1)

            product(0, 0, 16, 16)
            low_p(0, 0)
            with dve.Fori(0, 15) as it:
                for s in range(8):
                    i2 = it * 8 + s
                    product(i2 + 1, s + 1, it * 32 + 16 * (1 + (s + 1) // 4), it * 16 + (16 if s < 7 else 32))
                    low(i2 + (KEYS + 1), s + 1)
                    low_p(i2 + 1, s + 1)
            for s in range(7):
                i2 = KEYS - 8 + s
                product(i2 + 1, s + 1, 15 * 32 + 16 * (1 + (s + 1) // 4), 16 * 16)
                low(i2 + KEYS + 1, s + 1)
                low_p(i2 + 1, s + 1)
            dve.wait_ge(sq_used, 44)
            inverse_variance(D, T)
            for k in range(KD):
                link(nc.vector.tensor_tensor(ffn[:, k, :], ffn[:, k, :], rstd[:, :], ALU.mult))
                nc.vector.scalar_tensor_tensor(x1[:, k, :], ffn[:, k, :], coef[:, 4, k:k + 1], x1[:, k, :],
                                               ALU.mult, ALU.add).then_inc(final_ready, 1)

        @block.tensor
        def _(pe):
            n_sq = [0]

            def sum_squares(count, width):
                for k in range(count):
                    pe.wait_ge(sq_ready, n_sq[0] + 1)
                    ins = nc.tensor.matmul(ps[:, BANK_STAT, 0:width], ones[:, :], sq[:, n_sq[0] % 2, 0:width],
                                           start=k == 0, stop=k == count - 1)
                    ins.then_inc(sq_used, 1)
                    n_sq[0] += 1

            def attention():
                for t in range(tile[0] - 4, tile[0]):
                    wait_tile_out(pe, t)
                pe.wait_ge(rotated, 10)
                pe.sem_inc(s_done, 1)
                pe.sem_inc(tb_done, 2)
                pe.sem_inc(pv_done, 2)
                pe.sem_inc(ta_out, 1)
                pe.sem_inc(tb_out, 1)
                pe.sem_inc(y_out, 1)
                for a in range(2):
                    with pe.Fori(0, 4) as it:
                        r = it + 4 * a

                        def scores_of(u):
                            qb, s = u // 2, u % 2
                            rows = slice(64 * s, 64 * s + 64)
                            w = windows(qb)
                            lo = w[0] * P
                            width = P * (len(w) - 2)
                            col = 128 if len(w) == 5 else 256
                            q = q_now[rows, qb * P:(qb + 1) * P]
                            nc.tensor.matmul(ps[:, 2 * (u % 2), col:512], q, kT[rows, a, lo:lo + width], start=True, stop=True)
                            nc.tensor.matmul(ps[:, 2 * (u % 2) + 1, 0:C], q, kT[rows, a, T:T + C],
                                             start=True, stop=True).then_inc(s_done, 1)

                        def times_v(u):
                            qb, s = u // 2, u % 2
                            w = windows(qb)
                            pe.wait_ge(ta_out, r * 8 + u + 2)
                            pe.wait_ge(tb_out, r * 8 + u + 2)
                            if u == 0:
                                pe.wait_ge(y_out, r + 1)
                            g = 2 * a + s
                            for i, b in enumerate(w):
                                ins = nc.tensor.matmul(ps[64 * s:64 * s + 64, 6, qb * P:(qb + 1) * P], v_sb[:, b, g * HD:(g + 1) * HD],
                                                       probsT[:, u % 2, i * P:(i + 1) * P], start=i == 0, stop=i == len(w) - 1)
                            ins.then_inc(pv_done, 1)

                        pe.wait_ge(q_ready, r * 2 + 1)
                        scores_of(0)
                        scores_of(1)
                        for u in range(8):
                            pe.wait_ge(p_ready, r * 8 + u + 1)
                            pe.wait_ge(ta_out, r * 8 + u + 1)
                            pe.wait_ge(tb_out, r * 8 + u + 1)
                            for i in range(len(windows(u // 2))):
                                dst = ps[:, 4, i * P:(i + 1) * P] if i < 3 else ps[:, 5, (i - 3) * P:(i - 2) * P]
                                ins = nc.tensor.transpose(dst, probs[:, u % 2, i * P:(i + 1) * P], ident[:, :])
                                if i == 2:
                                    ins.then_inc(ta_done, 1)
                            ins.then_inc(tb_done, 1)
                            if u >= 1:
                                times_v(u - 1)
                            if u + 2 < 8:
                                scores_of(u + 2)
                        times_v(7)

            tile = [0]
            pe.wait_ge(filled, 1)
            sum_squares(KD, C)
            pe.wait_ge(var_ready, 1)
            sum_squares(KD, T)
            pe.wait_ge(cond_ready, 1)

            for n, (kind, m) in enumerate(ORDER):
                slot = n % RING
                pe.wait_ge(chunk_in[slot], 16 * (n // RING + 1))
                w = ring[:, slot, :, :]

                def product(pairs, width):
                    t = tile[0]
                    if t >= 4:
                        wait_tile_out(pe, t - 4)
                    for i, (a, b) in enumerate(pairs):
                        ins = nc.tensor.matmul(ps[:, tile_bank(t), 0:width], a, b, start=i == 0, stop=i == len(pairs) - 1)
                    ins.then_inc(tile_done, 1)
                    tile[0] += 1
                    return ins

                if kind == "ada":
                    for i in range(4):
                        t = 4 * m + i
                        for k in range(KD):
                            ins = nc.tensor.matmul(ps[:, BANK_ADA, 2 * t:2 * t + 2], w[:, k, i * P:(i + 1) * P], cond[:, k, :],
                                                   start=k == 0, stop=k == KD - 1)
                    ins.then_inc(ada_used, 1)
                    continue
                if kind in ("conv_a", "conv_g", "q0", "q1") or kind.startswith("gate"):
                    if kind == "conv_a":
                        pe.wait_ge(hx_ready, KD)
                    for i in range(4):
                        product([(w[:, k, i * P:(i + 1) * P], hT[:, k, :]) for k in range(KD)], T)
                elif kind == "kv":
                    pe.wait_ge(hc_ready, KD)
                    for i in range(2):
                        product([(w[:, k, i * P:(i + 1) * P], hT[:, k, :]) for k in range(KD)], T)
                    for i in range(2):
                        product([(w[:, k, i * P:(i + 1) * P], hcT[:, k, :]) for k in range(KD)], C)
                    for i in range(4):
                        product([(hT[:, k, i * P:(i + 1) * P], w[:, k, 256:512]) for k in range(KD)], 256)
                    for i in range(2):
                        product([(hcT[:, k, i * P:(i + 1) * P], w[:, k, 256:512]) for k in range(KD)], 256)
                elif kind == "o_attn":
                    pe.wait_ge(y_out, 8 + 1)
                    for i in range(4):
                        product([(w[:, k, i * P:(i + 1) * P], yT[:, k, :]) for k in range(KD)], T)
                elif kind == "o_conv":
                    pe.wait_ge(conv_out, KC)
                    wo = w.rearrange("p k n -> p (k n)").rearrange("p (k n) -> p k n", k=KC)
                    for i in range(8):
                        product([(wo[:, k, i * P:(i + 1) * P], conv_acc[:, k, :]) for k in range(KC)], T)
                elif kind == "out":
                    for i in range(4):
                        pe.wait_ge(z_ready, KD)
                        product([(w[:, k, i * P:(i + 1) * P], gates[:, k, :]) for k in range(KD)], T)
                        t = 4 * m + i
                        if t >= 1:
                            pe.wait_ge(sq_ready, n_sq[0] + 1)
                            nc.tensor.matmul(ps[:, BANK_STAT, :], ones[:, :], sq[:, n_sq[0] % 2, :], start=t == 1,
                                             stop=False).then_inc(sq_used, 1)
                            n_sq[0] += 1
                elif kind == "wq":
                    for i in range(4):
                        if m == 0 and i == 0:
                            pe.wait_ge(h2_ready, KD)
                            pe.wait_ge(keys_in, 16)
                        product([(w[:, k, i * P:(i + 1) * P], h2[:, k, :]) for k in range(KD)], T)
                        t = 4 * m + i
                        wait_tile_out(pe, tile_no["peer", t])
                        if t >= 2:
                            pe.wait_ge(sc_out, t - 1)
                        for x in range(TT):
                            ins = nc.tensor.matmul(ps[:, 4 + t % 2, x * P:(x + 1) * P], q_peer[:, t % 2, x * P:(x + 1) * P],
                                                   keys[:, t, :], start=True, stop=True)
                        ins.then_inc(sc_done, 1)
                if kind == "gate2":
                    pe.wait_ge(conv_summed, KC)
                    pe.wait_ge(var_ready, 2)
                    for c in range(KC):
                        ins = nc.tensor.matmul(ps[:, BANK_STAT, :], ones[:, :], conv_acc[:, c, :], start=c == 0, stop=c == KC - 1)
                    ins.then_inc(mean_done, 1)
                if kind == "gate3":
                    pe.wait_ge(conv_centred, KC)
                    sum_squares(KC, T)
                    attention()
                if kind == "out" and m == 1:
                    pe.wait_ge(sq_ready, n_sq[0] + 1)
                    nc.tensor.matmul(ps[:, BANK_STAT, :], ones[:, :], sq[:, n_sq[0] % 2, :], start=False,
                                     stop=True).then_inc(sq_used, 1)
                    n_sq[0] += 1
                    pe.wait_ge(var_ready, 4)
                    sum_squares(KD, T)

            pe.wait_ge(var_ready, 5)
            pe.wait_ge(h2_parts, KD)
            pe.wait_ge(tile_out_act, sum(e == "act" for _, _, e in tiles))
            pe.wait_ge(sc_out, 2 * PEER_HEADS)
            pe.sem_inc(step_done, 2)

            def act_step(n, s):
                pe.wait_ge(lo_ready, n + 1)
                pe.wait_ge(gelu_done, n + 1)
                for k in range(KD):
                    hi, lo = st_hi[:, s % 2, k * P:(k + 1) * P], st_lo[:, s % 2, k * P:(k + 1) * P]
                    for i, (a, b) in enumerate(((hi, h2_hi), (hi, h2_lo), (lo, h2_hi))):
                        ins = nc.tensor.matmul(ps[:, s % 2, :], a, b[:, k, :], start=k == 0 and i == 0,
                                               stop=k == KD - 1 and i == 2)
                ins.then_inc(step_done, 1)

            with pe.Fori(0, 16) as it:
                for s in range(4):
                    act_step(it * 4 + s, s)
            pe.wait_ge(gate_ready, 1)
            for j, src in enumerate((i1_all, i2_all, best)):
                for x in range(TT):
                    ins = nc.tensor.transpose(ps[:, 4 + j, x * P:(x + 1) * P],
                                              src[:, 8 * x:8 * x + 8, :].rearrange("p a b -> p (a b)"), ident[:, :])
                ins.then_inc(turned, 1)
            pe.sem_inc(w_done, 2)
            with pe.Fori(0, 8) as it:
                for s in range(8):
                    n = it * 8 + (64 + s)
                    act_step(n, s)
                    for g in (2 * s, 2 * s + 1):
                        pe.wait_ge(a_ready, it * 16 + (g + 1))
                        pe.wait_ge(b_ready, it * 16 + (g + 2))
                        pe.wait_ge(w_out_s, it * 16 + (g + 1))
                        for j in range(4):
                            for i, a in enumerate((one_hi, one_lo)):
                                ins = nc.tensor.matmul(ps[:, 2 + g % 2, j * P:(j + 1) * P], a[:, g % 2, j, :],
                                                       one_b[:, g % 2, j, :], start=i == 0, stop=i == 1)
                        ins.then_inc(w_done, 1)
            pe.wait_ge(gelu_done, KEYS + 2)
            pe.wait_ge(w_out_s, T // 4 + 2)
            pe.wait_ge(zero_ready, 1)
            for d in range(KD):
                nc.tensor.matmul(ps[:, d, :], zeros[:, 0:P], zeros[:, :], start=True, stop=False)

            def out_step(i2, s, last):
                pe.wait_ge(lo_ready, i2 + (KEYS + 1))
                pe.wait_ge(pl_ready, i2 + 1)
                for d in range(KD):
                    hi, lo = st_hi[:, s % 2, d * P:(d + 1) * P], st_lo[:, s % 2, d * P:(d + 1) * P]
                    for i, (a, b) in enumerate(((hi, p_hi), (hi, p_lo), (lo, p_hi))):
                        ins = nc.tensor.matmul(ps[:, d, :], a, b[:, s % 2, :], start=False, stop=last and i == 2)
                ins.then_inc(step_done, 1)

            with pe.Fori(0, 15) as it:
                for s in range(8):
                    out_step(it * 8 + s, s, False)
            for s in range(8):
                out_step(KEYS - 8 + s, s, s == 7)
            pe.wait_ge(acc_out, KD)
            sum_squares(KD, T)


def fixed_tables():
    t = np.arange(T, dtype=np.int32)
    place = [(t // GRID_W).astype(np.float32), (t % GRID_W).astype(np.float32)]
    half = HD // 4
    freqs = (np.float32(10000.0) ** (-np.arange(0, HD // 2, 2, dtype=np.float32) / np.float32(HD // 2))).astype(np.float32)
    cos, sin = np.zeros((P, T), np.float32), np.zeros((P, T), np.float32)
    for p in range(P):
        d = p % HD
        angle = place[d // (HD // 2)] * freqs[d % half]
        cos[p] = np.cos(angle)
        sin[p] = np.sin(angle) * (-1 if d % (HD // 2) < half else 1)
    q, k = np.arange(P)[:, None], np.arange(P)[None, :]
    before = np.where(k >= q, 0.0, NEG).astype(np.float32)
    after = np.where(k <= q, 0.0, NEG).astype(np.float32)
    free = np.zeros((P, P), np.float32)
    mask = np.concatenate([before, free, after, free, free, before, free, free, free], axis=1)
    return np.concatenate([np.eye(P, dtype=np.float32), np.tile(np.arange(P, dtype=np.float32), (P, 1)), cos, sin, mask], axis=1)


def columns(v):
    return np.asarray(v).reshape(-1, P).T


def lay_out(inputs):
    a = {k: np.asarray(v) for k, v in inputs.items()}

    def chunk(m):
        return m.reshape(-1, P, m.shape[1]).transpose(1, 0, 2).reshape(P, KD * CHUNK)

    w_in = a["w_in"][0]
    kv0 = HEADS * HD
    conv0 = kv0 + 2 * KV_HEADS * HD
    gate0 = conv0 + 2 * CONV
    q_cols = np.concatenate([np.arange(h * HD, (h + 1) * HD) for h in HEAD_ORDER])
    parts = {
        "ada": a["w_ada"][0], "conv_a": w_in[:, conv0:conv0 + CONV], "conv_g": w_in[:, conv0 + CONV:gate0],
        "kv": w_in[:, kv0:conv0], "q0": w_in[:, q_cols[:512]], "q1": w_in[:, q_cols[512:]],
        "o_attn": a["w_o_attn"][0][q_cols], "o_conv": a["w_o_conv"][0], "out": a["w_out"][0], "wq": a["peer_wq"][0],
    }
    for i in range(4):
        parts[f"gate{i}"] = w_in[:, gate0 + i * CHUNK:gate0 + (i + 1) * CHUNK]
    wchunks = np.stack([chunk(parts[k] if k == "o_conv" else parts[k][:, n * CHUNK:(n + 1) * CHUNK]) for k, n in ORDER])
    dw = a["conv_dw"][0].T.reshape(KC, P, TAPS).transpose(1, 0, 2).reshape(P, KC * TAPS)
    vec = np.concatenate([columns(a["b_ada"][0]), columns(a["g_pre_mix"][0]), columns(a["g_post_mix"][0]),
                          columns(a["g_pre_ffn"][0]), columns(a["g_post_ffn"][0]), dw, columns(a["conv_dw_b"][0]),
                          columns(a["conv_ln_g"][0]), columns(a["conv_ln_b"][0]),
                          np.tile(a["attn_sink"][0][HEAD_ORDER][None, :], (P, 1))], axis=1)
    rows = np.empty((NSTEP, P, ROW), a["peer_u"].dtype)
    u = a["peer_u"][0].reshape(KEYS, KEYS, KD, P)
    rows[:KEYS] = u.transpose(1, 3, 2, 0).reshape(KEYS, P, ROW)
    rows[KEYS:] = a["peer_v"][0].reshape(KEYS, KEYS, D).transpose(1, 0, 2)
    return {
        "xT": a["x"][0].T.reshape(KD, P, T).transpose(1, 0, 2),
        "ctxT": a["ctx"][0].T.reshape(KD, P, C).transpose(1, 0, 2),
        "cc": np.stack([columns(a["c"][0]), columns(a["c_ctx"])], axis=2),
        "wchunks": wchunks.reshape(len(ORDER), P, KD, CHUNK),
        "vec": vec,
        "keysT": a["peer_keys"][0].reshape(2 * PEER_HEADS, KEYS, P).transpose(2, 0, 1),
        "expert_rows": rows,
        "consts": fixed_tables(),
    }


def kernel(**inputs):
    import concourse.bacc as bacc
    from concourse.bass_utils import run_bass_kernel_spmd

    nc = bacc.Bacc("TRN2", target_bir_lowering=False, num_devices=1)
    arrays, args = {}, {}
    for name, a in lay_out(inputs).items():
        arrays[name] = np.ascontiguousarray(a)
        args[name] = nc.dram_tensor(name, arrays[name].shape, mybir.dt.from_np(arrays[name].dtype), kind="ExternalInput").ap()
    out = nc.dram_tensor("outT", (P, KD, T), mybir.dt.float32, kind="ExternalOutput").ap()
    layer_kernel(nc, out=out, **args)
    r = run_bass_kernel_spmd(nc, [arrays], core_ids=[0])
    return np.asarray(r.results[0]["outT"]).transpose(2, 1, 0).reshape(1, T, D)
```

```python
from contextlib import ExitStack

import numpy as np

import concourse.bass as bass
from concourse import mybir

D = 1024
T = 512
C = 256
P = 128
KD = D // P
TT = T // P
GRID_W = 64
HEADS, KV_HEADS, HD = 16, 4, 64
GROUP = HEADS // KV_HEADS
CONV = 512
KC = CONV // P
TAPS = 31
PEER_HEADS, KEYS, TOPK = 8, 128, 16
EPS = 1e-6
NEG = -1e30
FLOOR = -3.0e38

CHUNK = 512
RING = 3
N_ADA = 6 * D // CHUNK
ADA_FIRST = 4
ORDER = [("ada", n) for n in range(ADA_FIRST)]
ORDER += [(kind, 0) for kind in ("conv_a", "conv_g", "kv", "q0", "q1", "gate0", "gate1", "gate2", "gate3")]
ORDER += [("ada", 4), ("ada", 5), ("o_attn", 0), ("o_attn", 1), ("o_conv", 0), ("out", 0), ("out", 1)]
ORDER += [("ada", n) for n in range(6, N_ADA)] + [("wq", n) for n in range(4)]

V_BADA, V_PREMIX, V_POSTMIX, V_PREFFN, V_POSTFFN = 0, 48, 56, 64, 72
V_DW, V_DWB, V_LNG, V_LNB, V_SINK, V_N = 80, 204, 208, 212, 216, 232
SH1, SC1, GT1, SH2, SC2, GT2 = (8 * n for n in range(6))
SWAP = [(i + 16) % 32 for i in range(32)]
HEAD_ORDER = [GROUP * (2 * a + s) + j for a in range(2) for j in range(GROUP) for s in range(2)]

NSTEP = 2 * KEYS
ROW = KD * P


class Step:

    def __init__(self, it, K, c):
        self.it, self.K, self.c = it, K, c
        self.n = it * K + c if K else c
        self.pairs = it * (K // 2) + (c // 2 + 1) if K else c // 2 + 1
        self.fours = it * (K // 4) + (c // 4 + 1) if K else c // 4 + 1

    def plus(self, k):
        return Step(self.it, self.K, self.c + k)


def alone(n):
    return Step(0, 0, n)


def windows(qb):
    return list(range(max(0, qb - 1), min(TT - 1, qb + 1) + 1)) + [TT, TT + 1]


def layer_kernel(nc, xT, ctxT, cc, wchunks, vec, keysT, expert_rows, consts, out):
    fp32 = mybir.dt.float32
    f32r = mybir.dt.float32r
    u32 = mybir.dt.uint32
    ALU = mybir.AluOpType
    ACT = mybir.ActivationFunctionType
    AX = mybir.AxisListType.X

    act_dram = nc.dram_tensor("act_dram", [KEYS, P, T], fp32).ap()
    w_dram = nc.dram_tensor("w_dram", [T // 32, P, KEYS, 32], fp32).ap()

    ctx = ExitStack()
    with ctx:
        BASE = 16512
        ctx.enter_context(nc.sbuf_tensor("slab", [P, (229344 - BASE) // 4], fp32))
        top = [BASE]

        def at(name, shape, offset, dt=fp32):
            return nc.alloc_sbuf_tensor_at(name, [P, *shape], dt, offset=offset)

        def take(n):
            top[0] += n
            return top[0] - n

        KB = 1024
        x1 = at("x1", [KD, T], take(16 * KB))
        vecs = at("vecs", [V_N], take(KB))
        mod = at("mod", [48, 2], take(512))
        ident = at("ident", [P], take(512))
        iota = at("iota", [P], take(512))
        ones = at("ones", [P], take(512))
        cond = at("cond", [KD, 2], take(64))
        coef = at("coef", [6, KD], take(256))
        rstd = at("rstd", [T], take(2 * KB))
        sq = at("sq", [2, T], take(4 * KB))
        small = at("small", [256], take(KB))
        r_ring, r_h, r_ctx, r_q, r_gate = take(RING * 16 * KB), take(16 * KB), take(16 * KB), take(16 * KB), take(32 * KB)
        r_tail = take(46 * KB)
        assert top[0] <= 229368, top[0]
        ring = at("ring", [RING, KD, CHUNK], r_ring)
        hT = at("hT", [KD, T], r_h)
        yT = at("yT", [KD, T], r_h)
        mixed = at("mixed", [KD, T], r_h)
        ctx_sb = at("ctx_sb", [KD, C], r_ctx)
        hcT = at("hcT", [KD, C], r_ctx + 8 * KB)
        probs = at("probs", [4, 640], r_ctx)
        probsT = at("probsT", [2, 640], r_ctx + 10240)
        qT = at("qT", [KD, T], r_q)
        gates = at("gates", [2 * KD, T], r_gate)
        kT = at("kT", [2, T + C], r_tail)
        v_sb = at("v_sb", [6, 256], r_tail + 6144)
        u_w = T + TAPS - 1
        conv_in = at("conv_in", [KC, u_w], r_tail + 12288)
        conv_acc = at("conv_acc", [KC, T], r_tail + 12288 + 4 * KC * u_w)
        o = r_tail + 12288 + 4 * KC * u_w + 8 * KB
        cos_t = at("cos_t", [T], o)
        sin_t = at("sin_t", [T], o + 2048)
        mask = at("mask", [640 + 512], o + 4096)
        glu = at("glu", [KC, T], o + 4096 + 4608)
        assert o + 4096 + 4608 + 8 * KB <= r_tail + 46 * KB
        h2 = at("h2", [KD, T], r_q)
        h2_hi = at("h2_hi", [KD, T], r_gate, f32r)
        h2_lo = at("h2_lo", [KD, T], r_gate + 16 * KB, f32r)
        scores = at("scores", [TT * PEER_HEADS * 2, KEYS], r_h)
        keys = at("keys", [2 * PEER_HEADS, KEYS], r_tail)
        q_peer = at("q_peer", [2, T], r_tail + 8 * KB)
        raw = at("raw", [4, ROW], r_tail + 12 * KB)
        st_hi = at("st_hi", [2, ROW], r_ring, f32r)
        st_lo = at("st_lo", [2, ROW], r_ring + 8 * KB, f32r)
        w_tile = at("w_tile", [2, KEYS, 32], r_ring + 16 * KB)
        o = r_tail + 28 * KB
        best = at("best", [32, TOPK], o)
        i1_all = at("i1_all", [32, TOPK], o + 2 * KB)
        i2_all = at("i2_all", [32, TOPK], o + 4 * KB)
        sc_now = at("sc_now", [4, KEYS], o + 6 * KB)
        cand = at("cand", [2, TOPK * TOPK], o + 8 * KB)
        hit = at("hit", [2, TOPK, TOPK], o + 10 * KB)
        p_lo = at("p_lo", [2, T], o + 12 * KB, f32r)
        tops = at("tops", [4, TOPK], o + 16 * KB)
        top_ix = at("top_ix", [4, TOPK], o + 16 * KB + 256, u32)
        top_ixf = at("top_ixf", [4, TOPK], o + 16 * KB + 512)
        best_now = at("best_now", [2, TOPK], o + 16 * KB + 768)
        pos = at("pos", [2, TOPK], o + 16 * KB + 896, u32)
        pos_ab = at("pos_ab", [2, 2, TOPK], o + 16 * KB + 1024, u32)
        pos_f = at("pos_f", [2, 2, TOPK], o + 16 * KB + 1280)
        e_sum = at("e_sum", [2, 32], o + 16 * KB + 1536)
        act_out = at("act_out", [2, T], r_q)
        i1T = at("i1T", [T], r_q + 4 * KB)
        i2T = at("i2T", [T], r_q + 6 * KB)
        gT = at("gT", [T], r_q + 8 * KB)
        now = at("now", [3, 128], r_q + 10 * KB)
        one_a = at("one_a", [2, 4, P], r_h)
        one_b = at("one_b", [2, 4, P], r_h + 4 * KB)
        w_in = at("w_in", [2, 16, 4, 32], r_h + 12 * KB)
        p_full = at("p_full", [2, T], r_h + 28 * KB)
        act_in = at("act_in", [4, T], r_q + 4 * KB)
        p_hi = at("p_hi", [2, T], r_q + 12 * KB, f32r)
        zeros = at("zeros", [T], o + 6 * KB, mybir.dt.bfloat16)
        ffn = at("ffn", [KD, T], r_ring)
        ps = ctx.enter_context(nc.psum_tensor("ps", [P, 8, 512], fp32))
        BANK_STAT, BANK_ADA = 4, 7
        LAST_ORDER = [BANK_STAT] + [k for k in range(KD) if k != BANK_STAT]

        def sem(name):
            return ctx.enter_context(nc.semaphore(name))

        x_in, ctx_in, cc_in, vec_in, const_in, keys_in = map(sem, ("x_in", "ctx_in", "cc_in", "vec_in", "const_in", "keys_in"))
        chunk_in = [sem(f"chunk_in{i}") for i in range(RING)]
        ada_used, mod_ready = sem("ada_used"), sem("mod_ready")
        cond_ready, filled = sem("cond_ready"), sem("filled")
        sq_ready, sq_used, mean_done, var_ready, rstd_ready = map(
            sem, ("sq_ready", "sq_used", "mean_done", "var_ready", "rstd_ready"))
        hx_ready, hc_ready = sem("hx_ready"), sem("hc_ready")
        tile_done, tile_out_act, tile_out_dve = sem("tile_done"), sem("tile_out_act"), sem("tile_out_dve")
        conv_summed, conv_centred, conv_normed, conv_out = map(sem, ("conv_summed", "conv_centred", "conv_normed", "conv_out"))
        rotated = sem("rotated")
        s_done, neg_ready, exp_done, p_ready = map(sem, ("s_done", "neg_ready", "exp_done", "p_ready"))
        ta_done, tb_done, ta_out, tb_out, pv_done, y_out = map(sem, ("ta_done", "tb_done", "ta_out", "tb_out", "pv_done", "y_out"))
        z_ready, x1_ready, h2_ready, h2_split, h2_parts = map(sem, ("z_ready", "x1_ready", "h2_ready", "h2_split", "h2_parts"))
        qp_ready, sc_done, sc_out = sem("qp_ready"), sem("sc_done"), sem("sc_out")
        row_in = [sem(f"row_in{i}") for i in range(4)]
        hi_ready, step_done = sem("hi_ready"), sem("step_done")
        lo_ready = [sem(f"lo_ready{i}") for i in range(2)]
        gelu_done, act_stored = sem("gelu_done"), [sem(f"act_stored{i}") for i in range(2)]
        picked, gate_exp, gate_ready, turned, turned_out = map(sem, ("picked", "gate_exp", "gate_ready", "turned", "turned_out"))
        now_ready, b_ready, a_ready, w_done, w_out_s = map(sem, ("now_ready", "b_ready", "a_ready", "w_done", "w_out_s"))
        w_stored = [sem(f"w_stored{i}") for i in range(2)]
        w_loaded = [sem(f"w_loaded{i}") for i in range(2)]
        act_loaded = [sem(f"act_loaded{i}") for i in range(4)]
        pf_ready, ph_ready, pl_ready, acc_out, final_ready, out_done = map(
            sem, ("pf_ready", "ph_ready", "pl_ready", "acc_out", "final_ready", "out_done"))
        dve_chain, act_chain, zero_ready = sem("dve_chain"), sem("act_chain"), sem("zero_ready")
        settled = sem("settled")

        tiles, chunk_tiles = [], []
        for kind, n in ORDER:
            if kind in ("conv_a", "conv_g"):
                tiles += [(kind, i, "act") for i in range(4)]
            elif kind == "kv":
                tiles += [("k", i, "act") for i in range(2)] + [("kc", i, "act") for i in range(2)]
                tiles += [("v", i, "act") for i in range(4)] + [("vc", i, "act") for i in range(2)]
            elif kind in ("q0", "q1"):
                tiles += [("q", 4 * int(kind[1]) + i, "act") for i in range(4)]
            elif kind.startswith("gate"):
                tiles += [("gate", 4 * int(kind[4]) + i, "act") for i in range(4)]
            elif kind == "o_attn":
                tiles += [("ya", 4 * n + i, "dve") for i in range(4)]
            elif kind == "o_conv":
                tiles += [("yc", i, "dve") for i in range(8)]
            elif kind == "out":
                tiles += [("mix", 4 * n + i, "act") for i in range(4)]
            elif kind == "wq":
                tiles += [("peer", 4 * n + i, "act") for i in range(4)]
            chunk_tiles.append(len(tiles))
        tile_no = {(k, i): n for n, (k, i, _) in enumerate(tiles)}
        tile_count = []
        for n, (_, _, e) in enumerate(tiles):
            tile_count.append(sum(x == e for _, _, x in tiles[: n + 1]))

        def tile_bank(n):
            return n % 4

        def wait_tile_out(eng, n):
            eng.wait_ge(tile_out_act if tiles[n][2] == "act" else tile_out_dve, tile_count[n])

        def settle(eng):
            eng.sem_inc(settled, 1)

        def wait_chunk_used(eng, n):
            if ORDER[n][0] == "ada":
                eng.wait_ge(ada_used, sum(k == "ada" for k, _ in ORDER[: n + 1]))
            else:
                eng.wait_ge(tile_done, chunk_tiles[n])

        def wait_low(eng, step):
            eng.wait_ge(lo_ready[step.c % 2], step.pairs)

        def low_rows(eng, ops, step):
            eng.wait_ge(hi_ready, step.n + 1)
            ops.tensor_tensor(st_lo[:, step.c % 2, :], raw[:, step.c % 4, :], st_hi[:, step.c % 2, :].bitcast(fp32),
                              ALU.subtract).then_inc(lo_ready[step.c % 2], 1)

        ROUND = 12

        def groups(s):
            return range(s * 32 // ROUND, (s + 1) * 32 // ROUND)

        UNITS = [(t, qb, s) for t in range(KD) for qb in range(TT) for s in range(2)]

        def unit(n):
            t, qb, s = UNITS[n]
            return t, qb, s, windows(qb)

        def score_bank(n, w):
            col = 512 - P * (len(w) - 2)
            return ps[:, 2 * (n % 2):2 * (n % 2) + 2, :].rearrange("p b n -> p (b n)")[:, col:col + P * len(w)]

        def cell(kind, n):
            return small[:, 4 * kind + n % 4:4 * kind + n % 4 + 1]

        def g2(col, k):
            return vecs[:, col + k:col + k + 1]

        block = ctx.enter_context(nc.Block())

        @block.sync
        def _(sp):
            sp.dma_start(cond[:, :, :], cc).then_inc(cc_in, 16)
            sp.dma_start(vecs[:, :], vec).then_inc(vec_in, 16)
            sp.dma_start(x1[:, :, :], xT).then_inc(x_in, 16)
            for n in range(len(ORDER)):
                if n >= RING:
                    wait_chunk_used(sp, n - RING)
                sp.dma_start(ring[:, n % RING, :, :], wchunks[n]).then_inc(chunk_in[n % RING], 16)
                if n == ADA_FIRST:
                    sp.dma_start(ctx_sb[:, :, :], ctxT).then_inc(ctx_in, 16)
                    for dst, a, b in ((ident, 0, 128), (iota, 128, 256), (cos_t, 256, 768), (sin_t, 768, 1280), (mask, 1280, 2432)):
                        sp.dma_start(dst[:, :], consts[:, a:b]).then_inc(const_in, 16)
                if n == len(ORDER) - 4:
                    wait_tile_out(sp, tile_no["yc", 7])
                    sp.dma_start(keys[:, :, :], keysT).then_inc(keys_in, 16)
                    for s in range(4):
                        sp.dma_start(raw[:, s, :], expert_rows[s]).then_inc(row_in[s], 16)

            def load_row(step):
                wait_low(sp, step)
                sp.dma_start(raw[:, step.c % 4, :],
                             expert_rows[bass.ds(step.n + 4, 1)].rearrange("a p n -> (a p) n")).then_inc(row_in[step.c % 4], 16)

            def store_act(step):
                sp.wait_ge(gelu_done, step.n + 3)
                sp.dma_start(act_dram[bass.ds(step.n, 1)].rearrange("a p n -> (a p) n"),
                             act_out[:, step.c % 2, :]).then_inc(act_stored[step.c % 2], 16)

            with sp.Fori(0, 16) as it:
                for s in range(4):
                    load_row(Step(it, 4, s))
                    store_act(Step(it, 4, s))
            with sp.Fori(0, 4) as it:
                for s in range(ROUND):
                    load_row(Step(it, ROUND, 64 + s))
                    store_act(Step(it, ROUND, 64 + s))
                    if s % 3 == 2:
                        h = s // 3
                        sp.wait_ge(w_out_s, it * 32 + (8 * (h + 1) + 2))
                        sp.dma_start(w_dram[bass.ds(it * 4 + h, 1)].rearrange("a p i t -> (a p) (i t)"),
                                     w_tile[:, h % 2, :, :].rearrange("p i t -> p (i t)")).then_inc(w_stored[h % 2], 16)
            for s in range(2):
                sp.wait_ge(w_stored[s], 16 * (8 + 1))
            sp.wait_ge(w_done, T // 4 + 2)

            def load_w(g, h):
                sp.dma_start(w_in[:, h, :, :, :].rearrange("p t i s -> p t (i s)"),
                             w_dram[:, :, bass.ds(g * 4, 4), :].rearrange("t p i s -> p t (i s)")).then_inc(w_loaded[h], 16)

            def load_act(i2, s):
                sp.dma_start(act_in[:, s, :], act_dram[bass.ds(i2, 1)].rearrange("a p n -> (a p) n")).then_inc(act_loaded[s], 16)

            for s in range(2):
                sp.wait_ge(act_stored[s], 16 * (56 + 1))
            for s in range(4):
                load_act(s, s)
            load_w(0, 0)
            load_w(1, 1)
            with sp.Fori(0, 4) as it:
                for s in range(4):
                    load_row(Step(it, 4, 112 + s))
                    store_act(Step(it, 4, 112 + s))
            for s in range(2):
                sp.wait_ge(act_stored[s], 16 * (KEYS // 2 + 1))

            with sp.Fori(0, 15) as it:
                for s in range(8):
                    i2 = it * 8 + s
                    load_row(Step(it, 8, KEYS + s))
                    sp.wait_ge(pf_ready, i2 + 1)
                    load_act(i2 + 4, s % 4)
                    if s % 4 == 3:
                        load_w(it * 2 + (2 + s // 4), s // 4)
            for s in range(4):
                load_row(alone(NSTEP - 8 + s))
                sp.wait_ge(pf_ready, KEYS - 8 + s + 1)
                load_act(KEYS - 4 + s, s)
            for k in range(KD):
                sp.wait_ge(final_ready, k + 1)
                sp.dma_start(out[:, k, :], x1[:, k, :]).then_inc(out_done, 16)
            sp.wait_ge(out_done, 16 * KD)

        @block.gpsimd
        def _(pool):
            nc.gpsimd.memset(ones[:, :], 1.0).then_inc(filled, 1)
            nc.gpsimd.memset(conv_in[:, :, 0:TAPS // 2], 0.0).then_inc(filled, 1)
            nc.gpsimd.memset(conv_in[:, :, T + TAPS // 2:u_w], 0.0).then_inc(filled, 1)
            pool.wait_ge(vec_in, 16)
            low_rows(pool, nc.gpsimd, alone(0))
            with pool.Fori(0, 16) as it:
                for s in (2, 4):
                    low_rows(pool, nc.gpsimd, Step(it, 4, s))
            pool.sem_inc(b_ready, 1)
            with pool.Fori(0, 4) as it:
                pool.wait_ge(now_ready, it + 1)
                for g in range(32):
                    pool.wait_ge(w_done, it * 32 + (g + 1))
                    settle(pool)
                    for j in range(4):
                        ins = nc.gpsimd.tensor_scalar(one_b[:, g % 2, j, :], iota[:, :], now[:, 1, 4 * g + j:4 * g + j + 1],
                                                      None, ALU.is_equal)
                    ins.then_inc(b_ready, 1)

        @block.scalar
        def _(act):
            n_sq = [0]
            n_stat = [0]

            def square(dst_src, width):
                n = n_sq[0]
                if n >= 2:
                    act.wait_ge(sq_used, n - 1)
                nc.scalar.activation(sq[:, n % 2, 0:width], dst_src, ACT.Square).then_inc(sq_ready, 1)
                n_sq[0] += 1

            def root(width):
                n_stat[0] += 1
                act.wait_ge(var_ready, n_stat[0])
                nc.scalar.activation(rstd[:, 0:width], rstd[:, 0:width], ACT.Sqrt).then_inc(rstd_ready, 1)

            act.wait_ge(cc_in, 16)
            nc.scalar.activation(cond[:, :, :], cond[:, :, :], ACT.Silu).then_inc(cond_ready, 1)
            act.wait_ge(x_in, 16)
            for k in range(KD):
                square(x1[:, k, :], T)
            root(T)

            def drain_tiles(kinds):
                for n, (k, i, e) in enumerate(tiles):
                    if k not in kinds:
                        continue
                    act.wait_ge(tile_done, n + 1)
                    src = ps[:, tile_bank(n), :]
                    if k == "conv_a":
                        if i == 0:
                            act.wait_ge(filled, 3)
                        dst, fn, sc = conv_in[:, i, TAPS // 2:TAPS // 2 + T], ACT.Copy, 1.0
                    elif k == "conv_g":
                        dst, fn, sc = glu[:, i, :], ACT.Sigmoid, 1.0
                    elif k == "k":
                        dst, fn, sc = kT[:, i, 0:T], ACT.Copy, 1.0
                    elif k == "kc":
                        dst, src, fn, sc = kT[:, i, T:T + C], src[:, 0:C], ACT.Copy, 1.0
                    elif k == "v":
                        dst, src, fn, sc = v_sb[:, i, :], src[:, 0:256], ACT.Copy, 1.0
                    elif k == "vc":
                        dst, src, fn, sc = v_sb[:, TT + i, :], src[:, 0:256], ACT.Copy, 1.0
                    elif k == "q":
                        dst, fn, sc = qT[:, i, :], ACT.Copy, float(HD) ** -0.5
                    elif k == "gate":
                        dst, fn, sc = gates[:, i, :], ACT.Sigmoid, 1.0
                    nc.scalar.activation(dst, src, fn, scale=sc).then_inc(tile_out_act, 1)

            drain_tiles(("conv_a",))
            act.wait_ge(ctx_in, 16)
            for k in range(KD):
                square(ctx_sb[:, k, :], C)
            root(C)
            drain_tiles(("conv_g", "k", "kc", "v", "vc", "q"))
            drain_tiles(("gate",))
            act.wait_ge(conv_centred, KC)
            for c in range(KC):
                square(conv_acc[:, c, :], T)
            root(T)
            act.wait_ge(conv_normed, KC)
            for c in range(KC):
                nc.scalar.activation(conv_acc[:, c, :], conv_acc[:, c, :], ACT.Silu, bias=g2(V_LNB, c),
                                     scale=g2(V_LNG, c)).then_inc(conv_out, 1)
            for n in range(len(UNITS) + 3):
                if n < len(UNITS):
                    t, qb, s, w = unit(n)
                    act.wait_ge(neg_ready, n + 1)
                    nc.scalar.activation(probs[:, n % 4, 0:P * len(w)], probs[:, n % 4, 0:P * len(w)], ACT.Exp,
                                         bias=cell(1, n), accum_out=cell(2, n))
                    nc.scalar.activation(cell(3, n), vecs[:, V_SINK + 2 * t + s:V_SINK + 2 * t + s + 1], ACT.Exp,
                                         bias=cell(1, n)).then_inc(exp_done, 1)
                m = n - 2
                if 0 <= m < len(UNITS):
                    act.wait_ge(ta_done, m + 1)
                    if m >= 2:
                        act.wait_ge(pv_done, m - 1)
                    nc.scalar.copy(probsT[:, m % 2, 0:384], ps[:, 4, 0:384]).then_inc(ta_out, 1)
                m = n - 3
                if m >= 0 and m % 8 == 7:
                    act.wait_ge(pv_done, m + 1)
                    nc.scalar.copy(yT[:, m // 8, :], ps[:, 6 + (m // 8) % 2, :]).then_inc(y_out, 1)
            for i in range(KD):
                n = tile_no["mix", i]
                act.wait_ge(tile_done, n + 1)
                square(ps[:, tile_bank(n), :], T)
                nc.scalar.activation(mixed[:, i, :], ps[:, tile_bank(n), :], ACT.Copy, scale=coef[:, 2, i:i + 1]).then_inc(tile_out_act, 1)
            root(T)
            for k in range(KD):
                act.wait_ge(x1_ready, k + 1)
                square(x1[:, k, :], T)
            root(T)
            for k in range(KD):
                act.wait_ge(h2_ready, k + 1)
                nc.scalar.copy(h2_hi[:, k, :], h2[:, k, :]).then_inc(h2_split, 1)
            for i in range(2 * PEER_HEADS):
                n = tile_no["peer", i]
                act.wait_ge(tile_done, n + 1)
                if i >= 2:
                    act.wait_ge(sc_done, i - 1)
                nc.scalar.copy(q_peer[:, i % 2, :], ps[:, tile_bank(n), :]).then_inc(tile_out_act, 1)
                act.wait_ge(sc_done, i + 1)
                nc.scalar.copy(scores[:, i:i + 2 * PEER_HEADS * (TT - 1) + 1:2 * PEER_HEADS, :],
                               ps[:, 4 + i % 2, :].rearrange("p (t k) -> p t k", t=TT)).then_inc(sc_out, 1)

            def high(step):
                act.wait_ge(row_in[step.c % 4], step.fours * 16)
                act.wait_ge(step_done, step.n + 1)
                nc.scalar.copy(st_hi[:, step.c % 2, :], raw[:, step.c % 4, :]).then_inc(hi_ready, 1)

            def gelu(step):
                act.wait_ge(step_done, step.n + 3)
                act.wait_ge(act_stored[step.c % 2], step.pairs * 16)
                nc.scalar.activation(act_out[:, step.c % 2, :], ps[:, step.c % 2, :], ACT.Gelu).then_inc(gelu_done, 1)

            act.wait_ge(step_done, 2)
            high(alone(0))
            for x in (*act_stored, *w_stored):
                act.sem_inc(x, 16)
            act.sem_inc(gelu_done, 2)
            act.sem_inc(w_out_s, 2)
            nc.scalar.preload_act_table(ACT.Gelu)
            with act.Fori(0, 16) as it:
                for s in range(4):
                    high(Step(it, 4, s + 1))
                    gelu(Step(it, 4, s))
            act.wait_ge(picked, 1)
            nc.scalar.activation(best[:, :, :], best[:, :, :], ACT.Exp).then_inc(gate_exp, 1)
            for j in range(3):
                act.wait_ge(turned, j + 1)
                nc.scalar.copy((i1T, i2T, gT)[j][:, :], ps[:, 4 + j, :]).then_inc(turned_out, 1)
            nc.scalar.preload_act_table(ACT.Gelu)
            with act.Fori(0, 4) as it:
                for s in range(ROUND):
                    high(Step(it, ROUND, 64 + s + 1))
                    gelu(Step(it, ROUND, 64 + s))
                    for g in groups(s):
                        act.wait_ge(w_done, it * 32 + (g + 3))
                        h = g // 8
                        if g % 8 == 0:
                            act.wait_ge(w_stored[h % 2], it * 32 + 16 * (h // 2 + 1))
                        nc.scalar.copy(w_tile[:, h % 2, :, 4 * (g % 8):4 * (g % 8) + 4].rearrange("p i t -> p t i"),
                                       ps[:, 2 + g % 2, :].rearrange("p (t i) -> p t i", t=4)).then_inc(w_out_s, 1)
            with act.Fori(0, 4) as it:
                for s in range(4):
                    high(Step(it, 4, 112 + s + 1))
                    gelu(Step(it, 4, 112 + s))

            def high_p(i2, s):
                act.wait_ge(pf_ready, i2 + 1)
                act.wait_ge(step_done, i2 + (KEYS + 1))
                nc.scalar.copy(p_hi[:, s % 2, :], p_full[:, s % 2, :]).then_inc(ph_ready, 1)

            high_p(0, 0)
            with act.Fori(0, 15) as it:
                for s in range(8):
                    high(Step(it, 8, KEYS + s + 1))
                    high_p(it * 8 + (s + 1), s + 1)
            for s in range(7):
                high(alone(NSTEP - 8 + s + 1))
                high_p(KEYS - 8 + s + 1, s + 1)
            act.wait_ge(step_done, NSTEP + 2)
            for k in LAST_ORDER:
                square(ps[:, k, :], T)
            root(T)

        @block.vector
        def _(dve):
            chain = [0]

            def link(ins):
                chain[0] += 1
                ins.then_inc(dve_chain, 1)
                dve.wait_ge(dve_chain, chain[0])

            n_stat = [0]
            n_mod = [0]

            def inverse_variance(features, width):
                dve.drain()
                n_stat[0] += 1
                link(nc.vector.tensor_scalar(rstd[:, 0:width], ps[:, BANK_STAT, 0:width], 1.0 / features, EPS, ALU.mult, ALU.add))
                nc.vector.reciprocal(rstd[:, 0:width], rstd[:, 0:width]).then_inc(var_ready, 1)
                dve.wait_ge(rstd_ready, n_stat[0])

            dve.wait_ge(sq_used, 8)
            inverse_variance(D, T)
            for k in range(KD):
                ins = nc.vector.tensor_tensor(hT[:, k, :], x1[:, k, :], rstd[:, :], ALU.mult)
            link(ins)
            dve.wait_ge(vec_in, 16)

            def mod_tiles(a, b):
                bada = vecs[:, V_BADA + a:V_BADA + b].unsqueeze(2).to_broadcast([P, b - a, 2])
                n_mod[0] += 1
                nc.vector.tensor_tensor(mod[:, a:b, :], ps[:, BANK_ADA, 2 * a:2 * b].rearrange("p (n c) -> p n c", c=2),
                                        bada, ALU.add).then_inc(mod_ready, 1)
                dve.wait_ge(mod_ready, n_mod[0])

            wait_chunk_used(dve, ADA_FIRST - 1)
            mod_tiles(0, 16)
            for w in range(2):
                link(nc.vector.scalar_tensor_tensor(coef[:, w, :], mod[:, SC1:SC1 + 8, w], 1.0, vecs[:, V_PREMIX:V_PREMIX + 8],
                                                    ALU.add, ALU.mult))
            for k in range(KD):
                nc.vector.tensor_scalar(hT[:, k, :], hT[:, k, :], coef[:, 0, k:k + 1], mod[:, SH1 + k, 0:1],
                                        ALU.mult, ALU.add).then_inc(hx_ready, 1)
            dve.wait_ge(sq_used, 16)
            inverse_variance(D, C)
            for k in range(KD):
                ins = nc.vector.tensor_tensor(hcT[:, k, :], ctx_sb[:, k, :], rstd[:, 0:C], ALU.mult)
            link(ins)
            for k in range(KD):
                nc.vector.tensor_scalar(hcT[:, k, :], hcT[:, k, :], coef[:, 1, k:k + 1], mod[:, SH1 + k, 1:2],
                                        ALU.mult, ALU.add).then_inc(hc_ready, 1)
            for c in range(KC):
                dve.wait_ge(tile_out_act, tile_count[tile_no["conv_g", c]])
                ci = conv_in[:, c, TAPS // 2:TAPS // 2 + T]
                link(nc.vector.tensor_tensor(ci, ci, glu[:, c, :], ALU.mult))
            for c in range(KC):
                link(nc.vector.tensor_scalar(conv_acc[:, c, :], conv_in[:, c, 0:T], g2(V_DW, c * TAPS), g2(V_DWB, c),
                                             ALU.mult, ALU.add))
            for t in range(1, TAPS):
                for c in range(KC):
                    ins = nc.vector.scalar_tensor_tensor(conv_acc[:, c, :], conv_in[:, c, t:t + T], g2(V_DW, c * TAPS + t),
                                                         conv_acc[:, c, :], ALU.mult, ALU.add)
                    if t == TAPS - 1:
                        ins.then_inc(conv_summed, 1)
                    elif c == KC - 1:
                        link(ins)
            dve.wait_ge(const_in, 16 * 5)

            def rotate(x):
                dve.drain()
                link(nc.vector.stream_shuffle(glu[:, 0, :], x, SWAP))
                link(nc.vector.tensor_tensor(glu[:, 0, :], glu[:, 0, :], sin_t[:, :], ALU.mult))
                link(nc.vector.tensor_tensor(x, x, cos_t[:, :], ALU.mult))
                nc.vector.tensor_tensor(x, x, glu[:, 0, :], ALU.add).then_inc(rotated, 1)

            for i in range(2):
                dve.wait_ge(tile_out_act, tile_count[tile_no["k", i]])
                rotate(kT[:, i, 0:T])
            for i in range(KD):
                dve.wait_ge(tile_out_act, tile_count[tile_no["q", i]])
                rotate(qT[:, i, :])
            dve.drain()
            dve.wait_ge(mean_done, 1)
            link(nc.vector.tensor_scalar(rstd[:, :], ps[:, BANK_STAT, :], 1.0 / CONV, None, ALU.mult))
            for c in range(KC):
                nc.vector.tensor_tensor(conv_acc[:, c, :], conv_acc[:, c, :], rstd[:, :], ALU.subtract).then_inc(conv_centred, 1)
            dve.wait_ge(sq_used, 20)
            inverse_variance(CONV, T)
            for c in range(KC):
                ins = nc.vector.tensor_tensor(conv_acc[:, c, :], conv_acc[:, c, :], rstd[:, :], ALU.mult)
                ins.then_inc(conv_normed, 1)
            def wait_ada(m):
                wait_chunk_used(dve, ORDER.index(("ada", m)))

            wait_ada(5)
            mod_tiles(16, 24)
            link(nc.vector.tensor_tensor(coef[:, 2, :], mod[:, GT1:GT1 + 8, 0], vecs[:, V_POSTMIX:V_POSTMIX + 8], ALU.mult))
            for n in range(len(UNITS) + 2):
                if n < len(UNITS):
                    t, qb, s, w = unit(n)
                    size = P * len(w)
                    mk = mask[:, 0:640] if len(w) == 5 else (mask[:, 128:640] if qb == 0 else mask[:, 640:1152])
                    dve.wait_ge(s_done, n + 1)
                    if n >= 4:
                        dve.wait_ge(tb_done, n - 3)
                    nc.vector.tensor_tensor_reduce(out=probs[:, n % 4, 0:size], in0=score_bank(n, w), in1=mk, scale=1.0,
                                                   scalar=vecs[:, V_SINK + 2 * t + s:V_SINK + 2 * t + s + 1],
                                                   op0=ALU.add, op1=ALU.max, accum_out=cell(0, n))
                    dve.drain()
                    nc.vector.tensor_scalar(cell(1, n), cell(0, n), -1.0, None, ALU.mult).then_inc(neg_ready, 1)
                m = n - 1
                if 0 <= m < len(UNITS):
                    size = P * len(unit(m)[3])
                    dve.wait_ge(exp_done, m + 1)
                    nc.vector.tensor_tensor(cell(4, m), cell(2, m), cell(3, m), ALU.add)
                    dve.drain()
                    nc.vector.reciprocal(cell(5, m), cell(4, m))
                    dve.drain()
                    nc.vector.tensor_scalar(probs[:, m % 4, 0:size], probs[:, m % 4, 0:size], cell(5, m), None,
                                            ALU.mult).then_inc(p_ready, 1)
                m = n - 2
                if m >= 0:
                    size = P * len(unit(m)[3])
                    dve.wait_ge(tb_done, m + 1)
                    if m >= 2:
                        dve.wait_ge(pv_done, m - 1)
                    nc.vector.tensor_copy(probsT[:, m % 2, 384:size], ps[:, 5, 0:size - 384]).then_inc(tb_out, 1)
            for i in range(KD):
                n = tile_no["ya", i]
                dve.wait_ge(tile_done, n + 1)
                nc.vector.tensor_tensor(gates[:, i, :], gates[:, i, :], ps[:, tile_bank(n), :], ALU.mult).then_inc(tile_out_dve, 1)
            for i in range(KD):
                n = tile_no["yc", i]
                dve.wait_ge(tile_done, n + 1)
                nc.vector.tensor_tensor(gates[:, KD + i, :], gates[:, KD + i, :], ps[:, tile_bank(n), :],
                                        ALU.mult).then_inc(tile_out_dve, 1)
                dve.wait_ge(tile_out_dve, KD + i + 1)
                nc.vector.tensor_tensor(gates[:, i, :], gates[:, i, :], gates[:, KD + i, :], ALU.add).then_inc(z_ready, 1)
            dve.wait_ge(sq_used, 28)
            inverse_variance(D, T)
            for k in range(KD):
                nc.vector.tensor_tensor(mixed[:, k, :], mixed[:, k, :], rstd[:, :], ALU.mult)
                dve.drain()
                nc.vector.tensor_tensor(x1[:, k, :], mixed[:, k, :], x1[:, k, :], ALU.add).then_inc(x1_ready, 1)
            wait_ada(9)
            mod_tiles(24, 40)
            link(nc.vector.scalar_tensor_tensor(coef[:, 3, :], mod[:, SC2:SC2 + 8, 0], 1.0, vecs[:, V_PREFFN:V_PREFFN + 8],
                                                ALU.add, ALU.mult))
            dve.wait_ge(sq_used, 36)
            inverse_variance(D, T)
            for k in range(KD):
                nc.vector.scalar_tensor_tensor(h2[:, k, :], x1[:, k, :], coef[:, 3, k:k + 1], rstd[:, :], ALU.mult, ALU.mult)
                dve.drain()
                nc.vector.tensor_scalar(h2[:, k, :], h2[:, k, :], mod[:, SH2 + k, 0:1], None, ALU.add).then_inc(h2_ready, 1)
            for k in range(KD):
                dve.wait_ge(h2_split, k + 1)
                nc.vector.tensor_tensor(h2_lo[:, k, :], h2[:, k, :], h2_hi[:, k, :].bitcast(fp32), ALU.subtract).then_inc(h2_parts, 1)
            wait_ada(11)
            mod_tiles(40, 48)
            link(nc.vector.tensor_tensor(coef[:, 4, :], mod[:, GT2:GT2 + 8, 0], vecs[:, V_POSTFFN:V_POSTFFN + 8], ALU.mult))

            dve.wait_ge(sc_out, 2 * PEER_HEADS)
            with dve.Fori(0, 16) as it:

                def lk(ins):
                    dve.drain()

                def top16(values, ix, x):
                    lk(nc.vector.max(values[:, 0:8], x))
                    nc.vector.max_index(ix[:, 0:8], values[:, 0:8], x)
                    lk(nc.vector.match_replace(x, values[:, 0:8], x, FLOOR))
                    lk(nc.vector.max(values[:, 8:16], x))
                    lk(nc.vector.max_index(ix[:, 8:16], values[:, 8:16], x))

                low_rows(dve, nc.vector, Step(it, 4, 1))
                lk(nc.vector.tensor_copy(sc_now[:, :, :], scores[:, bass.ds(it * 4, 4), :]))
                for x in range(4):
                    top16(tops[:, x, :], top_ix[:, x, :], sc_now[:, x, :])
                lk(nc.vector.tensor_copy(top_ixf[:, :, :], top_ix[:, :, :]))
                low_rows(dve, nc.vector, Step(it, 4, 3))
                for x in range(2):
                    lk(nc.vector.tensor_tensor(cand[:, x, :].rearrange("p (a b) -> p a b", a=TOPK),
                                               tops[:, 2 * x, :].unsqueeze(2).to_broadcast([P, TOPK, TOPK]),
                                               tops[:, 2 * x + 1, :].unsqueeze(1).to_broadcast([P, TOPK, TOPK]), ALU.add))
                    top16(best_now[:, x, :], pos[:, x, :], cand[:, x, :])
                nc.vector.tensor_copy(best[:, bass.ds(it * 2, 2), :], best_now[:, :, :])
                nc.vector.tensor_scalar(pos_ab[:, 0, :, :], pos[:, :, :], 4, None, ALU.logical_shift_right)
                lk(nc.vector.tensor_scalar(pos_ab[:, 1, :, :], pos[:, :, :], 15, None, ALU.bitwise_and))
                lk(nc.vector.tensor_copy(pos_f[:, :, :, :], pos_ab[:, :, :, :]))
                for half, dst in ((0, i1_all), (1, i2_all)):
                    for x in range(2):
                        nc.vector.tensor_tensor(hit[:, x, :, :], pos_f[:, half, x, :].unsqueeze(2).to_broadcast([P, TOPK, TOPK]),
                                                iota[:, 0:TOPK].unsqueeze(1).to_broadcast([P, TOPK, TOPK]), ALU.is_equal)
                    dve.drain()
                    for x in range(2):
                        nc.vector.tensor_tensor(hit[:, x, :, :], hit[:, x, :, :],
                                                top_ixf[:, 2 * x + half, :].unsqueeze(1).to_broadcast([P, TOPK, TOPK]), ALU.mult)
                    dve.drain()
                    lk(nc.vector.tensor_reduce(dst[:, bass.ds(it * 2, 2), :], hit[:, :, :, :], AX, ALU.add))
            link(nc.vector.tensor_copy(tops[:, 0:2, :].rearrange("p a b -> p (a b)").unsqueeze(2), best[:, :, 0:1]))
            nc.vector.tensor_tensor(best[:, :, :], best[:, :, :],
                                    tops[:, 0:2, :].rearrange("p a b -> p (a b)").unsqueeze(2).to_broadcast([P, 32, TOPK]),
                                    ALU.subtract).then_inc(picked, 1)
            dve.wait_ge(gate_exp, 1)
            link(nc.vector.tensor_reduce(e_sum[:, 0, :], best[:, :, :], AX, ALU.add))
            link(nc.vector.reciprocal(e_sum[:, 1, :], e_sum[:, 0, :]))
            nc.vector.tensor_tensor(best[:, :, :], best[:, :, :], e_sum[:, 1, :].unsqueeze(2).to_broadcast([P, 32, TOPK]),
                                    ALU.mult).then_inc(gate_ready, 1)
            dve.wait_ge(turned_out, 3)
            with dve.Fori(0, 4) as it:
                dve.drain()
                dve.wait_ge(b_ready, it * 32 + 1)
                for j, src in ((0, i1T), (2, gT)):
                    nc.vector.tensor_copy(now[:, j, :], src[:, bass.ds(it * 128, 128)])
                nc.vector.tensor_copy(now[:, 1, :], i2T[:, bass.ds(it * 128, 128)]).then_inc(now_ready, 1)
                dve.drain()
                for s in range(ROUND):
                    low_rows(dve, nc.vector, Step(it, ROUND, 64 + s + 1))
                    for g in groups(s):
                        dve.wait_ge(w_done, it * 32 + (g + 1))
                        for j in range(4):
                            t = 4 * g + j
                            ins = nc.vector.tensor_scalar(one_a[:, g % 2, j, :], iota[:, :], now[:, 0, t:t + 1],
                                                          now[:, 2, t:t + 1], ALU.is_equal, ALU.mult)
                        ins.then_inc(a_ready, 1)
            nc.vector.memset(zeros[:, :], 0.0).then_inc(zero_ready, 1)
            with dve.Fori(0, 4) as it:
                for s in range(4):
                    low_rows(dve, nc.vector, Step(it, 4, 112 + s + 1))

            def product(i2, s, acts, ws):
                dve.wait_ge(act_loaded[s % 4], acts)
                dve.wait_ge(w_loaded[(s // 4) % 2], ws)
                nc.vector.tensor_tensor(p_full[:, s % 2, :].rearrange("p (t s) -> p t s", s=32),
                                        act_in[:, s % 4, :].rearrange("p (t s) -> p t s", s=32),
                                        w_in[:, (s // 4) % 2, :, s % 4, :], ALU.mult).then_inc(pf_ready, 1)

            def low_p(i2, s):
                dve.wait_ge(ph_ready, i2 + 1)
                nc.vector.tensor_tensor(p_lo[:, s % 2, :], p_full[:, s % 2, :], p_hi[:, s % 2, :].bitcast(fp32),
                                        ALU.subtract).then_inc(pl_ready, 1)

            product(0, 0, 16, 16)
            low_p(0, 0)
            with dve.Fori(0, 15) as it:
                for s in range(8):
                    i2 = it * 8 + s
                    product(i2 + 1, s + 1, it * 32 + 16 * (1 + (s + 1) // 4), it * 16 + (16 if s < 7 else 32))
                    low_rows(dve, nc.vector, Step(it, 8, KEYS + s + 1))
                    low_p(i2 + 1, s + 1)
            for s in range(7):
                i2 = KEYS - 8 + s
                product(i2 + 1, s + 1, 15 * 32 + 16 * (1 + (s + 1) // 4), 16 * 16)
                low_rows(dve, nc.vector, alone(NSTEP - 8 + s + 1))
                low_p(i2 + 1, s + 1)
            dve.wait_ge(step_done, NSTEP + 2)
            for i, k in enumerate(LAST_ORDER):
                dve.wait_ge(sq_ready, 36 + i + 1)
                nc.vector.tensor_scalar(ffn[:, k, :], ps[:, k, :], coef[:, 4, k:k + 1], None, ALU.mult).then_inc(acc_out, 1)
            dve.wait_ge(sq_used, 44)
            inverse_variance(D, T)
            for k in range(KD):
                nc.vector.tensor_tensor(ffn[:, k, :], ffn[:, k, :], rstd[:, :], ALU.mult)
                dve.drain()
                nc.vector.tensor_tensor(x1[:, k, :], ffn[:, k, :], x1[:, k, :], ALU.add).then_inc(final_ready, 1)

        @block.tensor
        def _(pe):
            n_sq = [0]

            def sum_squares(count, width):
                for k in range(count):
                    pe.wait_ge(sq_ready, n_sq[0] + 1)
                    ins = nc.tensor.matmul(ps[:, BANK_STAT, 0:width], ones[:, :], sq[:, n_sq[0] % 2, 0:width],
                                           start=k == 0, stop=k == count - 1)
                    ins.then_inc(sq_used, 1)
                    n_sq[0] += 1

            def attention():
                for t in range(tile[0] - 4, tile[0]):
                    wait_tile_out(pe, t)
                pe.wait_ge(rotated, 10)
                pe.wait_ge(mod_ready, 2)

                def scores_of(n):
                    t, qb, s, w = unit(n)
                    if n >= 2:
                        pe.wait_ge(neg_ready, n - 1)
                    rows = slice(64 * s, 64 * s + 64)
                    dst = score_bank(n, w)
                    width = P * (len(w) - 2)
                    q = qT[rows, t, qb * P:(qb + 1) * P]
                    nc.tensor.matmul(dst[:, 0:width], q, kT[rows, t // 4, w[0] * P:w[0] * P + width], start=True, stop=True)
                    nc.tensor.matmul(dst[:, width:width + C], q, kT[rows, t // 4, T:T + C],
                                     start=True, stop=True).then_inc(s_done, 1)

                def times_v(n):
                    t, qb, s, w = unit(n)
                    pe.wait_ge(ta_out, n + 1)
                    pe.wait_ge(tb_out, n + 1)
                    if n % 8 == 0 and t >= 2:
                        pe.wait_ge(y_out, t - 1)
                    g = 2 * (t // 4) + s
                    for i, b in enumerate(w):
                        ins = nc.tensor.matmul(ps[64 * s:64 * s + 64, 6 + t % 2, qb * P:(qb + 1) * P],
                                               v_sb[:, b, g * HD:(g + 1) * HD], probsT[:, n % 2, i * P:(i + 1) * P],
                                               start=i == 0, stop=i == len(w) - 1)
                    ins.then_inc(pv_done, 1)

                for n in range(3):
                    scores_of(n)
                for n in range(len(UNITS)):
                    pe.wait_ge(p_ready, n + 1)
                    if n >= 1:
                        pe.wait_ge(ta_out, n)
                        pe.wait_ge(tb_out, n)
                    for i in range(len(unit(n)[3])):
                        dst = ps[:, 4, i * P:(i + 1) * P] if i < 3 else ps[:, 5, (i - 3) * P:(i - 2) * P]
                        ins = nc.tensor.transpose(dst, probs[:, n % 4, i * P:(i + 1) * P], ident[:, :])
                        if i == 2:
                            ins.then_inc(ta_done, 1)
                    ins.then_inc(tb_done, 1)
                    if n >= 1:
                        times_v(n - 1)
                    if n + 3 < len(UNITS):
                        scores_of(n + 3)
                times_v(len(UNITS) - 1)

            tile = [0]
            pe.wait_ge(filled, 1)
            sum_squares(KD, T)
            pe.wait_ge(cond_ready, 1)

            for n, (kind, m) in enumerate(ORDER):
                slot = n % RING
                pe.wait_ge(chunk_in[slot], 16 * (n // RING + 1))
                w = ring[:, slot, :, :]

                def product(pairs, width):
                    t = tile[0]
                    if t >= 4:
                        wait_tile_out(pe, t - 4)
                    for i, (a, b) in enumerate(pairs):
                        ins = nc.tensor.matmul(ps[:, tile_bank(t), 0:width], a, b, start=i == 0, stop=i == len(pairs) - 1)
                    ins.then_inc(tile_done, 1)
                    tile[0] += 1
                    return ins

                if kind == "ada":
                    if m in (ADA_FIRST, 10):
                        pe.wait_ge(mod_ready, 1 if m == ADA_FIRST else 3)
                    for i in range(4):
                        t = 4 * m + i
                        for k in range(KD):
                            ins = nc.tensor.matmul(ps[:, BANK_ADA, 2 * t:2 * t + 2], w[:, k, i * P:(i + 1) * P], cond[:, k, :],
                                                   start=k == 0, stop=k == KD - 1)
                    ins.then_inc(ada_used, 1)
                    if m == 5:
                        pe.wait_ge(conv_centred, KC)
                        sum_squares(KC, T)
                        wait_chunk_used(pe, n)
                        attention()
                    if m == 9:
                        pe.wait_ge(var_ready, 4)
                        sum_squares(KD, T)
                    continue
                if kind in ("conv_a", "conv_g", "q0", "q1") or kind.startswith("gate"):
                    if kind == "conv_a":
                        pe.wait_ge(hx_ready, KD)
                    for i in range(4):
                        product([(w[:, k, i * P:(i + 1) * P], hT[:, k, :]) for k in range(KD)], T)
                elif kind == "kv":
                    pe.wait_ge(hc_ready, KD)
                    for i in range(2):
                        product([(w[:, k, i * P:(i + 1) * P], hT[:, k, :]) for k in range(KD)], T)
                    for i in range(2):
                        product([(w[:, k, i * P:(i + 1) * P], hcT[:, k, :]) for k in range(KD)], C)
                    for i in range(4):
                        product([(hT[:, k, i * P:(i + 1) * P], w[:, k, 256:512]) for k in range(KD)], 256)
                    for i in range(2):
                        product([(hcT[:, k, i * P:(i + 1) * P], w[:, k, 256:512]) for k in range(KD)], 256)
                elif kind == "o_attn":
                    pe.wait_ge(y_out, KD)
                    for i in range(4):
                        product([(w[:, k, i * P:(i + 1) * P], yT[:, k, :]) for k in range(KD)], T)
                elif kind == "o_conv":
                    pe.wait_ge(conv_out, KC)
                    wo = w.rearrange("p k n -> p (k n)").rearrange("p (k n) -> p k n", k=KC)
                    for i in range(8):
                        product([(wo[:, k, i * P:(i + 1) * P], conv_acc[:, k, :]) for k in range(KC)], T)
                elif kind == "out":
                    for i in range(4):
                        pe.wait_ge(z_ready, KD)
                        product([(w[:, k, i * P:(i + 1) * P], gates[:, k, :]) for k in range(KD)], T)
                        t = 4 * m + i
                        if t >= 1:
                            pe.wait_ge(sq_ready, n_sq[0] + 1)
                            nc.tensor.matmul(ps[:, BANK_STAT, :], ones[:, :], sq[:, n_sq[0] % 2, :], start=t == 1,
                                             stop=False).then_inc(sq_used, 1)
                            n_sq[0] += 1
                elif kind == "wq":
                    for i in range(4):
                        if m == 0 and i == 0:
                            pe.wait_ge(h2_ready, KD)
                            pe.wait_ge(keys_in, 16)
                        product([(w[:, k, i * P:(i + 1) * P], h2[:, k, :]) for k in range(KD)], T)
                        t = 4 * m + i
                        wait_tile_out(pe, tile_no["peer", t])
                        if t >= 2:
                            pe.wait_ge(sc_out, t - 1)
                        for x in range(TT):
                            ins = nc.tensor.matmul(ps[:, 4 + t % 2, x * P:(x + 1) * P], q_peer[:, t % 2, x * P:(x + 1) * P],
                                                   keys[:, t, :], start=True, stop=True)
                        ins.then_inc(sc_done, 1)
                if kind == "gate2":
                    pe.wait_ge(conv_summed, KC)
                    pe.wait_ge(var_ready, 2)
                    for c in range(KC):
                        ins = nc.tensor.matmul(ps[:, BANK_STAT, :], ones[:, :], conv_acc[:, c, :], start=c == 0, stop=c == KC - 1)
                    ins.then_inc(mean_done, 1)
                if kind == "conv_a":
                    pe.wait_ge(var_ready, 1)
                    sum_squares(KD, C)
                if kind == "out" and m == 1:
                    pe.wait_ge(sq_ready, n_sq[0] + 1)
                    nc.tensor.matmul(ps[:, BANK_STAT, :], ones[:, :], sq[:, n_sq[0] % 2, :], start=False,
                                     stop=True).then_inc(sq_used, 1)
                    n_sq[0] += 1

            pe.wait_ge(var_ready, 5)
            pe.wait_ge(h2_parts, KD)
            pe.wait_ge(tile_out_act, sum(e == "act" for _, _, e in tiles))
            pe.wait_ge(sc_out, 2 * PEER_HEADS)
            pe.sem_inc(step_done, 2)

            def act_step(step):
                wait_low(pe, step)
                pe.wait_ge(gelu_done, step.n + 1)
                x = step.c % 2
                for k in range(KD):
                    hi, lo = st_hi[:, x, k * P:(k + 1) * P], st_lo[:, x, k * P:(k + 1) * P]
                    for i, (a, b) in enumerate(((hi, h2_hi), (hi, h2_lo), (lo, h2_hi))):
                        ins = nc.tensor.matmul(ps[:, x, :], a, b[:, k, :], start=k == 0 and i == 0,
                                               stop=k == KD - 1 and i == 2)
                ins.then_inc(step_done, 1)

            with pe.Fori(0, 16) as it:
                for s in range(4):
                    act_step(Step(it, 4, s))
            pe.wait_ge(gate_ready, 1)
            for j, src in enumerate((i1_all, i2_all, best)):
                for x in range(TT):
                    ins = nc.tensor.transpose(ps[:, 4 + j, x * P:(x + 1) * P],
                                              src[:, 8 * x:8 * x + 8, :].rearrange("p a b -> p (a b)"), ident[:, :])
                ins.then_inc(turned, 1)
            pe.sem_inc(w_done, 2)
            with pe.Fori(0, 4) as it:
                for s in range(ROUND):
                    act_step(Step(it, ROUND, 64 + s))
                    for g in groups(s):
                        pe.wait_ge(a_ready, it * 32 + (g + 1))
                        pe.wait_ge(b_ready, it * 32 + (g + 2))
                        pe.wait_ge(w_out_s, it * 32 + (g + 1))
                        for j in range(4):
                            ins = nc.tensor.matmul(ps[:, 2 + g % 2, j * P:(j + 1) * P], one_a[:, g % 2, j, :],
                                                   one_b[:, g % 2, j, :], start=True, stop=True)
                        ins.then_inc(w_done, 1)
            with pe.Fori(0, 4) as it:
                for s in range(4):
                    act_step(Step(it, 4, 112 + s))
            pe.wait_ge(w_out_s, T // 4 + 2)
            pe.wait_ge(zero_ready, 1)
            pe.wait_ge(mod_ready, 4)
            for d in (2, 3, 4, 5, 6, 7, 0, 1):
                if d == 0:
                    pe.wait_ge(gelu_done, KEYS + 2)
                nc.tensor.matmul(ps[:, d, :], zeros[:, 0:P], zeros[:, :], start=True, stop=False)

            def out_step(step, last=False):
                wait_low(pe, step)
                pe.wait_ge(pl_ready, step.n + (1 - KEYS))
                s = step.c
                for d in range(KD):
                    hi, lo = st_hi[:, s % 2, d * P:(d + 1) * P], st_lo[:, s % 2, d * P:(d + 1) * P]
                    for i, (a, b) in enumerate(((hi, p_hi), (hi, p_lo), (lo, p_hi))):
                        ins = nc.tensor.matmul(ps[:, d, :], a, b[:, s % 2, :], start=False, stop=last and i == 2)
                ins.then_inc(step_done, 1)

            with pe.Fori(0, 15) as it:
                for s in range(8):
                    out_step(Step(it, 8, KEYS + s))
            for s in range(8):
                out_step(alone(NSTEP - 8 + s), s == 7)
            pe.wait_ge(acc_out, 1)
            sum_squares(KD, T)


def fixed_tables():
    t = np.arange(T, dtype=np.int32)
    place = [(t // GRID_W).astype(np.float32), (t % GRID_W).astype(np.float32)]
    half = HD // 4
    freqs = (np.float32(10000.0) ** (-np.arange(0, HD // 2, 2, dtype=np.float32) / np.float32(HD // 2))).astype(np.float32)
    cos, sin = np.zeros((P, T), np.float32), np.zeros((P, T), np.float32)
    for p in range(P):
        d = p % HD
        angle = place[d // (HD // 2)] * freqs[d % half]
        cos[p] = np.cos(angle)
        sin[p] = np.sin(angle) * (-1 if d % (HD // 2) < half else 1)
    q, k = np.arange(P)[:, None], np.arange(P)[None, :]
    before = np.where(k >= q, 0.0, NEG).astype(np.float32)
    after = np.where(k <= q, 0.0, NEG).astype(np.float32)
    free = np.zeros((P, P), np.float32)
    mask = np.concatenate([before, free, after, free, free, before, free, free, free], axis=1)
    return np.concatenate([np.eye(P, dtype=np.float32), np.tile(np.arange(P, dtype=np.float32), (P, 1)), cos, sin, mask], axis=1)


def columns(v):
    return np.asarray(v).reshape(-1, P).T


def lay_out(inputs):
    a = {k: np.asarray(v) for k, v in inputs.items()}

    def chunk(m):
        return m.reshape(-1, P, m.shape[1]).transpose(1, 0, 2).reshape(P, KD * CHUNK)

    w_in = a["w_in"][0]
    kv0 = HEADS * HD
    conv0 = kv0 + 2 * KV_HEADS * HD
    gate0 = conv0 + 2 * CONV
    q_cols = np.concatenate([np.arange(h * HD, (h + 1) * HD) for h in HEAD_ORDER])
    parts = {
        "ada": a["w_ada"][0], "conv_a": w_in[:, conv0:conv0 + CONV], "conv_g": w_in[:, conv0 + CONV:gate0],
        "kv": w_in[:, kv0:conv0], "q0": w_in[:, q_cols[:512]], "q1": w_in[:, q_cols[512:]],
        "o_attn": a["w_o_attn"][0][q_cols], "o_conv": a["w_o_conv"][0], "out": a["w_out"][0], "wq": a["peer_wq"][0],
    }
    for i in range(4):
        parts[f"gate{i}"] = w_in[:, gate0 + i * CHUNK:gate0 + (i + 1) * CHUNK]
    wchunks = np.stack([chunk(parts[k] if k == "o_conv" else parts[k][:, n * CHUNK:(n + 1) * CHUNK]) for k, n in ORDER])
    dw = a["conv_dw"][0].T.reshape(KC, P, TAPS).transpose(1, 0, 2).reshape(P, KC * TAPS)
    vec = np.concatenate([columns(a["b_ada"][0]), columns(a["g_pre_mix"][0]), columns(a["g_post_mix"][0]),
                          columns(a["g_pre_ffn"][0]), columns(a["g_post_ffn"][0]), dw, columns(a["conv_dw_b"][0]),
                          columns(a["conv_ln_g"][0]), columns(a["conv_ln_b"][0]),
                          np.tile(a["attn_sink"][0][HEAD_ORDER][None, :], (P, 1))], axis=1)
    rows = np.empty((NSTEP, P, ROW), a["peer_u"].dtype)
    u = a["peer_u"][0].reshape(KEYS, KEYS, KD, P)
    rows[:KEYS] = u.transpose(1, 3, 2, 0).reshape(KEYS, P, ROW)
    rows[KEYS:] = a["peer_v"][0].reshape(KEYS, KEYS, D).transpose(1, 0, 2)
    return {
        "xT": a["x"][0].T.reshape(KD, P, T).transpose(1, 0, 2),
        "ctxT": a["ctx"][0].T.reshape(KD, P, C).transpose(1, 0, 2),
        "cc": np.stack([columns(a["c"][0]), columns(a["c_ctx"])], axis=2),
        "wchunks": wchunks.reshape(len(ORDER), P, KD, CHUNK),
        "vec": vec,
        "keysT": a["peer_keys"][0].reshape(2 * PEER_HEADS, KEYS, P).transpose(2, 0, 1),
        "expert_rows": rows,
        "consts": fixed_tables(),
    }


def kernel(**inputs):
    import concourse.bacc as bacc
    from concourse.bass_utils import run_bass_kernel_spmd

    nc = bacc.Bacc("TRN2", target_bir_lowering=False, num_devices=1)
    arrays, args = {}, {}
    for name, a in lay_out(inputs).items():
        arrays[name] = np.ascontiguousarray(a)
        args[name] = nc.dram_tensor(name, arrays[name].shape, mybir.dt.from_np(arrays[name].dtype), kind="ExternalInput").ap()
    out = nc.dram_tensor("outT", (P, KD, T), mybir.dt.float32, kind="ExternalOutput").ap()
    layer_kernel(nc, out=out, **args)
    r = run_bass_kernel_spmd(nc, [arrays], core_ids=[0])
    return np.asarray(r.results[0]["outT"]).transpose(2, 1, 0).reshape(1, T, D)
```

```python
from contextlib import ExitStack

import numpy as np

import concourse.bass as bass
from concourse import mybir

D = 1024
T = 512
C = 256
P = 128
KD = D // P
TT = T // P
GRID_W = 64
HEADS, KV_HEADS, HD = 16, 4, 64
GROUP = HEADS // KV_HEADS
CONV = 512
KC = CONV // P
TAPS = 31
PEER_HEADS, KEYS, TOPK = 8, 128, 16
EPS = 1e-6
NEG = -1e30
FLOOR = -3.0e38

CHUNK = 256
CHUNK_ROW = KD * CHUNK
RING, HIGHS = 4, 3
N_ADA = 6 * D // CHUNK
ADA_FIRST = 8
ORDER = [("ada", n) for n in range(ADA_FIRST)]
ORDER += [(kind, n) for kind, count in (("conv_a", 2), ("conv_g", 2)) for n in range(count)]
ORDER += [("q", 0), ("k", 0), ("v", 0), ("q", 1), ("q", 2), ("q", 3)] + [("gate", n) for n in range(8)]
ORDER += [("ada", n) for n in range(ADA_FIRST, N_ADA - 2)] + [("o_attn", 0), ("ada", N_ADA - 2), ("ada", N_ADA - 1)]
ORDER += [("o_attn", 1), ("o_attn", 2), ("o_attn", 3), ("o_conv", 0), ("o_conv", 1)]
ORDER += [("out", n) for n in range(4)] + [("wq", n) for n in range(8)]
GPSIMD_TILES = (1, 4, 7)
SPLIT = [entry for entry in ORDER if entry[0] != "ada"]

V_BADA, V_PREMIX, V_POSTMIX, V_PREFFN, V_POSTFFN = 0, 48, 56, 64, 72
V_DW, V_DWB, V_LNG, V_LNB, V_SINK, V_N = 80, 204, 208, 212, 216, 232
SH1, SC1, GT1, SH2, SC2, GT2 = (8 * n for n in range(6))
SWAP = [(i + 16) % 32 for i in range(32)]
HEAD_ORDER = [GROUP * (2 * a + s) + j for a in range(2) for j in range(GROUP) for s in range(2)]

NSTEP = 2 * KEYS
DEPTH = 4
ROW = KD * P


class Step:

    def __init__(self, it, K, c):
        self.it, self.K, self.c = it, K, c
        self.n = it * K + c if K else c
        self.pairs = it * (K // 2) + (c // 2 + 1) if K else c // 2 + 1
        self.fours = it * (K // 4) + (c // 4 + 1) if K else c // 4 + 1

    def plus(self, k):
        return Step(self.it, self.K, self.c + k)


def alone(n):
    return Step(0, 0, n)


def windows(qb):
    return list(range(max(0, qb - 1), min(TT - 1, qb + 1) + 1)) + [TT, TT + 1]


def layer_kernel(nc, xT, ctxT, cc, wchunks, vec, keysT, expert_rows, consts, out):
    fp32 = mybir.dt.float32
    f32r = mybir.dt.float32r
    u32 = mybir.dt.uint32
    ALU = mybir.AluOpType
    ACT = mybir.ActivationFunctionType
    AX = mybir.AxisListType.X

    act_dram = nc.dram_tensor("act_dram", [KEYS, P, T], fp32).ap()
    w_dram = nc.dram_tensor("w_dram", [T // 32, P, KEYS, 32], fp32).ap()

    ctx = ExitStack()
    with ctx:
        BASE = 16512
        ctx.enter_context(nc.sbuf_tensor("slab", [P, (229344 - BASE) // 4], fp32))
        top = [BASE]

        def at(name, shape, offset, dt=fp32):
            return nc.alloc_sbuf_tensor_at(name, [P, *shape], dt, offset=offset)

        def take(n):
            top[0] += n
            return top[0] - n

        KB = 1024
        x1 = at("x1", [KD, T], take(16 * KB))
        vecs = at("vecs", [V_N], take(KB))
        mod = at("mod", [48, 2], take(512))
        ident = at("ident", [P], take(512))
        iota = at("iota", [P], take(512))
        mean_of = at("mean_of", [P], take(512))
        one_col = at("one_col", [4], take(32))
        eps_col = at("eps_col", [4], take(32))
        neg_sink = at("neg_sink", [HEADS], take(64))
        cond = at("cond", [KD, 2], take(64))
        coef = at("coef", [6, KD], take(256))
        rstd = at("rstd", [T], take(2 * KB))
        sq = at("sq", [3, T], take(6 * KB))
        small = at("small", [256], take(KB))
        ada_acc = at("ada_acc", [2, CHUNK], take(2 * KB))
        r_ring, r_tail = take((RING + HIGHS) * 8 * KB), take(40 * KB)
        r_h, r_ctx, r_q, r_gate = take(16 * KB), take(16 * KB), take(16 * KB), take(32 * KB)
        assert top[0] <= 229368, top[0]
        ring = at("ring", [RING, CHUNK_ROW], r_ring)
        w_lo = at("w_lo", [RING, CHUNK_ROW], r_ring, f32r)
        w_hi = at("w_hi", [HIGHS, CHUNK_ROW], r_ring + RING * 8 * KB, f32r)
        hT = at("hT", [KD, T], r_h)
        hT_lo = at("hT_lo", [KD, T], r_h, f32r)
        hT_hi = at("hT_hi", [KD, T], BASE, f32r)
        y_lo = at("y_lo", [KD, T], r_h, f32r)
        y_hi = at("y_hi", [KD, T], BASE, f32r)
        mixed = at("mixed", [KD, T], r_h)
        ctx_sb = at("ctx_sb", [KD, C], r_ctx)
        hc_hi = at("hc_hi", [KD, C], r_ctx, f32r)
        hcT = at("hcT", [KD, C], r_ctx + 8 * KB)
        hc_lo = at("hc_lo", [KD, C], r_ctx + 8 * KB, f32r)
        probs = at("probs", [4, 640], r_ctx)
        probsT = at("probsT", [2, 640], r_ctx + 10240)
        sq_all = at("sq_all", [KD, T], r_ctx)
        qT = at("qT", [KD, T], r_q)
        gates = at("gates", [2 * KD, T], r_gate)
        ada_row = at("ada_row", [ADA_FIRST * CHUNK], r_gate)
        glu = at("glu", [KC, T], r_gate + 24 * KB)
        z_lo = at("z_lo", [KD, T], r_gate, f32r)
        z_hi = at("z_hi", [KD, T], r_gate + 16 * KB, f32r)
        kT = at("kT", [2, T + C], r_tail)
        v_sb = at("v_sb", [6, 256], r_tail + 6144)
        u_w = T + TAPS - 1
        conv_in = at("conv_in", [KC, u_w], r_tail + 12288)
        c_hi = at("c_hi", [KC, T], r_tail + 12288, f32r)
        o = r_tail + 12288 + 4 * KC * u_w
        conv_acc = at("conv_acc", [KC, T], o)
        c_lo = at("c_lo", [KC, T], o, f32r)
        o += 8 * KB
        cos_t = at("cos_t", [T], o)
        sin_t = at("sin_t", [T], o + 2048)
        turn = at("turn", [T], o + 4096)
        mask = at("mask", [640 + 512], o + 6144)
        assert o + 6144 + 4608 <= r_tail + 40 * KB
        h2 = at("h2", [KD, T], r_q)
        h2_hi = at("h2_hi", [KD, T], r_gate, f32r)
        h2_lo = at("h2_lo", [KD, T], r_gate + 16 * KB, f32r)
        scores = at("scores", [TT * PEER_HEADS * 2, KEYS], r_h)
        e_tail = r_ring + 48 * KB
        keys = at("keys", [2 * PEER_HEADS, KEYS], r_tail)
        q_peer = at("q_peer", [2, T], r_tail + 8 * KB)
        raw = at("raw", [4, ROW], r_tail + 12 * KB)
        st_hi = at("st_hi", [2, ROW], r_ring, f32r)
        st_lo = at("st_lo", [2, ROW], r_ring + 8 * KB, f32r)
        w_tile = at("w_tile", [2, KEYS, 32], r_ring + 16 * KB)
        best = at("best", [32, TOPK], e_tail)
        i1_all = at("i1_all", [32, TOPK], e_tail + 2 * KB)
        i2_all = at("i2_all", [32, TOPK], e_tail + 4 * KB)
        sc_now = at("sc_now", [4, KEYS], e_tail + 6 * KB)
        assert e_tail + 8 * KB == r_tail
        o = e_tail + 28 * KB
        cand = at("cand", [2, TOPK * TOPK], o + 8 * KB)
        hit = at("hit", [2, TOPK, TOPK], o + 10 * KB)
        p_lo = at("p_lo", [2, T], o + 12 * KB, f32r)
        tops = at("tops", [4, TOPK], o + 16 * KB)
        top_ix = at("top_ix", [4, TOPK], o + 16 * KB + 256, u32)
        top_ixf = at("top_ixf", [4, TOPK], o + 16 * KB + 512)
        best_now = at("best_now", [2, TOPK], o + 16 * KB + 768)
        pos = at("pos", [2, TOPK], o + 16 * KB + 896, u32)
        pos_ab = at("pos_ab", [2, 2, TOPK], o + 16 * KB + 1024, u32)
        pos_f = at("pos_f", [2, 2, TOPK], o + 16 * KB + 1280)
        e_sum = at("e_sum", [2, 32], o + 16 * KB + 1536)
        act_out = at("act_out", [2, T], r_q)
        i1T = at("i1T", [T], r_q + 4 * KB)
        i2T = at("i2T", [T], r_q + 6 * KB)
        gT = at("gT", [T], r_q + 8 * KB)
        now = at("now", [3, 128], r_q + 10 * KB)
        one_a = at("one_a", [DEPTH, 4, P], r_h)
        one_b = at("one_b", [DEPTH, 4, P], r_h + DEPTH * 2 * KB)
        w_in = at("w_in", [2, 16, 4, 32], r_h + 12 * KB)
        p_full = at("p_full", [2, T], r_h + 28 * KB)
        act_in = at("act_in", [4, T], r_q + 4 * KB)
        p_hi = at("p_hi", [2, T], r_q + 12 * KB, f32r)
        zeros = at("zeros", [T], e_tail + 6 * KB, mybir.dt.bfloat16)
        ffn = at("ffn", [KD, T], r_ring + 16 * KB)
        ps = ctx.enter_context(nc.psum_tensor("ps", [P, 8, 512], fp32))
        BANK_STAT, BANK_ADA, BANK_LATER, ADA_COL = 4, 7, 5, 256
        LAST_ORDER = [BANK_STAT] + [k for k in range(KD) if k != BANK_STAT]

        def sem(name):
            return ctx.enter_context(nc.semaphore(name))

        x_in, ctx_in, cc_in, vec_in, const_in, keys_in = map(sem, ("x_in", "ctx_in", "cc_in", "vec_in", "const_in", "keys_in"))
        chunk_in = [sem(f"chunk_in{i}") for i in range(RING)]
        ada_used, mod_ready = sem("ada_used"), sem("mod_ready")
        acc_ready, row_done, row_out = sem("acc_ready"), sem("row_done"), sem("row_out")
        w_high, w_parts = sem("w_high"), sem("w_parts")
        cond_ready, filled = sem("cond_ready"), sem("filled")
        sq_ready, sq_used, total_done, mean_done, std_ready = map(
            sem, ("sq_ready", "sq_used", "total_done", "mean_done", "std_ready"))
        hx_ready, hx_high, hx_parts = sem("hx_ready"), sem("hx_high"), sem("hx_parts")
        hc_ready, hc_high, hc_parts = sem("hc_ready"), sem("hc_high"), sem("hc_parts")
        glu_used, conv_high, conv_parts = sem("glu_used"), sem("conv_high"), sem("conv_parts")
        y_high, z_high, z_parts, mix_gain = sem("y_high"), sem("z_high"), sem("z_parts"), sem("mix_gain")
        tile_done, tile_out_act, tile_out_dve = sem("tile_done"), sem("tile_out_act"), sem("tile_out_dve")
        conv_summed, conv_centred, conv_normed, conv_out = map(sem, ("conv_summed", "conv_centred", "conv_normed", "conv_out"))
        rotated = sem("rotated")
        scores_done, neg_ready, exp_done, probs_ready = map(sem, ("scores_done", "neg_ready", "exp_done", "probs_ready"))
        probs_turned, turned_copied, values_done, y_out = map(sem, ("probs_turned", "turned_copied", "values_done", "y_out"))
        z_ready, x1_dve, x1_pool, h2_ready, h2_split, h2_parts = map(
            sem, ("z_ready", "x1_dve", "x1_pool", "h2_ready", "h2_split", "h2_parts"))
        routing_done, routing_out = sem("routing_done"), sem("routing_out")
        row_in = [sem(f"row_in{i}") for i in range(4)]
        hi_ready, step_done = sem("hi_ready"), sem("step_done")
        lo_ready = [sem(f"lo_ready{i}") for i in range(2)]
        gelu_done, act_stored = sem("gelu_done"), [sem(f"act_stored{i}") for i in range(2)]
        picked, gate_exp, gate_ready, turned, turned_out = map(sem, ("picked", "gate_exp", "gate_ready", "turned", "turned_out"))
        now_ready, b_ready, a_ready, w_done, w_tile_out = map(sem, ("now_ready", "b_ready", "a_ready", "w_done", "w_tile_out"))
        w_stored = [sem(f"w_stored{i}") for i in range(2)]
        w_loaded = [sem(f"w_loaded{i}") for i in range(2)]
        act_loaded = [sem(f"act_loaded{i}") for i in range(4)]
        pf_ready, ph_ready, pl_ready, acc_out, final_dve, final_pool, out_done, rstd_ready = map(
            sem, ("pf_ready", "ph_ready", "pl_ready", "acc_out", "final_dve", "final_pool", "out_done", "rstd_ready"))
        dve_chain, zero_ready, bank_done, four_added = map(sem, ("dve_chain", "zero_ready", "bank_done", "four_added"))
        settled = sem("settled")

        def tiles_of(kind, n):
            if kind == "k":
                return [("k", 0), ("k", 1), ("kc", 0), ("kc", 1)]
            if kind == "v":
                return [("v", i) for i in range(TT)] + [("vc", i) for i in range(2)]
            if kind == "o_conv":
                return [("yc", 4 * n + i) for i in range(4)]
            name = {"o_attn": "ya", "out": "mix", "wq": "peer"}.get(kind, kind)
            return [(name, 2 * n + i) for i in range(2)]

        tiles, chunk_tiles = [], []
        for kind, n in ORDER:
            if kind != "ada":
                tiles += [(name, i, "dve" if name in ("ya", "yc") else "act") for name, i in tiles_of(kind, n)]
            chunk_tiles.append(len(tiles))
        tile_no = {(k, i): n for n, (k, i, _) in enumerate(tiles)}
        tile_count = []
        for n, (_, _, e) in enumerate(tiles):
            tile_count.append(sum(x == e for _, _, x in tiles[: n + 1]))

        def tile_bank(n):
            return n % 4

        def wait_tile_out(eng, n):
            eng.wait_ge(tile_out_act if tiles[n][2] == "act" else tile_out_dve, tile_count[n])

        def residual(eng, ops, branch, done, in_pool):
            for k in range(KD):
                if (k in GPSIMD_TILES) == in_pool:
                    ops.tensor_tensor(branch[:, k, :], branch[:, k, :], rstd[:, :], ALU.mult)
                    eng.drain()
                    ops.tensor_tensor(x1[:, k, :], branch[:, k, :], x1[:, k, :], ALU.add).then_inc(done, 1)

        def wait_residual(eng, k, by_dve, by_pool):
            before = sum(x < k for x in GPSIMD_TILES)
            if k in GPSIMD_TILES:
                eng.wait_ge(by_pool, before + 1)
            else:
                eng.wait_ge(by_dve, k - before + 1)

        def settle(eng):
            eng.sem_inc(settled, 1)

        def wait_chunk_used(eng, n):
            kind, m = ORDER[n]
            if kind != "ada":
                eng.wait_ge(tile_done, chunk_tiles[n])
            elif m < ADA_FIRST:
                eng.wait_ge(row_done, m + 1)
            else:
                eng.wait_ge(acc_ready, m - ADA_FIRST + 1)

        def wait_chunk_in(eng, n):
            eng.wait_ge(chunk_in[n % RING], 16 * (n // RING + 1))

        def wait_low(eng, step):
            eng.wait_ge(lo_ready[step.c % 2], step.pairs)

        def low_rows(eng, ops, step):
            eng.wait_ge(hi_ready, step.n + 1)
            ops.tensor_tensor(st_lo[:, step.c % 2, :], raw[:, step.c % 4, :], st_hi[:, step.c % 2, :].bitcast(fp32),
                              ALU.subtract).then_inc(lo_ready[step.c % 2], 1)

        ROUND = 12

        def groups(s):
            return range(s * 32 // ROUND, (s + 1) * 32 // ROUND)

        UNITS = [(t, qb, s) for t in range(KD) for qb in range(TT) for s in range(2)]

        def unit(n):
            t, qb, s = UNITS[n]
            return t, qb, s, windows(qb)

        def score_bank(n, w):
            col = 512 - P * (len(w) - 2)
            return ps[:, 2 * (n % 2):2 * (n % 2) + 2, :].rearrange("p b n -> p (b n)")[:, col:col + P * len(w)]

        turned_bank = ps[:, 4:6, :].rearrange("p b n -> p (b n)")

        def cell(kind, n):
            return small[:, 4 * kind + n % 4:4 * kind + n % 4 + 1]

        def column(col, k):
            return vecs[:, col + k:col + k + 1]

        block = ctx.enter_context(nc.Block())

        @block.sync
        def _(sp):
            sp.dma_start(cond[:, :, :], cc).then_inc(cc_in, 16)
            sp.dma_start(vecs[:, :], vec).then_inc(vec_in, 16)
            sp.dma_start(ident[:, :], consts[:, 0:128]).then_inc(const_in, 16)
            for n in range(len(ORDER)):
                if n >= RING:
                    wait_chunk_used(sp, n - RING)
                sp.dma_start(ring[:, n % RING, :], wchunks[n]).then_inc(chunk_in[n % RING], 16)
                if n == 2:
                    sp.dma_start(x1[:, :, :], xT).then_inc(x_in, 16)
                if ORDER[n] == ("conv_a", 1):
                    sp.dma_start(ctx_sb[:, :, :], ctxT).then_inc(ctx_in, 16)
                    for dst, a, b in ((iota, 128, 256), (cos_t, 256, 768), (sin_t, 768, 1280), (mask, 1280, 2432)):
                        sp.dma_start(dst[:, :], consts[:, a:b]).then_inc(const_in, 16)
                if ORDER[n] == ("out", 0):
                    wait_tile_out(sp, tile_no["ya", KD - 1])
                    sp.dma_start(x1[:, :, :], xT).then_inc(x_in, 16)
                if ORDER[n] == ("wq", 3):
                    wait_tile_out(sp, tile_no["yc", 7])
                    sp.dma_start(keys[:, :, :], keysT).then_inc(keys_in, 16)
                    for s in range(4):
                        sp.dma_start(raw[:, s, :], expert_rows[s]).then_inc(row_in[s], 16)

            def load_row(step):
                wait_low(sp, step)
                sp.dma_start(raw[:, step.c % 4, :],
                             expert_rows[bass.ds(step.n + 4, 1)].rearrange("a p n -> (a p) n")).then_inc(row_in[step.c % 4], 16)

            def store_act(step):
                sp.wait_ge(gelu_done, step.n + 3)
                sp.dma_start(act_dram[bass.ds(step.n, 1)].rearrange("a p n -> (a p) n"),
                             act_out[:, step.c % 2, :]).then_inc(act_stored[step.c % 2], 16)

            with sp.Fori(0, 16) as it:
                for s in range(4):
                    load_row(Step(it, 4, s))
                    store_act(Step(it, 4, s))
            with sp.Fori(0, 4) as it:
                for s in range(ROUND):
                    load_row(Step(it, ROUND, 64 + s))
                    store_act(Step(it, ROUND, 64 + s))
                    if s % 3 == 2:
                        h = s // 3
                        sp.wait_ge(w_tile_out, it * 32 + (8 * (h + 1) + DEPTH))
                        sp.dma_start(w_dram[bass.ds(it * 4 + h, 1)].rearrange("a p i t -> (a p) (i t)"),
                                     w_tile[:, h % 2, :, :].rearrange("p i t -> p (i t)")).then_inc(w_stored[h % 2], 16)
            for s in range(2):
                sp.wait_ge(w_stored[s], 16 * (8 + 1))
            sp.wait_ge(w_done, T // 4 + DEPTH)

            def load_w(g, h):
                sp.dma_start(w_in[:, h, :, :, :].rearrange("p t i s -> p t (i s)"),
                             w_dram[:, :, bass.ds(g * 4, 4), :].rearrange("t p i s -> p t (i s)")).then_inc(w_loaded[h], 16)

            def load_act(i2, s):
                sp.dma_start(act_in[:, s, :], act_dram[bass.ds(i2, 1)].rearrange("a p n -> (a p) n")).then_inc(act_loaded[s], 16)

            for s in range(2):
                sp.wait_ge(act_stored[s], 16 * (56 + 1))
            for n in range(112, 128):
                load_row(alone(n))
                store_act(alone(n))
                if n in (114, 117):
                    load_w((n - 114) // 3, (n - 114) // 3)
                if 119 <= n < 123:
                    load_act(n - 119, n - 119)
            for s in range(2):
                sp.wait_ge(act_stored[s], 16 * (KEYS // 2 + 1))

            with sp.Fori(0, 15) as it:
                for s in range(8):
                    i2 = it * 8 + s
                    load_row(Step(it, 8, KEYS + s))
                    sp.wait_ge(pf_ready, i2 + 1)
                    load_act(i2 + 4, s % 4)
                    if s % 4 == 3:
                        load_w(it * 2 + (2 + s // 4), s // 4)
            for s in range(4):
                load_row(alone(NSTEP - 8 + s))
                sp.wait_ge(pf_ready, KEYS - 8 + s + 1)
                load_act(KEYS - 4 + s, s)
            for k in range(KD):
                wait_residual(sp, k, final_dve, final_pool)
                sp.dma_start(out[:, k, :], x1[:, k, :]).then_inc(out_done, 16)
            sp.wait_ge(out_done, 16 * KD)

        @block.gpsimd
        def _(pool):
            nc.gpsimd.memset(mean_of[:, :], 1.0 / D).then_inc(filled, 1)
            nc.gpsimd.memset(one_col[:, :], 1.0).then_inc(filled, 1)
            nc.gpsimd.memset(eps_col[:, :], EPS).then_inc(filled, 1)
            nc.gpsimd.memset(conv_in[:, :, 0:TAPS // 2], 0.0).then_inc(filled, 1)
            nc.gpsimd.memset(conv_in[:, :, T + TAPS // 2:u_w], 0.0).then_inc(filled, 1)
            for n, (kind, i) in enumerate(ORDER[ADA_FIRST:], ADA_FIRST):
                slot = n % RING
                if kind == "ada":
                    wait_chunk_in(pool, n)
                    w = ring[:, slot, :].rearrange("p (k n) -> p k n", k=KD)
                    nc.gpsimd.tensor_tensor(w, w, cond[:, :, 0:1].to_broadcast([P, KD, CHUNK]), ALU.mult)
                    pool.drain()
                    for half in (4, 2):
                        nc.gpsimd.tensor_tensor(w[:, 0:half, :], w[:, 0:half, :], w[:, half:2 * half, :], ALU.add)
                        pool.drain()
                    if i >= ADA_FIRST + 2:
                        pool.wait_ge(ada_used, i - ADA_FIRST)
                    nc.gpsimd.tensor_tensor(ada_acc[:, i % 2, :], w[:, 0, :], w[:, 1, :], ALU.add).then_inc(acc_ready, 1)
                    continue
                m = SPLIT.index((kind, i))
                pool.wait_ge(w_high, m + 1)
                nc.gpsimd.tensor_tensor(w_lo[:, slot, :], ring[:, slot, :], w_hi[:, m % HIGHS, :].bitcast(fp32),
                                        ALU.subtract).then_inc(w_parts, 1)
                if (kind, i) == ("v", 0):
                    pool.wait_ge(hc_high, 1)
                    nc.gpsimd.tensor_tensor(hc_lo[:, :, :], hcT[:, :, :], hc_hi[:, :, :].bitcast(fp32), ALU.subtract).then_inc(hc_parts, 1)
                if (kind, i) == ("o_attn", 3):
                    pool.wait_ge(conv_high, 1)
                    nc.gpsimd.tensor_tensor(c_lo[:, :, :], conv_acc[:, :, :], c_hi[:, :, :].bitcast(fp32), ALU.subtract).then_inc(conv_parts, 1)
                if (kind, i) == ("wq", 1):
                    pool.wait_ge(rstd_ready, 4)
                    residual(pool, nc.gpsimd, mixed, x1_pool, True)
                if (kind, i) == ("wq", 2):
                    for k in range(KD):
                        pool.wait_ge(h2_split, k + 1)
                        nc.gpsimd.tensor_tensor(h2_lo[:, k, :], h2[:, k, :], h2_hi[:, k, :].bitcast(fp32),
                                                ALU.subtract).then_inc(h2_parts, 1)
            low_rows(pool, nc.gpsimd, alone(0))
            with pool.Fori(0, 16) as it:
                for s in range(4):
                    low_rows(pool, nc.gpsimd, Step(it, 4, s + 1))
            pool.sem_inc(b_ready, 1)
            with pool.Fori(0, 4) as it:
                pool.wait_ge(now_ready, it + 1)
                for g in range(32):
                    pool.wait_ge(w_done, it * 32 + (g + 1))
                    settle(pool)
                    for j in range(4):
                        ins = nc.gpsimd.tensor_scalar(one_b[:, g % DEPTH, j, :], iota[:, :], now[:, 1, 4 * g + j:4 * g + j + 1],
                                                      None, ALU.is_equal)
                    ins.then_inc(b_ready, 1)
            pool.wait_ge(acc_out, KD)
            pool.wait_ge(rstd_ready, 6)
            residual(pool, nc.gpsimd, ffn, final_pool, True)

        @block.scalar
        def _(act):
            n_sq = [0]

            def square(src, width):
                n = n_sq[0]
                if n >= 3:
                    act.wait_ge(sq_used, n - 2)
                nc.scalar.activation(sq[:, n % 3, 0:width], src, ACT.Square).then_inc(sq_ready, 1)
                n_sq[0] += 1

            def square_all(src, k):
                nc.scalar.activation(sq_all[:, k, :], src, ACT.Square).then_inc(sq_ready, 1)
                n_sq[0] += 1

            def root(width, factor=1.0, total=None):
                nc.scalar.preload_act_table(ACT.Sqrt)
                if total is not None:
                    act.wait_ge(total_done, total)
                else:
                    act.wait_ge(sq_used, n_sq[0])
                nc.scalar.activation(rstd[:, 0:width], ps[:, BANK_STAT, 0:width], ACT.Sqrt, bias=eps_col[:, 0:1],
                                     scale=factor).then_inc(std_ready, 1)

            def weights_high(m):
                n = ORDER.index(SPLIT[m])
                wait_chunk_in(act, n)
                if m >= HIGHS:
                    wait_chunk_used(act, ORDER.index(SPLIT[m - HIGHS]))
                nc.scalar.copy(w_hi[:, m % HIGHS, :], ring[:, n % RING, :]).then_inc(w_high, 1)

            def tile_out(name, i):
                n = tile_no[name, i]
                act.wait_ge(tile_done, n + 1)
                src, fn, sc = ps[:, tile_bank(n), :], ACT.Copy, 1.0
                if name == "conv_a":
                    act.wait_ge(filled, 5)
                    dst = conv_in[:, i, TAPS // 2:TAPS // 2 + T]
                elif name == "conv_g":
                    dst, fn = glu[:, i, :], ACT.Sigmoid
                elif name == "k":
                    dst = kT[:, i, 0:T]
                elif name == "kc":
                    dst, src = kT[:, i, T:T + C], src[:, 0:C]
                elif name == "v":
                    dst, src = v_sb[:, i, :], src[:, 0:256]
                elif name == "vc":
                    dst, src = v_sb[:, TT + i, :], src[:, 0:256]
                elif name == "q":
                    dst, sc = qT[:, i, :], -float(HD) ** -0.5
                elif name == "gate":
                    if i == 12:
                        act.wait_ge(glu_used, KC)
                    dst, fn = gates[:, i, :], ACT.Sigmoid
                elif name == "mix":
                    square(src, T)
                    dst, sc = mixed[:, i, :], coef[:, 2, i:i + 1]
                nc.scalar.activation(dst, src, fn, scale=sc).then_inc(tile_out_act, 1)

            act.wait_ge(cc_in, 16)
            nc.scalar.activation(cond[:, :, :], cond[:, :, :], ACT.Silu).then_inc(cond_ready, 1)
            act.wait_ge(x_in, 16)
            for k in range(KD):
                square(x1[:, k, :], T)
            act.wait_ge(filled, 5)
            root(T, total=1)
            for b in range(4):
                if b == 3:
                    weights_high(0)
                    weights_high(1)
                act.wait_ge(row_done, 2 * (b + 1))
                nc.scalar.copy(ada_row[0:2, b * 512:(b + 1) * 512], ps[0:2, b, :]).then_inc(row_out, 1)
            for k in range(KD):
                act.wait_ge(hx_ready, k + 1)
                nc.scalar.copy(hT_hi[:, k, :], hT[:, k, :]).then_inc(hx_high, 1)

            def attention():
                for n in range(len(UNITS) + 3):
                    m = n - 2
                    if 0 <= m < len(UNITS):
                        act.wait_ge(probs_turned, m + 1)
                        if m >= 2:
                            act.wait_ge(values_done, m - 1)
                        size = P * len(unit(m)[3])
                        nc.scalar.copy(probsT[:, m % 2, 0:size], turned_bank[:, 0:size]).then_inc(turned_copied, 1)
                    if n < len(UNITS):
                        t, qb, s, w = unit(n)
                        act.wait_ge(neg_ready, n + 1)
                        nc.scalar.activation(probs[:, n % 4, 0:P * len(w)], probs[:, n % 4, 0:P * len(w)], ACT.Exp,
                                             bias=cell(1, n), scale=-1.0, accum_out=cell(2, n))
                        nc.scalar.activation(cell(3, n), vecs[:, V_SINK + 2 * t + s:V_SINK + 2 * t + s + 1], ACT.Exp,
                                             bias=cell(1, n)).then_inc(exp_done, 1)
                    if n == 48:
                        weights_high(SPLIT.index(("o_attn", 0)))
                    m = n - 3
                    if m >= 0 and m % 8 == 7:
                        act.wait_ge(values_done, m + 1)
                        nc.scalar.copy(y_hi[:, m // 8, :], ps[:, 6 + (m // 8) % 2, :]).then_inc(y_high, 1)
            for m, (kind, i) in enumerate(SPLIT[:SPLIT.index(("wq", 0))]):
                if (kind, i) not in (("gate", 6), ("gate", 7)):
                    weights_high(m + 2)
                if kind == "o_conv":
                    for k in range(4 * i, 4 * i + 4):
                        act.wait_ge(z_ready, k + 1)
                        nc.scalar.copy(z_hi[:, k, :], gates[:, k, :]).then_inc(z_high, 1)
                elif kind != "o_attn":
                    if (kind, i) == ("out", 0):
                        act.wait_ge(mix_gain, 1)
                    for name, t in tiles_of(kind, i):
                        if kind == "conv_g":
                            act.wait_ge(ctx_in, 16)
                            for k in (2 * t, 2 * t + 1):
                                square(ctx_sb[:, k, :], C)
                        tile_out(name, t)
                if (kind, i) == ("conv_g", 1):
                    root(C, total=2)
                elif (kind, i) == ("q", 0):
                    act.wait_ge(hc_ready, KD)
                    nc.scalar.copy(hc_hi[:, :, :], hcT[:, :, :]).then_inc(hc_high, 1)
                elif (kind, i) == ("gate", 7):
                    attention()
                    weights_high(SPLIT.index(("o_attn", 1)))
                    act.wait_ge(conv_centred, KC)
                    for c in range(KC):
                        square(conv_acc[:, c, :], T)
                    root(T, D / CONV, total=3)
                elif (kind, i) == ("o_attn", 1):
                    act.wait_ge(conv_normed, KC)
                    for c in range(KC):
                        nc.scalar.activation(conv_acc[:, c, :], conv_acc[:, c, :], ACT.Silu, bias=column(V_LNB, c),
                                             scale=column(V_LNG, c)).then_inc(conv_out, 1)
                    act.wait_ge(conv_out, KC)
                    nc.scalar.copy(c_hi[:, :, :], conv_acc[:, :, :]).then_inc(conv_high, 1)
            root(T, total=4)
            weights_high(SPLIT.index(("wq", 2)))
            for k in range(KD):
                wait_residual(act, k, x1_dve, x1_pool)
                square_all(x1[:, k, :], k)
            root(T)
            for k in range(KD):
                act.wait_ge(h2_ready, k + 1)
                nc.scalar.copy(h2_hi[:, k, :], h2[:, k, :]).then_inc(h2_split, 1)
            for i in range(2 * PEER_HEADS + 1):
                if i == 14:
                    assert all(ORDER.index(("wq", m)) % RING > 1 for m in (6, 7))
                    act.wait_ge(tile_done, tile_no["peer", 11] + 1)
                    act.wait_ge(row_in[0], 16)
                    nc.scalar.copy(st_hi[:, 0, :], raw[:, 0, :]).then_inc(hi_ready, 1)
                if i < 2 * PEER_HEADS:
                    if i % 2 == 0 and 2 <= i and i // 2 + 2 < 8:
                        weights_high(SPLIT.index(("wq", i // 2 + 2)))
                    n = tile_no["peer", i]
                    act.wait_ge(tile_done, n + 1)
                    if i >= 2:
                        act.wait_ge(routing_done, i - 1)
                    nc.scalar.copy(q_peer[:, i % 2, :], ps[:, tile_bank(n), :]).then_inc(tile_out_act, 1)
                if i >= 1:
                    act.wait_ge(routing_done, i)
                    nc.scalar.copy(scores[:, i - 1:i + 2 * PEER_HEADS * (TT - 1):2 * PEER_HEADS, :],
                                   ps[:, 4 + (i - 1) % 2, :].rearrange("p (t k) -> p t k", t=TT)).then_inc(routing_out, 1)

            def high(step):
                act.wait_ge(row_in[step.c % 4], step.fours * 16)
                act.wait_ge(step_done, step.n + 1)
                nc.scalar.copy(st_hi[:, step.c % 2, :], raw[:, step.c % 4, :]).then_inc(hi_ready, 1)

            def gelu(step):
                act.wait_ge(step_done, step.n + 3)
                act.wait_ge(act_stored[step.c % 2], step.pairs * 16)
                nc.scalar.activation(act_out[:, step.c % 2, :], ps[:, step.c % 2, :], ACT.Gelu).then_inc(gelu_done, 1)

            act.wait_ge(step_done, 2)
            for x in (*act_stored, *w_stored):
                act.sem_inc(x, 16)
            act.sem_inc(gelu_done, 2)
            act.sem_inc(w_tile_out, DEPTH)
            nc.scalar.preload_act_table(ACT.Gelu)
            with act.Fori(0, 15) as it:
                for s in range(4):
                    high(Step(it, 4, s + 1))
                    gelu(Step(it, 4, s))
            for n in range(60, 64):
                high(alone(n + 1))
                gelu(alone(n))
                if n == 60:
                    act.wait_ge(picked, 1)
                    nc.scalar.activation(best[:, :, :], best[:, :, :], ACT.Exp).then_inc(gate_exp, 1)
                    nc.scalar.preload_act_table(ACT.Gelu)
                if n == 61:
                    for j in range(3):
                        act.wait_ge(turned, j + 1)
                        nc.scalar.copy((i1T, i2T, gT)[j][:, :], ps[:, 4 + j, :]).then_inc(turned_out, 1)
            with act.Fori(0, 4) as it:
                for s in range(ROUND):
                    high(Step(it, ROUND, 64 + s + 1))
                    gelu(Step(it, ROUND, 64 + s))
                    for g in groups(s):
                        act.wait_ge(w_done, it * 32 + (g + 1 + DEPTH))
                        h = g // 8
                        if g % 8 == 0:
                            act.wait_ge(w_stored[h % 2], it * 32 + 16 * (h // 2 + 1))
                        nc.scalar.copy(w_tile[:, h % 2, :, 4 * (g % 8):4 * (g % 8) + 4].rearrange("p i t -> p t i"),
                                       ps[:, 2 + g % DEPTH, :].rearrange("p (t i) -> p t i", t=4)).then_inc(w_tile_out, 1)

            def high_p(i2, s, free=False):
                act.wait_ge(pf_ready, i2 + 1)
                if not free:
                    act.wait_ge(step_done, i2 + (KEYS + 1))
                nc.scalar.copy(p_hi[:, s % 2, :], p_full[:, s % 2, :]).then_inc(ph_ready, 1)

            with act.Fori(0, 3) as it:
                for s in range(4):
                    high(Step(it, 4, 112 + s + 1))
                    gelu(Step(it, 4, 112 + s))
            for n in range(124, 128):
                high(alone(n + 1))
                gelu(alone(n))
                if n == 125:
                    high_p(0, 0, free=True)
            with act.Fori(0, 15) as it:
                for s in range(8):
                    high(Step(it, 8, KEYS + s + 1))
                    high_p(it * 8 + (s + 1), s + 1)
            for s in range(7):
                high(alone(NSTEP - 8 + s + 1))
                high_p(KEYS - 8 + s + 1, s + 1)
            for i, k in enumerate(LAST_ORDER):
                act.wait_ge(bank_done, i + 1)
                square_all(ps[:, k, :], k)
            root(T, total=5)

        @block.vector
        def _(dve):
            chain = [0]

            def link(ins):
                chain[0] += 1
                ins.then_inc(dve_chain, 1)
                dve.wait_ge(dve_chain, chain[0])


            def inverse_root(n, width):
                dve.wait_ge(std_ready, n)
                nc.vector.reciprocal(rstd[:, 0:width], rstd[:, 0:width]).then_inc(rstd_ready, 1)
                dve.wait_ge(rstd_ready, n)

            def add_squares(first, width, count=KD):
                for k in range(count):
                    n = first + k
                    dve.drain()
                    dve.wait_ge(sq_ready, n + 1)
                    if k == 0:
                        ins = nc.vector.tensor_copy(rstd[:, 0:width], sq[:, n % 3, 0:width])
                    else:
                        ins = nc.vector.tensor_tensor(rstd[:, 0:width], rstd[:, 0:width], sq[:, n % 3, 0:width], ALU.add)
                    ins.then_inc(sq_used, 1)

            add_squares(0, T)
            inverse_root(1, T)
            for k in range(KD):
                nc.vector.tensor_tensor(hT[:, k, :], x1[:, k, :], rstd[:, :], ALU.mult)
            dve.wait_ge(vec_in, 16)
            dve.wait_ge(ada_used, 1)
            nc.vector.tensor_tensor(mod[:, 0:16, :], ps[:, BANK_ADA, 0:32].rearrange("p (n c) -> p n c", c=2),
                                    vecs[:, V_BADA:V_BADA + 16].unsqueeze(2).to_broadcast([P, 16, 2]), ALU.add).then_inc(mod_ready, 1)
            dve.drain()
            for w in range(2):
                nc.vector.scalar_tensor_tensor(coef[:, w, :], mod[:, SC1:SC1 + 8, w], 1.0, vecs[:, V_PREMIX:V_PREMIX + 8],
                                               ALU.add, ALU.mult)
            dve.drain()
            for k in range(KD + 2):
                if k < KD:
                    nc.vector.tensor_scalar(hT[:, k, :], hT[:, k, :], coef[:, 0, k:k + 1], mod[:, SH1 + k, 0:1],
                                            ALU.mult, ALU.add).then_inc(hx_ready, 1)
                if k >= 2:
                    dve.wait_ge(hx_high, k - 1)
                    nc.vector.tensor_tensor(hT_lo[:, k - 2, :], hT[:, k - 2, :], hT_hi[:, k - 2, :].bitcast(fp32),
                                            ALU.subtract).then_inc(hx_parts, 1)
            add_squares(8, C)
            inverse_root(2, C)
            for k in range(KD):
                nc.vector.tensor_tensor(hcT[:, k, :], ctx_sb[:, k, :], rstd[:, 0:C], ALU.mult)
            dve.drain()
            for k in range(KD):
                nc.vector.tensor_scalar(hcT[:, k, :], hcT[:, k, :], coef[:, 1, k:k + 1], mod[:, SH1 + k, 1:2],
                                        ALU.mult, ALU.add).then_inc(hc_ready, 1)
            for c in range(KC):
                dve.wait_ge(tile_out_act, tile_count[tile_no["conv_g", c]])
                ci = conv_in[:, c, TAPS // 2:TAPS // 2 + T]
                nc.vector.tensor_tensor(ci, ci, glu[:, c, :], ALU.mult).then_inc(glu_used, 1)
            dve.wait_ge(glu_used, KC)
            for c in range(KC):
                link(nc.vector.tensor_scalar(conv_acc[:, c, :], conv_in[:, c, 0:T], column(V_DW, c * TAPS), column(V_DWB, c),
                                             ALU.mult, ALU.add))
            for t in range(1, TAPS):
                for c in range(KC):
                    ins = nc.vector.scalar_tensor_tensor(conv_acc[:, c, :], conv_in[:, c, t:t + T], column(V_DW, c * TAPS + t),
                                                         conv_acc[:, c, :], ALU.mult, ALU.add)
                dve.drain()
            dve.wait_ge(const_in, 16 * 5)

            def rotate(x):
                dve.drain()
                nc.vector.stream_shuffle(turn[:, :], x, SWAP)
                dve.drain()
                nc.vector.tensor_tensor(turn[:, :], turn[:, :], sin_t[:, :], ALU.mult)
                nc.vector.tensor_tensor(x, x, cos_t[:, :], ALU.mult)
                dve.drain()
                nc.vector.tensor_tensor(x, x, turn[:, :], ALU.add).then_inc(rotated, 1)

            for i in range(2):
                dve.wait_ge(tile_out_act, tile_count[tile_no["k", i]])
                rotate(kT[:, i, 0:T])
            for i in range(KD):
                dve.wait_ge(tile_out_act, tile_count[tile_no["q", i]])
                rotate(qT[:, i, :])
            dve.drain()
            ins = nc.vector.tensor_tensor(rstd[:, :], conv_acc[:, 0, :], conv_acc[:, 1, :], ALU.add)
            for c in range(2, KC):
                dve.drain()
                ins = nc.vector.tensor_tensor(rstd[:, :], rstd[:, :], conv_acc[:, c, :], ALU.add)
            ins.then_inc(conv_summed, 1)
            dve.wait_ge(mean_done, 1)
            nc.vector.tensor_scalar(rstd[:, :], ps[:, BANK_STAT, :], D / CONV, None, ALU.mult)
            dve.drain()
            for c in range(KC):
                nc.vector.tensor_tensor(conv_acc[:, c, :], conv_acc[:, c, :], rstd[:, :], ALU.subtract).then_inc(conv_centred, 1)
            nc.vector.tensor_scalar(neg_sink[:, :], vecs[:, V_SINK:V_SINK + HEADS], -1.0, None, ALU.mult)
            dve.drain()
            for n in range(len(UNITS) + 4):
                if n < len(UNITS):
                    t, qb, s, w = unit(n)
                    size = P * len(w)
                    mk = mask[:, 0:640] if len(w) == 5 else (mask[:, 128:640] if qb == 0 else mask[:, 640:1152])
                    dve.wait_ge(scores_done, n + 1)
                    if n >= 4:
                        dve.wait_ge(probs_turned, n - 3)
                    nc.vector.tensor_tensor_reduce(out=probs[:, n % 4, 0:size], in0=score_bank(n, w), in1=mk, scale=1.0,
                                                   scalar=neg_sink[:, 2 * t + s:2 * t + s + 1],
                                                   op0=ALU.add, op1=ALU.min, accum_out=cell(1, n)).then_inc(neg_ready, 1)
                m = n - 1
                if 0 <= m < len(UNITS):
                    size = P * len(unit(m)[3])
                    dve.wait_ge(exp_done, m + 1)
                    nc.vector.tensor_tensor(cell(4, m), cell(2, m), cell(3, m), ALU.add)
                    dve.drain()
                    nc.vector.reciprocal(cell(5, m), cell(4, m))
                    dve.drain()
                    nc.vector.tensor_scalar(probs[:, m % 4, 0:size], probs[:, m % 4, 0:size], cell(5, m), None,
                                            ALU.mult).then_inc(probs_ready, 1)
                m = n - 4
                if m >= 0 and m % 8 == 7:
                    dve.wait_ge(y_high, m // 8 + 1)
                    nc.vector.tensor_tensor(y_lo[:, m // 8, :], ps[:, 6 + (m // 8) % 2, :], y_hi[:, m // 8, :].bitcast(fp32),
                                            ALU.subtract).then_inc(y_out, 1)

            def low_z(k):
                dve.wait_ge(z_high, k + 1)
                nc.vector.tensor_tensor(z_lo[:, k, :], gates[:, k, :], z_hi[:, k, :].bitcast(fp32), ALU.subtract).then_inc(z_parts, 1)

            dve.wait_ge(ada_used, 1 + N_ADA - ADA_FIRST)
            nc.vector.tensor_tensor(mod[:, 16:48, 0], ps[:, BANK_LATER, ADA_COL + 16:ADA_COL + 48],
                                    vecs[:, V_BADA + 16:V_BADA + 48], ALU.add).then_inc(mod_ready, 1)
            dve.drain()
            nc.vector.tensor_tensor(coef[:, 2, :], mod[:, GT1:GT1 + 8, 0], vecs[:, V_POSTMIX:V_POSTMIX + 8], ALU.mult).then_inc(mix_gain, 1)
            nc.vector.scalar_tensor_tensor(coef[:, 3, :], mod[:, SC2:SC2 + 8, 0], 1.0, vecs[:, V_PREFFN:V_PREFFN + 8],
                                           ALU.add, ALU.mult)
            nc.vector.tensor_tensor(coef[:, 4, :], mod[:, GT2:GT2 + 8, 0], vecs[:, V_POSTFFN:V_POSTFFN + 8], ALU.mult)
            add_squares(16, T, KC)
            for kind, m in SPLIT[SPLIT.index(("o_attn", 0)):SPLIT.index(("out", 0))]:
                if kind == "o_attn":
                    if m == 1:
                        inverse_root(3, T)
                        for c in range(KC):
                            nc.vector.tensor_tensor(conv_acc[:, c, :], conv_acc[:, c, :], rstd[:, :], ALU.mult).then_inc(conv_normed, 1)
                    for i in (2 * m, 2 * m + 1):
                        n = tile_no["ya", i]
                        dve.wait_ge(tile_done, n + 1)
                        nc.vector.tensor_tensor(gates[:, i, :], gates[:, i, :], ps[:, tile_bank(n), :], ALU.mult).then_inc(tile_out_dve, 1)
                elif kind == "o_conv":
                    for i in range(4 * m, 4 * m + 4):
                        n = tile_no["yc", i]
                        dve.wait_ge(tile_done, n + 1)
                        nc.vector.tensor_tensor(gates[:, KD + i, :], gates[:, KD + i, :], ps[:, tile_bank(n), :],
                                                ALU.mult).then_inc(tile_out_dve, 1)
                        dve.wait_ge(tile_out_dve, KD + i + 1)
                        nc.vector.tensor_tensor(gates[:, i, :], gates[:, i, :], gates[:, KD + i, :], ALU.add).then_inc(z_ready, 1)
                        if i >= 1:
                            low_z(i - 1)
                    if m == 1:
                        low_z(KD - 1)
            add_squares(20, T)
            dve.wait_ge(x_in, 32)
            dve.wait_ge(tile_out_act, tile_count[tile_no["mix", KD - 1]])
            inverse_root(4, T)
            residual(dve, nc.vector, mixed, x1_dve, False)
            inverse_root(5, T)
            for k in range(KD):
                nc.vector.scalar_tensor_tensor(h2[:, k, :], x1[:, k, :], coef[:, 3, k:k + 1], rstd[:, :], ALU.mult, ALU.mult)
                dve.drain()
                nc.vector.tensor_scalar(h2[:, k, :], h2[:, k, :], mod[:, SH2 + k, 0:1], None, ALU.add).then_inc(h2_ready, 1)

            dve.wait_ge(routing_out, 2 * PEER_HEADS)
            with dve.Fori(0, 16) as it:

                def lk(ins):
                    dve.drain()

                def top16(values, ix, x):
                    lk(nc.vector.max(values[:, 0:8], x))
                    nc.vector.max_index(ix[:, 0:8], values[:, 0:8], x)
                    lk(nc.vector.match_replace(x, values[:, 0:8], x, FLOOR))
                    lk(nc.vector.max(values[:, 8:16], x))
                    lk(nc.vector.max_index(ix[:, 8:16], values[:, 8:16], x))

                lk(nc.vector.tensor_copy(sc_now[:, :, :], scores[:, bass.ds(it * 4, 4), :]))
                for x in range(4):
                    top16(tops[:, x, :], top_ix[:, x, :], sc_now[:, x, :])
                lk(nc.vector.tensor_copy(top_ixf[:, :, :], top_ix[:, :, :]))
                for x in range(2):
                    lk(nc.vector.tensor_tensor(cand[:, x, :].rearrange("p (a b) -> p a b", a=TOPK),
                                               tops[:, 2 * x, :].unsqueeze(2).to_broadcast([P, TOPK, TOPK]),
                                               tops[:, 2 * x + 1, :].unsqueeze(1).to_broadcast([P, TOPK, TOPK]), ALU.add))
                    top16(best_now[:, x, :], pos[:, x, :], cand[:, x, :])
                nc.vector.tensor_copy(best[:, bass.ds(it * 2, 2), :], best_now[:, :, :])
                nc.vector.tensor_scalar(pos_ab[:, 0, :, :], pos[:, :, :], 4, None, ALU.logical_shift_right)
                lk(nc.vector.tensor_scalar(pos_ab[:, 1, :, :], pos[:, :, :], 15, None, ALU.bitwise_and))
                lk(nc.vector.tensor_copy(pos_f[:, :, :, :], pos_ab[:, :, :, :]))
                for half, dst in ((0, i1_all), (1, i2_all)):
                    for x in range(2):
                        nc.vector.tensor_tensor(hit[:, x, :, :], pos_f[:, half, x, :].unsqueeze(2).to_broadcast([P, TOPK, TOPK]),
                                                iota[:, 0:TOPK].unsqueeze(1).to_broadcast([P, TOPK, TOPK]), ALU.is_equal)
                    dve.drain()
                    for x in range(2):
                        nc.vector.tensor_tensor(hit[:, x, :, :], hit[:, x, :, :],
                                                top_ixf[:, 2 * x + half, :].unsqueeze(1).to_broadcast([P, TOPK, TOPK]), ALU.mult)
                    dve.drain()
                    lk(nc.vector.tensor_reduce(dst[:, bass.ds(it * 2, 2), :], hit[:, :, :, :], AX, ALU.add))
            link(nc.vector.tensor_copy(tops[:, 0:2, :].rearrange("p a b -> p (a b)").unsqueeze(2), best[:, :, 0:1]))
            nc.vector.tensor_tensor(best[:, :, :], best[:, :, :],
                                    tops[:, 0:2, :].rearrange("p a b -> p (a b)").unsqueeze(2).to_broadcast([P, 32, TOPK]),
                                    ALU.subtract).then_inc(picked, 1)
            dve.wait_ge(gate_exp, 1)
            link(nc.vector.tensor_reduce(e_sum[:, 0, :], best[:, :, :], AX, ALU.add))
            link(nc.vector.reciprocal(e_sum[:, 1, :], e_sum[:, 0, :]))
            nc.vector.tensor_tensor(best[:, :, :], best[:, :, :], e_sum[:, 1, :].unsqueeze(2).to_broadcast([P, 32, TOPK]),
                                    ALU.mult).then_inc(gate_ready, 1)
            dve.wait_ge(turned_out, 3)
            with dve.Fori(0, 4) as it:
                dve.drain()
                dve.wait_ge(b_ready, it * 32 + 1)
                for j, src in ((0, i1T), (2, gT)):
                    nc.vector.tensor_copy(now[:, j, :], src[:, bass.ds(it * 128, 128)])
                nc.vector.tensor_copy(now[:, 1, :], i2T[:, bass.ds(it * 128, 128)]).then_inc(now_ready, 1)
                dve.drain()
                for s in range(ROUND):
                    low_rows(dve, nc.vector, Step(it, ROUND, 64 + s + 1))
                    for g in groups(s):
                        dve.wait_ge(w_done, it * 32 + (g + 1))
                        for j in range(4):
                            t = 4 * g + j
                            ins = nc.vector.tensor_scalar(one_a[:, g % DEPTH, j, :], iota[:, :], now[:, 0, t:t + 1],
                                                          now[:, 2, t:t + 1], ALU.is_equal, ALU.mult)
                        ins.then_inc(a_ready, 1)
            nc.vector.memset(zeros[:, :], 0.0).then_inc(zero_ready, 1)

            def product(i2, s, acts, ws):
                dve.wait_ge(act_loaded[s % 4], acts)
                dve.wait_ge(w_loaded[(s // 4) % 2], ws)
                nc.vector.tensor_tensor(p_full[:, s % 2, :].rearrange("p (t s) -> p t s", s=32),
                                        act_in[:, s % 4, :].rearrange("p (t s) -> p t s", s=32),
                                        w_in[:, (s // 4) % 2, :, s % 4, :], ALU.mult).then_inc(pf_ready, 1)

            def low_p(i2, s):
                dve.wait_ge(ph_ready, i2 + 1)
                nc.vector.tensor_tensor(p_lo[:, s % 2, :], p_full[:, s % 2, :], p_hi[:, s % 2, :].bitcast(fp32),
                                        ALU.subtract).then_inc(pl_ready, 1)

            with dve.Fori(0, 3) as it:
                for s in range(4):
                    low_rows(dve, nc.vector, Step(it, 4, 112 + s + 1))
            for n in range(124, 128):
                low_rows(dve, nc.vector, alone(n + 1))
                if n == 124:
                    product(0, 0, 16, 16)
                if n == 126:
                    low_p(0, 0)
            with dve.Fori(0, 15) as it:
                for s in range(8):
                    i2 = it * 8 + s
                    product(i2 + 1, s + 1, it * 32 + 16 * (1 + (s + 1) // 4), it * 16 + (16 if s < 7 else 32))
                    low_rows(dve, nc.vector, Step(it, 8, KEYS + s + 1))
                    low_p(i2 + 1, s + 1)
            for s in range(7):
                i2 = KEYS - 8 + s
                product(i2 + 1, s + 1, 15 * 32 + 16 * (1 + (s + 1) // 4), 16 * 16)
                low_rows(dve, nc.vector, alone(NSTEP - 8 + s + 1))
                low_p(i2 + 1, s + 1)
            for i, k in enumerate(LAST_ORDER):
                dve.wait_ge(sq_ready, 36 + i + 1)
                nc.vector.tensor_scalar(ffn[:, k, :], ps[:, k, :], coef[:, 4, k:k + 1], None, ALU.mult).then_inc(acc_out, 1)
            into = sq_all[:, LAST_ORDER[4], :]
            for i in range(5, KD):
                nc.vector.tensor_tensor(into, into, sq_all[:, LAST_ORDER[i], :], ALU.add).then_inc(four_added, 1)
                dve.wait_ge(four_added, i - 4)
            inverse_root(6, T)
            residual(dve, nc.vector, ffn, final_dve, False)

        @block.tensor
        def _(pe):
            n_sq = [0]

            def sum_squares(order):
                for i, k in enumerate(order):
                    pe.wait_ge(sq_ready, n_sq[0] + 1)
                    ins = nc.tensor.matmul(ps[:, BANK_STAT, :], mean_of[:, :], sq_all[:, k, :], start=i == 0, stop=i == KD - 1)
                    ins.then_inc(sq_used, 1)
                    n_sq[0] += 1

            def total(width, count=KD):
                n_sq[0] += count
                pe.wait_ge(sq_used, n_sq[0])
                nc.tensor.matmul(ps[:, BANK_STAT, 0:width], mean_of[:, :], rstd[:, 0:width], start=True, stop=True).then_inc(total_done, 1)

            def attention():
                for t in range(tile[0] - 4, tile[0]):
                    wait_tile_out(pe, t)
                pe.wait_ge(rotated, 10)
                pe.wait_ge(mod_ready, 1)

                def scores_of(n):
                    t, qb, s, w = unit(n)
                    if n >= 2:
                        pe.wait_ge(neg_ready, n - 1)
                    rows = slice(64 * s, 64 * s + 64)
                    dst = score_bank(n, w)
                    width = P * (len(w) - 2)
                    q = qT[rows, t, qb * P:(qb + 1) * P]
                    nc.tensor.matmul(dst[:, 0:width], q, kT[rows, t // 4, w[0] * P:w[0] * P + width], start=True, stop=True)
                    nc.tensor.matmul(dst[:, width:width + C], q, kT[rows, t // 4, T:T + C],
                                     start=True, stop=True).then_inc(scores_done, 1)

                def times_v(n):
                    t, qb, s, w = unit(n)
                    pe.wait_ge(turned_copied, n + 1)
                    if n % 8 == 0 and t >= 2:
                        pe.wait_ge(y_out, t - 1)
                    g = 2 * (t // 4) + s
                    for i, b in enumerate(w):
                        ins = nc.tensor.matmul(ps[64 * s:64 * s + 64, 6 + t % 2, qb * P:(qb + 1) * P],
                                               v_sb[:, b, g * HD:(g + 1) * HD], probsT[:, n % 2, i * P:(i + 1) * P],
                                               start=i == 0, stop=i == len(w) - 1)
                    ins.then_inc(values_done, 1)

                def later_ada(j):
                    pe.wait_ge(acc_ready, j + 1)
                    for i in range(2):
                        t = 2 * (ADA_FIRST + j) + i
                        ins = nc.tensor.matmul(ps[:, BANK_LATER, ADA_COL + t:ADA_COL + t + 1], ada_acc[:, j % 2, i * P:(i + 1) * P],
                                               one_col[:, 0:1], start=True, stop=True)
                    ins.then_inc(ada_used, 1)

                for n in range(3):
                    scores_of(n)
                for n in range(len(UNITS)):
                    pe.wait_ge(probs_ready, n + 1)
                    if n >= 1:
                        pe.wait_ge(turned_copied, n)
                    if n % 4 == 0 and n >= 4:
                        later_ada(n // 4 - 1)
                    for i in range(len(unit(n)[3])):
                        ins = nc.tensor.transpose(turned_bank[:, i * P:(i + 1) * P], probs[:, n % 4, i * P:(i + 1) * P], ident[:, :])
                    ins.then_inc(probs_turned, 1)
                    if n + 3 < len(UNITS):
                        scores_of(n + 3)
                    if n >= 1:
                        times_v(n - 1)
                times_v(len(UNITS) - 1)
                pe.wait_ge(turned_copied, len(UNITS))
                later_ada(N_ADA - ADA_FIRST - 1)

            tile = [0]
            pe.wait_ge(filled, 2)
            pe.wait_ge(cond_ready, 1)

            def chunk_view(x, slot, kind):
                return x[:, slot, :].rearrange("p (k n) -> p k n", k=KC if kind == "o_conv" else KD)

            def product(stationary, moving, width, ks=KD):
                t = tile[0]
                if t >= 4:
                    wait_tile_out(pe, t - 4)
                for k in range(ks):
                    for i, (a, b) in enumerate(((0, 0), (0, 1), (1, 0))):
                        ins = nc.tensor.matmul(ps[:, tile_bank(t), 0:width], stationary[a](k), moving[b](k),
                                               start=k == 0 and i == 0, stop=k == ks - 1 and i == 2)
                ins.then_inc(tile_done, 1)
                tile[0] += 1

            def pair_product(w, moving, ready):
                t = tile[0]
                for i in range(2):
                    if t + i >= 4:
                        wait_tile_out(pe, t + i - 4)
                for k in range(KD):
                    pe.wait_ge(ready, k + 1)
                    for i in range(2):
                        for j, (a, b) in enumerate(((0, 0), (0, 1), (1, 0))):
                            ins = nc.tensor.matmul(ps[:, tile_bank(t + i), :], w[a][:, k, i * P:(i + 1) * P], moving[b][:, k, :],
                                                   start=k == 0 and j == 0, stop=k == KD - 1 and j == 2)
                        if k == KD - 1:
                            ins.then_inc(tile_done, 1)
                tile[0] += 2

            def routing_scores(t):
                if t == 0:
                    pe.wait_ge(mod_ready, 2)
                    pe.wait_ge(keys_in, 16)
                    pe.wait_ge(std_ready, 5)
                wait_tile_out(pe, tile_no["peer", t])
                if t >= 2:
                    pe.wait_ge(routing_out, t - 1)
                for b in range(TT):
                    ins = nc.tensor.matmul(ps[:, 4 + t % 2, b * P:(b + 1) * P], q_peer[:, t % 2, b * P:(b + 1) * P],
                                           keys[:, t, :], start=True, stop=True)
                ins.then_inc(routing_done, 1)

            def whole(x):
                return lambda k: x[:, k, :]

            def part(x, a, b):
                return lambda k: x[:, k, a:b]

            SPLIT_MOVING = {"conv_a": (hT_hi, hT_lo), "conv_g": (hT_hi, hT_lo), "k": (hT_hi, hT_lo), "q": (hT_hi, hT_lo),
                            "gate": (hT_hi, hT_lo), "o_attn": (y_hi, y_lo), "o_conv": (c_hi, c_lo), "out": (z_hi, z_lo),
                            "wq": (h2_hi, h2_lo)}

            FIRST_READY = {("conv_a", 0): hx_parts, ("out", 0): z_parts, ("wq", 0): h2_parts}

            for n, (kind, m) in enumerate(ORDER):
                if kind == "ada" and m < ADA_FIRST:
                    wait_chunk_in(pe, n)
                    w = ring[:, n % RING, :].rearrange("p (k n) -> p k n", k=KD)
                    for k in range(KD):
                        ins = nc.tensor.matmul(ps[0:2, m // 2, (m % 2) * CHUNK:(m % 2 + 1) * CHUNK], cond[:, k, :], w[:, k, :],
                                               start=k == 0, stop=k == KD - 1)
                    ins.then_inc(row_done, 1)
                    if m == 3:
                        total(T)
                    if m == ADA_FIRST - 1:
                        pe.wait_ge(const_in, 16)
                        for t in range(16):
                            if t % 4 == 0:
                                pe.wait_ge(row_out, t // 4 + 1)
                            ins = nc.tensor.transpose(ps[:, BANK_ADA, 2 * t:2 * t + 2], ada_row[0:2, t * P:(t + 1) * P], ident[0:2, 0:2])
                        ins.then_inc(ada_used, 1)
                    continue
                if kind == "ada":
                    continue
                x = SPLIT.index((kind, m))
                pe.wait_ge(w_parts, x + 1)
                w = chunk_view(w_hi, x % HIGHS, kind), chunk_view(w_lo, n % RING, kind)
                if kind == "v":
                    for i in range(TT):
                        product((part(hT_hi, i * P, (i + 1) * P), part(hT_lo, i * P, (i + 1) * P)), (whole(w[0]), whole(w[1])), 256)
                    for i in range(2):
                        product((part(hc_hi, i * P, (i + 1) * P), part(hc_lo, i * P, (i + 1) * P)), (whole(w[0]), whole(w[1])), 256)
                    continue
                if (kind, m) == ("o_attn", 0):
                    pe.wait_ge(y_out, KD)
                if (kind, m) == ("o_conv", 0):
                    pe.wait_ge(conv_parts, 1)
                moving = tuple(whole(v) for v in SPLIT_MOVING[kind])
                for i in range(4 if kind == "o_conv" else 2):
                    if (kind, m) in FIRST_READY:
                        if i == 0:
                            pair_product(w, SPLIT_MOVING[kind], FIRST_READY[kind, m])
                    else:
                        product((part(w[0], i * P, (i + 1) * P), part(w[1], i * P, (i + 1) * P)), moving, T,
                                KC if kind == "o_conv" else KD)
                    if kind == "wq" and 2 * m + i >= 1:
                        routing_scores(2 * m + i - 1)
                if (kind, m) == ("wq", 7):
                    routing_scores(2 * PEER_HEADS - 1)
                if (kind, m) == ("conv_g", 1):
                    total(C)
                if kind == "k":
                    pe.wait_ge(hc_parts, 1)
                    for i in range(2):
                        product((part(w[0], i * P, (i + 1) * P), part(w[1], i * P, (i + 1) * P)), (whole(hc_hi), whole(hc_lo)), C)
                if (kind, m) == ("gate", 7):
                    pe.wait_ge(conv_summed, 1)
                    pe.wait_ge(std_ready, 2)
                    nc.tensor.matmul(ps[:, BANK_STAT, :], mean_of[:, :], rstd[:, :], start=True, stop=True).then_inc(mean_done, 1)
                    attention()
                if (kind, m) == ("o_attn", 0):
                    total(T, KC)
                if (kind, m) == ("out", 3):
                    total(T)
                    pe.wait_ge(std_ready, 4)
                    sum_squares(range(KD))

            pe.wait_ge(std_ready, 5)
            pe.wait_ge(h2_parts, KD)
            pe.wait_ge(tile_out_act, sum(e == "act" for _, _, e in tiles))
            pe.wait_ge(routing_out, 2 * PEER_HEADS)
            pe.sem_inc(step_done, 2)

            def act_step(step):
                wait_low(pe, step)
                pe.wait_ge(gelu_done, step.n + 1)
                x = step.c % 2
                for k in range(KD):
                    hi, lo = st_hi[:, x, k * P:(k + 1) * P], st_lo[:, x, k * P:(k + 1) * P]
                    for i, (a, b) in enumerate(((hi, h2_hi), (hi, h2_lo), (lo, h2_hi))):
                        ins = nc.tensor.matmul(ps[:, x, :], a, b[:, k, :], start=k == 0 and i == 0,
                                               stop=k == KD - 1 and i == 2)
                ins.then_inc(step_done, 1)

            with pe.Fori(0, 15) as it:
                for s in range(4):
                    act_step(Step(it, 4, s))
            for n in range(60, 64):
                act_step(alone(n))
                if n == 61:
                    pe.wait_ge(gate_ready, 1)
                    for j, src in enumerate((i1_all, i2_all, best)):
                        for x in range(TT):
                            ins = nc.tensor.transpose(ps[:, 4 + j, x * P:(x + 1) * P],
                                                      src[:, 8 * x:8 * x + 8, :].rearrange("p a b -> p (a b)"), ident[:, :])
                        ins.then_inc(turned, 1)
            pe.sem_inc(w_done, DEPTH)
            with pe.Fori(0, 4) as it:
                for s in range(ROUND):
                    act_step(Step(it, ROUND, 64 + s))
                    for g in groups(s):
                        pe.wait_ge(a_ready, it * 32 + (g + 1))
                        pe.wait_ge(b_ready, it * 32 + (g + 2))
                        pe.wait_ge(w_tile_out, it * 32 + (g + 1))
                        for j in range(4):
                            ins = nc.tensor.matmul(ps[:, 2 + g % DEPTH, j * P:(j + 1) * P], one_a[:, g % DEPTH, j, :],
                                                   one_b[:, g % DEPTH, j, :], start=True, stop=True)
                        ins.then_inc(w_done, 1)
            with pe.Fori(0, 4) as it:
                for s in range(4):
                    act_step(Step(it, 4, 112 + s))
            pe.wait_ge(w_tile_out, T // 4 + DEPTH)
            pe.wait_ge(zero_ready, 1)
            for d in (2, 3, 4, 5, 6, 7, 0, 1):
                if d == 0:
                    pe.wait_ge(gelu_done, KEYS + 2)
                nc.tensor.matmul(ps[:, d, :], zeros[:, 0:P], zeros[:, :], start=True, stop=False)

            def out_step(step, last=False):
                wait_low(pe, step)
                pe.wait_ge(pl_ready, step.n + (1 - KEYS))
                s = step.c
                for d in LAST_ORDER if last else range(KD):
                    hi, lo = st_hi[:, s % 2, d * P:(d + 1) * P], st_lo[:, s % 2, d * P:(d + 1) * P]
                    for i, (a, b) in enumerate(((hi, p_hi), (hi, p_lo), (lo, p_hi))):
                        ins = nc.tensor.matmul(ps[:, d, :], a, b[:, s % 2, :], start=False, stop=last and i == 2)
                    if last:
                        ins.then_inc(bank_done, 1)
                if not last:
                    ins.then_inc(step_done, 1)

            with pe.Fori(0, 15) as it:
                for s in range(8):
                    out_step(Step(it, 8, KEYS + s))
            for s in range(8):
                out_step(alone(NSTEP - 8 + s), s == 7)
            pe.wait_ge(acc_out, 1)
            for i, k in enumerate(LAST_ORDER[:5]):
                if i < 4:
                    pe.wait_ge(sq_ready, 36 + i + 1)
                else:
                    pe.wait_ge(four_added, 3)
                ins = nc.tensor.matmul(ps[:, BANK_STAT, :], mean_of[:, :], sq_all[:, k, :], start=i == 0, stop=i == 4)
            ins.then_inc(total_done, 1)


def fixed_tables():
    t = np.arange(T, dtype=np.int32)
    place = [(t // GRID_W).astype(np.float32), (t % GRID_W).astype(np.float32)]
    half = HD // 4
    freqs = (np.float32(10000.0) ** (-np.arange(0, HD // 2, 2, dtype=np.float32) / np.float32(HD // 2))).astype(np.float32)
    cos, sin = np.zeros((P, T), np.float32), np.zeros((P, T), np.float32)
    for p in range(P):
        d = p % HD
        angle = place[d // (HD // 2)] * freqs[d % half]
        cos[p] = np.cos(angle)
        sin[p] = np.sin(angle) * (-1 if d % (HD // 2) < half else 1)
    q, k = np.arange(P)[:, None], np.arange(P)[None, :]
    before = np.where(k >= q, 0.0, -NEG).astype(np.float32)
    after = np.where(k <= q, 0.0, -NEG).astype(np.float32)
    free = np.zeros((P, P), np.float32)
    mask = np.concatenate([before, free, after, free, free, before, free, free, free], axis=1)
    return np.concatenate([np.eye(P, dtype=np.float32), np.tile(np.arange(P, dtype=np.float32), (P, 1)), cos, sin, mask], axis=1)


def columns(v):
    return np.asarray(v).reshape(-1, P).T


def lay_out(inputs):
    a = {k: np.asarray(v) for k, v in inputs.items()}

    def chunk(kind, m):
        width = 2 * CHUNK if kind == "o_conv" else CHUNK
        return lambda n: m[:, n * width:(n + 1) * width].reshape(-1, P, width).transpose(1, 0, 2).reshape(P, CHUNK_ROW)

    w_in = a["w_in"][0]
    kv0 = HEADS * HD
    conv0 = kv0 + 2 * KV_HEADS * HD
    gate0 = conv0 + 2 * CONV
    q_cols = np.concatenate([np.arange(h * HD, (h + 1) * HD) for h in HEAD_ORDER])
    v0 = kv0 + KV_HEADS * HD
    parts = {
        "ada": a["w_ada"][0], "conv_a": w_in[:, conv0:conv0 + CONV], "conv_g": w_in[:, conv0 + CONV:gate0],
        "k": w_in[:, kv0:v0], "v": w_in[:, v0:conv0], "q": w_in[:, q_cols], "gate": w_in[:, gate0:],
        "o_attn": a["w_o_attn"][0][q_cols], "o_conv": a["w_o_conv"][0], "out": a["w_out"][0], "wq": a["peer_wq"][0],
    }
    wchunks = np.stack([chunk(k, parts[k])(n) for k, n in ORDER])
    dw = a["conv_dw"][0].T.reshape(KC, P, TAPS).transpose(1, 0, 2).reshape(P, KC * TAPS)
    vec = np.concatenate([columns(a["b_ada"][0]), columns(a["g_pre_mix"][0]), columns(a["g_post_mix"][0]),
                          columns(a["g_pre_ffn"][0]), columns(a["g_post_ffn"][0]), dw, columns(a["conv_dw_b"][0]),
                          columns(a["conv_ln_g"][0]), columns(a["conv_ln_b"][0]),
                          np.tile(a["attn_sink"][0][HEAD_ORDER][None, :], (P, 1))], axis=1)
    rows = np.empty((NSTEP, P, ROW), a["peer_u"].dtype)
    u = a["peer_u"][0].reshape(KEYS, KEYS, KD, P)
    rows[:KEYS] = u.transpose(1, 3, 2, 0).reshape(KEYS, P, ROW)
    rows[KEYS:] = a["peer_v"][0].reshape(KEYS, KEYS, D).transpose(1, 0, 2)
    return {
        "xT": a["x"][0].T.reshape(KD, P, T).transpose(1, 0, 2),
        "ctxT": a["ctx"][0].T.reshape(KD, P, C).transpose(1, 0, 2),
        "cc": np.stack([columns(a["c"][0]), columns(a["c_ctx"])], axis=2),
        "wchunks": wchunks,
        "vec": vec,
        "keysT": a["peer_keys"][0].reshape(2 * PEER_HEADS, KEYS, P).transpose(2, 0, 1),
        "expert_rows": rows,
        "consts": fixed_tables(),
    }


def kernel(**inputs):
    import concourse.bacc as bacc
    from concourse.bass_utils import run_bass_kernel_spmd

    nc = bacc.Bacc("TRN2", target_bir_lowering=False, num_devices=1)
    arrays, args = {}, {}
    for name, a in lay_out(inputs).items():
        arrays[name] = np.ascontiguousarray(a)
        args[name] = nc.dram_tensor(name, arrays[name].shape, mybir.dt.from_np(arrays[name].dtype), kind="ExternalInput").ap()
    out = nc.dram_tensor("outT", (P, KD, T), mybir.dt.float32, kind="ExternalOutput").ap()
    layer_kernel(nc, out=out, **args)
    r = run_bass_kernel_spmd(nc, [arrays], core_ids=[0])
    return np.asarray(r.results[0]["outT"]).transpose(2, 1, 0).reshape(1, T, D)
```
